# Optimizing a Trainium2 kernel written in Bass

```python
import math
import jax, jax.numpy as jnp
from jax import lax
import numpy as np

D_MODEL = 1024
BATCH = 1
SEQ = 256
DEPTH = 2

RET_WIDTH = D_MODEL // 2
RET_HEAD_DIM = 64
RET_HEADS = RET_WIDTH // RET_HEAD_DIM
DIFF_WIDTH = D_MODEL - RET_WIDTH
DIFF_HEAD_DIM = 64
DIFF_V_DIM = 2 * DIFF_HEAD_DIM
DIFF_HEADS = DIFF_WIDTH // DIFF_V_DIM
MIX_WIDTH = RET_WIDTH + DIFF_WIDTH
D_IN_PROJ = 4 * RET_WIDTH + 3 * DIFF_WIDTH
D_FF = -(-8 * D_MODEL // (3 * 256)) * 256
CHUNK = 128
Q_BLOCK = 128
EPS = 1e-6


def rms_norm(x, g):
    xf = x.astype(jnp.float32)
    y = xf * lax.rsqrt(jnp.mean(xf * xf, axis=-1, keepdims=True) + EPS)
    return (y * g.astype(jnp.float32)).astype(x.dtype)

def alibi_slopes(n):
    return 2.0 ** (-8.0 * jnp.arange(1, n + 1, dtype=jnp.float32) / n)

def retention_bidir(q, k, v, lg_f, lg_b):
    B, S, H, D = q.shape
    N = S // CHUNK
    qc = q.astype(jnp.float32).reshape(B, N, CHUNK, H, D)
    kc = k.astype(jnp.float32).reshape(B, N, CHUNK, H, D)
    vc = v.astype(jnp.float32).reshape(B, N, CHUNK, H, D)
    pos = jnp.arange(CHUNK, dtype=jnp.float32)
    dist = pos[:, None] - pos[None, :]
    mask_f = jnp.where(dist >= 0, jnp.exp(lg_f[:, None, None] * jnp.maximum(dist, 0.0)), 0.0)
    mask_b = jnp.where(dist < 0, jnp.exp(lg_b[:, None, None] * jnp.maximum(-dist, 0.0)), 0.0)
    dmask = mask_f + mask_b
    scores = jnp.einsum('bnthd,bnshd->bnhts', qc, kc) * dmask[None, None]
    intra = jnp.einsum('bnhts,bnshd->bnthd', scores, vc)

    wk_f = jnp.exp(lg_f[None, :] * (CHUNK - 1 - pos)[:, None])
    wq_f = jnp.exp(lg_f[None, :] * (pos + 1)[:, None])
    kv_f = jnp.einsum('bnshd,bnshe->nbhde', kc * wk_f[None, None, :, :, None], vc)
    dc_f = jnp.exp(lg_f * CHUNK)[None, :, None, None]
    wk_b = jnp.exp(lg_b[None, :] * pos[:, None])
    wq_b = jnp.exp(lg_b[None, :] * (CHUNK - pos)[:, None])
    kv_b = jnp.einsum('bnshd,bnshe->nbhde', kc * wk_b[None, None, :, :, None], vc)
    dc_b = jnp.exp(lg_b * CHUNK)[None, :, None, None]

    zeros = jnp.zeros((B, H, D, D), jnp.float32)

    def fwd_step(R, kv):
        return dc_f * R + kv, R

    def bwd_step(R, kv):
        return dc_b * R + kv, R

    _, R_f = lax.scan(fwd_step, zeros, kv_f)
    _, R_b = lax.scan(bwd_step, zeros, kv_b, reverse=True)
    cross_f = jnp.einsum('bnthd,nbhde->bnthe', qc * wq_f[None, None, :, :, None], R_f)
    cross_b = jnp.einsum('bnthd,nbhde->bnthe', qc * wq_b[None, None, :, :, None], R_b)
    out = (intra + cross_f + cross_b).reshape(B, S, H, D)
    return out.astype(q.dtype)

def diff_attention(q, k, v, lam, slopes):
    B, S, H, _, Dh = q.shape
    NB = S // Q_BLOCK
    q_blocks = q.reshape(B, NB, Q_BLOCK, H, 2, Dh).transpose(1, 0, 2, 3, 4, 5)
    starts = jnp.arange(NB, dtype=jnp.int32) * Q_BLOCK
    kpos = jnp.arange(S, dtype=jnp.int32)
    vf = v.astype(jnp.float32)

    def block(args):
        qb, start = args
        s = jnp.einsum('bqhmd,bkhmd->bhmqk', qb, k).astype(jnp.float32)
        qpos = start + jnp.arange(Q_BLOCK, dtype=jnp.int32)
        dist = jnp.abs(qpos[:, None] - kpos[None, :]).astype(jnp.float32)
        s = s - slopes[None, :, None, None, None] * dist[None, None, None]
        p = jax.nn.softmax(s, axis=-1)
        a = p[:, :, 0] - lam * p[:, :, 1]
        return jnp.einsum('bhqk,bkhe->bqhe', a, vf)

    o = lax.map(block, (q_blocks, starts))
    return o.transpose(1, 0, 2, 3, 4).reshape(B, S, H, DIFF_V_DIM).astype(q.dtype)

def first_inputs(seed: int = 0) -> dict:
    key = jax.random.key(seed)
    ks = jax.random.split(key, 20)
    f32 = jnp.float32
    nrm = lambda k, shape, scale: jax.random.normal(k, shape, f32) * scale
    heads = jnp.arange(RET_HEADS, dtype=f32)
    base = jnp.log(-jnp.log1p(-(2.0 ** (-5.0 - heads))))
    return {
        "x": jax.random.normal(ks[0], (BATCH, SEQ, D_MODEL), f32),
        "attn_norm_g": 1.0 + nrm(ks[1], (DEPTH, D_MODEL), 0.02),
        "w_in": nrm(ks[2], (DEPTH, D_MODEL, D_IN_PROJ), D_MODEL ** -0.5),
        "ret_decay_fwd": base[None, :] + nrm(ks[3], (DEPTH, RET_HEADS), 0.1),
        "ret_decay_bwd": base[None, :] + nrm(ks[4], (DEPTH, RET_HEADS), 0.1),
        "ret_norm_g": 1.0 + nrm(ks[5], (DEPTH, RET_HEAD_DIM), 0.02),
        "dq_norm_g": 1.0 + nrm(ks[6], (DEPTH, DIFF_HEAD_DIM), 0.02),
        "dk_norm_g": 1.0 + nrm(ks[7], (DEPTH, DIFF_HEAD_DIM), 0.02),
        "lambda_q1": nrm(ks[8], (DEPTH, DIFF_HEAD_DIM), 0.1),
        "lambda_k1": nrm(ks[9], (DEPTH, DIFF_HEAD_DIM), 0.1),
        "lambda_q2": nrm(ks[10], (DEPTH, DIFF_HEAD_DIM), 0.1),
        "lambda_k2": nrm(ks[11], (DEPTH, DIFF_HEAD_DIM), 0.1),
        "diff_norm_g": 1.0 + nrm(ks[12], (DEPTH, DIFF_V_DIM), 0.02),
        "w_out": nrm(ks[13], (DEPTH, MIX_WIDTH, D_MODEL), MIX_WIDTH ** -0.5),
        "ffn_norm_g": 1.0 + nrm(ks[14], (DEPTH, D_MODEL), 0.02),
        "w_gate": nrm(ks[15], (DEPTH, D_MODEL, D_FF), D_MODEL ** -0.5),
        "w_up": nrm(ks[16], (DEPTH, D_MODEL, D_FF), D_MODEL ** -0.5),
        "w_down": nrm(ks[17], (DEPTH, D_FF, D_MODEL), D_FF ** -0.5),
    }

def first_block(x, attn_norm_g, w_in, ret_decay_fwd, ret_decay_bwd, ret_norm_g,
              dq_norm_g, dk_norm_g, lambda_q1, lambda_k1, lambda_q2, lambda_k2,
              diff_norm_g, w_out, ffn_norm_g, w_gate, w_up, w_down):
    B, S, _ = x.shape
    slopes = alibi_slopes(DIFF_HEADS)
    split_at = [RET_WIDTH, 2 * RET_WIDTH, 3 * RET_WIDTH, 4 * RET_WIDTH,
                4 * RET_WIDTH + DIFF_WIDTH, 4 * RET_WIDTH + 2 * DIFF_WIDTH]
    for l in range(DEPTH):
        lam_init = 0.8 - 0.6 * math.exp(-0.3 * l)
        h = rms_norm(x, attn_norm_g[l])
        proj = h @ w_in[l]
        rq, rk, rv, rg, dq, dk, dv = jnp.split(proj, split_at, axis=-1)

        shp = (B, S, RET_HEADS, RET_HEAD_DIM)
        lg_f = -jnp.exp(ret_decay_fwd[l].astype(jnp.float32))
        lg_b = -jnp.exp(ret_decay_bwd[l].astype(jnp.float32))
        ret = retention_bidir(rq.reshape(shp), rk.reshape(shp) * RET_HEAD_DIM ** -0.5,
                              rv.reshape(shp), lg_f, lg_b)
        ret = rms_norm(ret, ret_norm_g[l]) * jax.nn.silu(rg.reshape(shp))
        ret = ret.reshape(B, S, RET_WIDTH)

        qk_shp = (B, S, DIFF_HEADS, 2, DIFF_HEAD_DIM)
        dqn = rms_norm(dq.reshape(qk_shp), dq_norm_g[l]) * DIFF_HEAD_DIM ** -0.5
        dkn = rms_norm(dk.reshape(qk_shp), dk_norm_g[l])
        lam = (jnp.exp(jnp.sum(lambda_q1[l].astype(jnp.float32) * lambda_k1[l].astype(jnp.float32)))
               - jnp.exp(jnp.sum(lambda_q2[l].astype(jnp.float32) * lambda_k2[l].astype(jnp.float32)))
               + lam_init)
        da = diff_attention(dqn, dkn, dv.reshape(B, S, DIFF_HEADS, DIFF_V_DIM), lam, slopes)
        da = (rms_norm(da, diff_norm_g[l]) * (1.0 - lam_init)).reshape(B, S, DIFF_WIDTH)

        x = x + jnp.concatenate([ret, da], axis=-1) @ w_out[l]

        h = rms_norm(x, ffn_norm_g[l])
        x = x + (jax.nn.silu(h @ w_gate[l]) * (h @ w_up[l])) @ w_down[l]
    return x


CHUNK_2 = 64
HEAD_DIM = 64
NORM_EPS = 1e-6

A_HEADS = 4
A_W = A_HEADS * HEAD_DIM
A_LEFT_CHUNKS = 8
A_MAX_REL = 128

B_HEADS = 4
B_Q_LORA = 256
B_KV_LORA = 128
B_NOPE = 64
B_ROPE = 32
B_V = 64
ROPE_THETA = 10000.0

C_HEADS = 4
C_W = C_HEADS * HEAD_DIM
FORGET_BIAS_MEAN = 3.0

CONV_CH = 256
CONV_K = 31

N_BRANCH = 4
BRANCH_W = 256
D_FF_2 = 4 * D_MODEL

IN_SPLITS = (A_W, A_W, A_W,
             B_Q_LORA, B_KV_LORA, B_ROPE,
             C_W, C_W, C_W, C_HEADS,
             CONV_CH, CONV_CH)
IN_COLS = sum(IN_SPLITS)


def _normal(key, shape, scale):
    return scale * jax.random.normal(key, shape, jnp.float32)

def rms_norm_2(x, g):
    xf = x.astype(jnp.float32)
    y = xf * lax.rsqrt(jnp.mean(xf * xf, axis=-1, keepdims=True) + NORM_EPS)
    return (y * g.astype(jnp.float32)).astype(x.dtype)

def layer_norm(x, g, b):
    xf = x.astype(jnp.float32)
    mu = jnp.mean(xf, axis=-1, keepdims=True)
    xc = xf - mu
    var = jnp.mean(xc * xc, axis=-1, keepdims=True)
    y = xc * lax.rsqrt(var + NORM_EPS) * g.astype(jnp.float32) + b.astype(jnp.float32)
    return y.astype(x.dtype)

def apply_rope(x, positions):
    half = x.shape[-1] // 2
    inv_freq = 1.0 / (ROPE_THETA ** (jnp.arange(half, dtype=jnp.float32) / half))
    ang = positions.astype(jnp.float32)[..., None] * inv_freq
    if x.ndim == 4:
        ang = ang[:, :, None, :]
    cos, sin = jnp.cos(ang), jnp.sin(ang)
    xf = x.astype(jnp.float32)
    x1, x2 = xf[..., :half], xf[..., half:]
    return jnp.concatenate([x1 * cos - x2 * sin, x2 * cos + x1 * sin], axis=-1).astype(x.dtype)

def chunk_band_attention(q, k, v, rel_table):
    b, s, h, d = q.shape
    nc = s // CHUNK_2
    w = A_LEFT_CHUNKS + 1
    qc = q.reshape(b, nc, CHUNK_2, h, d)

    def band(t):
        tc = t.reshape(b, nc, CHUNK_2, h, t.shape[-1])
        tp = jnp.pad(tc, ((0, 0), (A_LEFT_CHUNKS, 0), (0, 0), (0, 0), (0, 0)))
        return jnp.concatenate([tp[:, j:j + nc] for j in range(w)], axis=2)

    kb, vb = band(k), band(v)
    key_chunk = jnp.arange(nc)[:, None] + jnp.arange(w)[None, :] - A_LEFT_CHUNKS
    valid = jnp.repeat(key_chunk >= 0, CHUNK_2, axis=1)
    rel = (jnp.arange(CHUNK_2)[:, None] + A_LEFT_CHUNKS * CHUNK_2) - jnp.arange(w * CHUNK_2)[None, :]
    rel_idx = jnp.clip(rel, -A_MAX_REL, A_MAX_REL) + A_MAX_REL
    bias = rel_table[:, rel_idx].astype(jnp.float32)
    scores = jnp.einsum('bcqhd,bckhd->bchqk', qc, kb).astype(jnp.float32) * (d ** -0.5)
    scores = scores + bias[None, None]
    scores = jnp.where(valid[None, :, None, None, :], scores, -jnp.inf)
    p = jax.nn.softmax(scores, axis=-1).astype(v.dtype)
    out = jnp.einsum('bchqk,bckhd->bcqhd', p, vb)
    return out.reshape(b, s, h, -1)

def block_causal_attention(q, k, v, causal_unit, log_forget_cum=None):
    b, s, h, dk = q.shape
    nb = s // Q_BLOCK
    scale = dk ** -0.5
    key_unit = jnp.arange(s) // causal_unit
    qb = q.reshape(b, nb, Q_BLOCK, h, dk).swapaxes(0, 1)
    starts = jnp.arange(nb) * Q_BLOCK

    def attend(q_blk, start, f_blk):
        sc = jnp.einsum('bqhd,bkhd->bhqk', q_blk, k).astype(jnp.float32) * scale
        if f_blk is not None:
            f_k = log_forget_cum.transpose(0, 2, 1)[:, :, None, :]
            sc = sc + f_blk.transpose(0, 2, 1)[..., None] - f_k
        q_unit = (start + jnp.arange(Q_BLOCK)) // causal_unit
        mask = key_unit[None, :] <= q_unit[:, None]
        sc = jnp.where(mask[None, None], sc, -jnp.inf)
        p = jax.nn.softmax(sc, axis=-1).astype(v.dtype)
        return jnp.einsum('bhqk,bkhd->bqhd', p, v)

    if log_forget_cum is None:
        out = lax.map(lambda xs: attend(xs[0], xs[1], None), (qb, starts))
    else:
        fb = log_forget_cum.reshape(b, nb, Q_BLOCK, h).swapaxes(0, 1)
        out = lax.map(lambda xs: attend(xs[0], xs[1], xs[2]), (qb, starts, fb))
    return out.swapaxes(0, 1).reshape(b, s, h, -1)

def hybrid_layer(x, positions, g_mix, w_in, w_gate, b_gate, rel_bias, g_q_lat, w_uq, g_kv_lat, w_ukv,
                 b_forget, w_dw, b_dw, g_conv_ln, b_conv_ln, w_branch, w_o, g_ffn, w_up, w_down):
    b, s, _ = x.shape
    h = rms_norm_2(x, g_mix)
    split_points = [int(i) for i in np.cumsum(IN_SPLITS)[:-1]]
    (a_q, a_k, a_v, b_qlat, b_kvlat, b_krope,
     c_q, c_k, c_v, c_f, d_val, d_gate) = jnp.split(h @ w_in, split_points, axis=-1)

    def heads(t, n):
        return t.reshape(b, s, n, -1)

    out_a = chunk_band_attention(heads(a_q, A_HEADS), heads(a_k, A_HEADS), heads(a_v, A_HEADS), rel_bias)

    q = (rms_norm_2(b_qlat, g_q_lat) @ w_uq).reshape(b, s, B_HEADS, B_NOPE + B_ROPE)
    q = jnp.concatenate([q[..., :B_NOPE], apply_rope(q[..., B_NOPE:], positions)], axis=-1)
    kv = (rms_norm_2(b_kvlat, g_kv_lat) @ w_ukv).reshape(b, s, B_HEADS, B_NOPE + B_V)
    k_rot = apply_rope(b_krope, positions)
    k = jnp.concatenate([kv[..., :B_NOPE],
                         jnp.broadcast_to(k_rot[:, :, None, :], (b, s, B_HEADS, B_ROPE))], axis=-1)
    out_b = block_causal_attention(q, k, kv[..., B_NOPE:], CHUNK_2)

    log_f = jax.nn.log_sigmoid(c_f.astype(jnp.float32) + b_forget.astype(jnp.float32))
    f_cum = jnp.cumsum(log_f, axis=1)
    out_c = block_causal_attention(heads(c_q, C_HEADS), heads(c_k, C_HEADS), heads(c_v, C_HEADS), 1, f_cum)

    u = d_val * jax.nn.sigmoid(d_gate)
    u = lax.conv_general_dilated(u, w_dw[:, None, :], window_strides=(1,), padding=[(CONV_K - 1, 0)],
                                 dimension_numbers=('NWC', 'WIO', 'NWC'),
                                 feature_group_count=CONV_CH) + b_dw
    out_d = jax.nn.silu(layer_norm(u, g_conv_ln, b_conv_ln))

    branches = jnp.stack([out_a.reshape(b, s, BRANCH_W), out_b.reshape(b, s, BRANCH_W),
                          out_c.reshape(b, s, BRANCH_W), out_d], axis=2)
    proj = jnp.einsum('bsnc,ncd->bsnd', branches, w_branch)
    gates = jax.nn.sigmoid(h @ w_gate + b_gate).reshape(b, s, N_BRANCH, D_MODEL)
    x = x + jnp.sum(gates * proj, axis=2) @ w_o

    hf = rms_norm_2(x, g_ffn)
    x = x + jnp.square(jax.nn.relu(hf @ w_up)) @ w_down
    return x

def second_inputs(seed: int = 0) -> dict:
    key = jax.random.key(seed)
    ks = jax.random.split(key, 24)
    L = DEPTH
    x = _normal(ks[0], (BATCH, SEQ, D_MODEL), 1.0)
    offset = jax.random.randint(ks[1], (BATCH, 1), 0, 4 * SEQ, dtype=jnp.int32)
    positions = offset + jnp.arange(SEQ, dtype=jnp.int32)[None, :]
    return dict(
        x=x,
        positions=positions,
        g_mix=1.0 + _normal(ks[2], (L, D_MODEL), 0.05),
        w_in=_normal(ks[3], (L, D_MODEL, IN_COLS), D_MODEL ** -0.5),
        w_gate=_normal(ks[4], (L, D_MODEL, N_BRANCH * D_MODEL), D_MODEL ** -0.5),
        b_gate=_normal(ks[5], (L, N_BRANCH * D_MODEL), 0.02),
        rel_bias=_normal(ks[6], (L, A_HEADS, 2 * A_MAX_REL + 1), 0.2),
        g_q_lat=1.0 + _normal(ks[7], (L, B_Q_LORA), 0.05),
        w_uq=_normal(ks[8], (L, B_Q_LORA, B_HEADS * (B_NOPE + B_ROPE)), B_Q_LORA ** -0.5),
        g_kv_lat=1.0 + _normal(ks[9], (L, B_KV_LORA), 0.05),
        w_ukv=_normal(ks[10], (L, B_KV_LORA, B_HEADS * (B_NOPE + B_V)), B_KV_LORA ** -0.5),
        b_forget=FORGET_BIAS_MEAN + _normal(ks[11], (L, C_HEADS), 0.5),
        w_dw=_normal(ks[12], (L, CONV_K, CONV_CH), CONV_K ** -0.5),
        b_dw=_normal(ks[13], (L, CONV_CH), 0.02),
        g_conv_ln=1.0 + _normal(ks[14], (L, CONV_CH), 0.05),
        b_conv_ln=_normal(ks[15], (L, CONV_CH), 0.02),
        w_branch=_normal(ks[16], (L, N_BRANCH, BRANCH_W, D_MODEL), BRANCH_W ** -0.5),
        w_o=_normal(ks[17], (L, D_MODEL, D_MODEL), D_MODEL ** -0.5),
        g_ffn=1.0 + _normal(ks[18], (L, D_MODEL), 0.05),
        w_up=_normal(ks[19], (L, D_MODEL, D_FF_2), D_MODEL ** -0.5),
        w_down=_normal(ks[20], (L, D_FF_2, D_MODEL), D_FF_2 ** -0.5),
        g_final=1.0 + _normal(ks[21], (D_MODEL,), 0.05),
    )

def second_block(x, positions, g_mix, w_in, w_gate, b_gate, rel_bias, g_q_lat, w_uq, g_kv_lat, w_ukv,
              b_forget, w_dw, b_dw, g_conv_ln, b_conv_ln, w_branch, w_o, g_ffn, w_up, w_down, g_final):
    for l in range(DEPTH):
        x = hybrid_layer(x, positions, g_mix[l], w_in[l], w_gate[l], b_gate[l], rel_bias[l],
                         g_q_lat[l], w_uq[l], g_kv_lat[l], w_ukv[l], b_forget[l], w_dw[l], b_dw[l],
                         g_conv_ln[l], b_conv_ln[l], w_branch[l], w_o[l], g_ffn[l], w_up[l], w_down[l])
    return rms_norm_2(x, g_final)


def setup_inputs(seed=0):
    out = dict(first_inputs(seed))
    for name, value in second_inputs(seed + 1).items():
        if name != "x":
            out[name + "_2"] = value
    return out


def reference(
    x, attn_norm_g, w_in, ret_decay_fwd, ret_decay_bwd, ret_norm_g, dq_norm_g, dk_norm_g,
    lambda_q1, lambda_k1, lambda_q2, lambda_k2, diff_norm_g, w_out, ffn_norm_g, w_gate, w_up,
    w_down, positions_2, g_mix_2, w_in_2, w_gate_2, b_gate_2, rel_bias_2, g_q_lat_2, w_uq_2,
    g_kv_lat_2, w_ukv_2, b_forget_2, w_dw_2, b_dw_2, g_conv_ln_2, b_conv_ln_2, w_branch_2,
    w_o_2, g_ffn_2, w_up_2, w_down_2, g_final_2,
):
    x = first_block(
        x, attn_norm_g, w_in, ret_decay_fwd, ret_decay_bwd, ret_norm_g, dq_norm_g, dk_norm_g,
        lambda_q1, lambda_k1, lambda_q2, lambda_k2, diff_norm_g, w_out, ffn_norm_g, w_gate,
        w_up, w_down,
    )
    return second_block(
        x, positions_2, g_mix_2, w_in_2, w_gate_2, b_gate_2, rel_bias_2, g_q_lat_2, w_uq_2,
        g_kv_lat_2, w_ukv_2, b_forget_2, w_dw_2, b_dw_2, g_conv_ln_2, b_conv_ln_2, w_branch_2,
        w_o_2, g_ffn_2, w_up_2, w_down_2, g_final_2,
    )


_drawn_inputs = setup_inputs


def setup_inputs(seed=0):
    import zlib

    import numpy as np

    out = dict(_drawn_inputs(seed))
    spreads = {}
    factors = {'ret_norm_g': 4.038,
     'dq_norm_g': 3.789,
     'dk_norm_g': 3.652,
     'diff_norm_g': 3.439,
     'b_gate_2': 8.0,
     'rel_bias_2': 4.692,
     'g_q_lat_2': 8.0,
     'g_kv_lat_2': 7.835,
     'b_dw_2': 4.753,
     'g_conv_ln_2': 3.383,
     'b_conv_ln_2': 8.0}
    for name, (base, spread) in spreads.items():
        noise = np.random.default_rng([zlib.crc32(name.encode()), seed]).standard_normal(out[name].shape)
        drawn = base * np.exp(spread * noise) if base else spread * noise
        out[name] = __import__('jax').numpy.asarray(drawn.astype(out[name].dtype))
    for name, factor in factors.items():
        out[name] = (out[name] * factor).astype(out[name].dtype)
    return out
```

```python
from contextlib import ExitStack

import numpy as np
import concourse.bass as bass
from concourse import mybir

F32 = mybir.dt.float32
F32R = mybir.dt.float32r
I32 = mybir.dt.int32
ALU = mybir.AluOpType
ACT = mybir.ActivationFunctionType
AX = mybir.AxisListType

P = 128
SEQ = 256
R = SEQ // P
D = 1024
KT = D // P
DEPTH = 2
EPS = 1e-6
NB = 512
RING = 4
AHEAD = 3

RETW, HD = 512, 64
RH = RETW // HD
DH, DVD = 4, 128
PROJ1 = 4 * RETW + 3 * 512
RQ, RK, RV, RG, DQ, DK, DV = (i * 512 for i in range(7))
FF1 = 2816
HALF = NB // 2
PROJ2 = 2468
AQ, AK, AV, QL, KL, KR, CQ, CK, CV, CF, DVAL, DGATE = (
    0, 256, 512, 768, 1024, 1152, 1184, 1440, 1696, 1952, 1956, 2212)
NBR, BW = 4, 256
FF2 = 4096
TAPS = 31
BQD = 96
CAD = 66
MASKED = -1e30

KTS1 = [4] * 14 + [4] * 4 + [4] * 22 + [4, 4, 4, 4, 4, 2] * 2
KTS2 = [4] * 10 + [2, 1] + [4, 4, 2] * 8 + [4] * 4 + [4] * 16 + [4] * 16
assert len(KTS1) % RING == 0 and len(KTS2) % RING == 0
BLOCKS1, BLOCKS2 = 7 + 1 + 1 + 2 + 11 + 2, 5 + 2 + 2 + 16 + 2 + 8 + 2 + 1
TURNS1, TURNS2 = 8 + 4 + 4 + 4 + 11 + 4 + 1, 2 + 2 + 1 + 1 + 10 + 12 + 1 + 4 + 4 + 4 + 16 + 4 + 1
assert not (BLOCKS1 % 2 or BLOCKS2 % 2 or TURNS1 % 2 or TURNS2 % 2)

C_ID, C_TRI, C_ANTI, C_DF, C_DB, C_DA = 0, 128, 256, 384, 896, 1408
C_MCH, C_MCA, C_INV, C_NEG, C_LI, C_OML, C_ONE = 1920, 2304, 2688, 2704, 2736, 2738, 2740
C_W = 2740 + 128


def shape_constants():
    c = np.zeros((P, C_W), np.float32)
    p = np.arange(P)
    c[:, C_ID:C_ID + P] = np.eye(P)
    c[:, C_TRI:C_TRI + P] = p[:, None] <= p[None, :]
    c[:, C_ANTI:C_ANTI + P] = np.eye(P)[::-1]
    t = np.arange(SEQ)
    for s in range(R):
        d = t[None, :] - (s * P + p)[:, None]
        c[:, C_DF + s * SEQ:C_DF + (s + 1) * SEQ] = np.maximum(d, 0)
        c[:, C_DB + s * SEQ:C_DB + (s + 1) * SEQ] = np.maximum(-d, 0)
        c[:, C_DA + s * SEQ:C_DA + (s + 1) * SEQ] = np.abs(d)
    for at, unit in ((C_MCH, 64), (C_MCA, 1)):
        k = np.arange(P)
        c[:, at:at + P] = np.where(k[None, :] // unit <= p[:, None] // unit, 0.0, MASKED)
        q = P + p
        c[:, at + P:at + P + SEQ] = np.where(t[None, :] // unit <= q[:, None] // unit, 0.0, MASKED)
    c[:, C_INV:C_INV + 16] = 1.0 / (np.float32(10000.0) ** (np.arange(16, dtype=np.float32) / np.float32(16)))
    c[:, C_NEG:C_NEG + 32] = -0.5
    for l in range(DEPTH):
        li = 0.8 - 0.6 * np.exp(-0.3 * l)
        c[:, C_LI + l] = li
        c[:, C_OML + l] = 1.0 - li
    c[:, C_ONE:C_ONE + P] = 1.0
    return c


S_X, S_XM, S_XR = 0, 4, 6
S_Q, S_QR = 8, 40
S_NM, S_RS, S_RC = 72, 80, 88
S_O, S_OR, S_P, S_PR = 96, 112, 128, 136
S_L, S_LR = 144, 148
S_Z, S_M, S_A, S_LF = 152, 160, 168, 176
S_NM2, S_RS2, S_RC2 = 184, 188, 212
S_BN, S_MV, S_VR = 236, 248, 252
STEPS_ACT1, STEPS_ACT2 = 4, 8
STEPS_DVE1, STEPS_DVE2 = 26, 82
STEPS_POOL1, STEPS_POOL2 = 9, 24
SMALL_LOADS = 8 + 6 + 7 + 4 + 3

B_RG, B_DG, B_QG, B_KG = 0, 128, 384, 512
B_DF, B_DB, B_FB = 640, 656, 672
B_W = 680


class Place:

    def __init__(self, e):
        self.e, self.base, self.k = e, {}, {}

    def now(self, name):
        return self.base.get(name, 0) + self.k.get(name, 0)

    def next(self, name, n=1):
        self.k[name] = self.k.get(name, 0) + n
        return self.now(name)

    def index(self, name):
        return self.k.get(name, 0)

    def rounds(self, n, per):
        base, k = dict(self.base), dict(self.k)
        with self.e.Fori(0, n) as i:
            for name, by in per.items():
                self.base[name] = i * by + base.get(name, 0)
            yield i
            grown = {x: self.k[x] - k.get(x, 0) for x in self.k if self.k[x] != k.get(x, 0)}
            assert grown == {x: y for x, y in per.items() if y}, (self.e, grown, per)
        self.base = base
        self.k = {x: k.get(x, 0) + n * per.get(x, 0) for x in {*k, *per}}


def bcast(row, at, n):
    return bass.AP(row.tensor, at, [[0, P], [1, n]])


def build(nc, t, out):
    with ExitStack() as ctx:
        def sb(name, shape, dt=F32):
            return ctx.enter_context(nc.sbuf_tensor(name, shape, dt))

        def sem(name):
            return ctx.enter_context(nc.semaphore(name))

        w_raw = sb("w_raw", [P, RING, 4, NB])
        w_hi = sb("w_hi", [P, RING, 4, NB], F32R)
        w_lo = sb("w_lo", [P, RING, 4, NB], F32R)
        x = sb("x", [P, R, D])
        hT_hi = sb("hT_hi", [P, KT, SEQ], F32R)
        hT_lo = sb("hT_lo", [P, KT, SEQ], F32R)
        cst = sb("cst", [P, C_W])
        small = sb("small", [P, B_W])
        gcols = sb("gcols", [P, 72])
        ccols = sb("ccols", [P, DEPTH * 65])
        rope = sb("rope", [P, 2, R, 16])
        stat = sb("stat", [P, 256])
        lam = sb("lam", [P, 4])

        arena_bytes = 68 * 1024
        base_at = -(-nc.sbuf_base // 32) * 32
        arena = sb("arena", [P, arena_bytes // 4 + 8])

        def over(name, shape, kb, dt=F32):
            n = 4
            for s in shape[1:]:
                n *= s
            at = int(kb * 1024)
            assert at + n <= arena_bytes, (name, at + n)
            return nc.alloc_sbuf_tensor_at(name, shape, dt, offset=base_at + at)

        proj1 = over("proj1", [P, R, PROJ1], 0)
        mixed1 = proj1[:, :, 0:D]
        qkT1 = over("qkT1", [P, 8, 512], 28)
        sq1 = over("sq1", [P, R, D], 44)
        decay = over("decay", [P, 2, R * SEQ], 52)
        ret_p = over("ret_p", [P, 2, R * SEQ], 56)
        soft1 = over("soft1", [P, 2, 2, R * SEQ], 52)
        comb1 = over("comb1", [P, R, SEQ], 60)
        combT1 = over("combT1", [P, R, SEQ], 62)
        pooltmp = over("pooltmp", [P, 2 * SEQ], 64)
        hid1T_hi = over("hid1T_hi", [P, FF1 // P, SEQ], 0, F32R)
        hid1T_lo = over("hid1T_lo", [P, FF1 // P, SEQ], 22, F32R)
        gate1 = over("gate1", [P, R, HALF], 44)
        hid1 = over("hid1", [P, R, HALF], 46)
        proj2 = over("proj2", [P, R, PROJ2], 0)
        branches = over("branches", [P, R, D], 19.5)
        hankel = over("hankel", [P, 4, SEQ], 19.5)
        qkT2 = over("qkT2", [P, 3, 512], 27.5)
        lat_hi = over("lat_hi", [P, 3, SEQ], 33.5, F32R)
        lat_lo = over("lat_lo", [P, 3, SEQ], 36.5, F32R)
        soft2 = over("soft2", [P, 2, 384], 33.5)
        softT2 = over("softT2", [P, 2, 384], 36.5)
        abias = over("abias", [P, 4, 384], 39.5)
        qB = over("qB", [P, R, 4, BQD], 45.5)
        kB = over("kB", [P, R, 4, BQD], 48.5)
        kvB = over("kvB", [P, R, 512], 51.5)
        cqa = over("cqa", [P, R, 4, CAD], 55.5)
        cka = over("cka", [P, R, 4, CAD], 57.625)
        uT = over("uT", [P, 2, SEQ + TAPS - 1], 59.75)
        yT = over("yT", [P, 2, SEQ], 62)
        convrow = over("convrow", [P, 3, 256], 64)
        conv_y = over("conv_y", [P, R, 256], 55.5)
        ropetmp = over("ropetmp", [P, 4, 64], 67.5 - 0.5)
        bgate = over("bgate", [P, NBR, D], 0)
        obT_hi = over("obT_hi", [P, KT, SEQ], 28, F32R)
        obT_lo = over("obT_lo", [P, KT, SEQ], 36, F32R)
        gate2 = over("gate2", [P, R, NB], 44)
        term2 = over("term2", [P, R, NB], 48)
        mix2 = over("mix2", [P, R, D], 52)
        hid2T_hi = over("hid2T_hi", [P, FF2 // P, SEQ], 0, F32R)
        hid2T_lo = over("hid2T_lo", [P, FF2 // P, SEQ], 32, F32R)
        hid2 = over("hid2", [P, R, NB], 64)
        grows = over("grows", [72, P], 0)
        crows = over("crows", [P, DEPTH, P], 1)
        lrows = over("lrows", [P, 4, DEPTH * HD], 3)
        lprod = over("lprod", [P, 2, DEPTH * HD], 5)
        pos_i = over("pos_i", [P, R], 7, I32)
        ropet = over("ropet", [P, 6, R, 16], 8)
        gfin = over("gfin", [P, D], 64)
        outrow = over("outrow", [P, R, D], 32)

        ident = cst[:, C_ID:C_ID + P]
        junk = sb("junk", [P, NB])
        relu = [junk, cst[:, C_DB:C_DB + NB]]

        bank = [ctx.enter_context(nc.psum_tensor(f"bank{i}", [P, NB], F32)) for i in range(8)]
        acc, turn, score = [bank[0:2], bank[2:4]], bank[4:6], bank[6:8]

        consts_in = sem("consts_in")
        small_in = sem("small_in")
        x_in = sem("x_in")
        slab_in = [sem(f"slab_in{i}") for i in range(RING)]
        hi_ready = sem("hi_ready")
        lo_ready = sem("lo_ready")
        slab_used = sem("slab_used")
        acc_free = sem("acc_free")
        turned = sem("turned")
        turn_hi = sem("turn_hi")
        turn_free = sem("turn_free")
        scores = sem("scores")
        scores_out = sem("scores_out")
        soft_ready = sem("soft_ready")
        probs = sem("probs")
        heads_out = sem("heads_out")
        decay_arg = sem("decay_arg")
        decay_ready = sem("decay_ready")
        squares = sem("squares")
        mean_ready = sem("mean_ready")
        rstd_ready = sem("rstd_ready")
        act_done = sem("act_done")
        dve_ready = sem("dve_ready")
        pool_ready = sem("pool_ready")
        pool_job = sem("pool_job")
        conv_in = sem("conv_in")
        act_job = sem("act_job")
        conv_out = sem("conv_out")
        act_step = sem("act_step")
        dve_step = sem("dve_step")
        pool_step = sem("pool_step")
        held = sem("held")
        layer_in = sem("layer_in")
        bgate_in = sem("bgate_in")
        out_ready = sem("out_ready")
        out_done = sem("out_done")
        block = ctx.enter_context(nc.Block())

        @block.sync
        def _(sp):
            q = Place(sp)
            sp.dma_start(x[:, :, :], t["x"].rearrange("b (r p) d -> p (b r) d", p=P)).then_inc(x_in, 16)
            sp.dma_start(cst[:, :], t["consts"]).then_inc(consts_in, 16)

            def slab(*parts):
                assert len(parts) == 2
                sp.wait_ge(lo_ready, q.next("slab"))
                for dst, src in parts:
                    s = (q.index("slab") - 1) % RING
                    sp.dma_start(dst(w_raw[:, s]), src).then_inc(slab_in[s], 16)

            def rows(w, k0, n, c0, cols):
                def part(a, b):
                    src = w[(k0 + a) * P:(k0 + b) * P, bass.ds(c0, cols)]
                    return lambda s: s[:, a:b, 0:cols], src.rearrange("(c p) n -> p c n", p=P)
                if n == 1:
                    h = cols // 2
                    src = w[k0 * P:(k0 + 1) * P, :]
                    return [(lambda s: s[:, 0, 0:h], src[:, c0:c0 + h]),
                            (lambda s: s[:, 0, h:cols], src[:, c0 + h:c0 + cols])]
                return [part(0, n // 2), part(n // 2, n)]

            def halves(w, k0, c0):
                src = w[k0 * P:(k0 + 4) * P, bass.ds(c0, HALF)]
                return src.rearrange("(c p) n -> p c n", p=P)

            for l in q.rounds(DEPTH, dict(slab=len(KTS1))):
                w = {n: t[n][bass.ds(l, 1)].rearrange("o k n -> (o k) n") for n in ("w_in", "w_out", "w_gate", "w_up", "w_down")}
                for i in q.rounds(3, dict(slab=4)):
                    for b in range(2):
                        for k0 in (0, 4):
                            slab(*rows(w["w_in"], k0, 4, i * (2 * NB) + b * NB, NB))
                for k0 in (0, 4):
                    slab(*rows(w["w_in"], k0, 4, 6 * NB, NB))
                for b in range(2):
                    for k0 in (0, 4):
                        slab(*rows(w["w_out"], k0, 4, b * NB, NB))

                def gate_up(c0):
                    for k0 in (0, 4):
                        slab((lambda s: s[:, :, 0:HALF], halves(w["w_gate"], k0, c0)),
                             (lambda s: s[:, :, HALF:NB], halves(w["w_up"], k0, c0)))

                gate_up(0)
                for i in q.rounds(5, dict(slab=4)):
                    gate_up(i * (2 * HALF) + HALF)
                    gate_up(i * (2 * HALF) + 2 * HALF)
                for b in range(2):
                    for k0 in range(0, 22, 4):
                        slab(*rows(w["w_down"], k0, min(4, 22 - k0), b * NB, NB))

            for l in q.rounds(DEPTH, dict(slab=len(KTS2))):
                w = {n: t[n + "_2"][bass.ds(l, 1)].rearrange("o k n -> (o k) n")
                     for n in ("w_in", "w_gate", "w_uq", "w_ukv", "w_o", "w_up", "w_down")}
                w["w_branch"] = t["w_branch_2"][bass.ds(l, 1)].rearrange("o b k n -> (o b k) n")
                for b in range(5):
                    for k0 in (0, 4):
                        slab(*rows(w["w_in"], k0, 4, b * NB, min(NB, PROJ2 - b * NB)))
                    if b == 3:
                        sp.dma_start(hankel[:, :, :], bass.AP(
                            t["rel_ext"].tensor, l * (4 * 384), [[1, P], [384, 4], [1, SEQ]])).then_inc(layer_in, 16)
                        for n, row in enumerate(("b_dw_2", "g_conv_ln_2", "b_conv_ln_2")):
                            sp.dma_start(convrow[:, n, :], bcast(t[row], l * 256, 256)).then_inc(layer_in, 16)
                slab(*rows(w["w_uq"], 0, 2, 0, 384))
                slab(*rows(w["w_ukv"], 0, 1, 0, 512))
                for b in range(2):
                    for n in range(NBR):
                        for k0 in (0, 4):
                            slab(*rows(w["w_gate"], k0, 4, n * D + b * NB, NB))
                        slab(*rows(w["w_branch"], 2 * n, 2, b * NB, NB))
                for b in range(2):
                    for k0 in (0, 4):
                        slab(*rows(w["w_o"], k0, 4, b * NB, NB))
                for i in q.rounds(4, dict(slab=4)):
                    for b in range(2):
                        for k0 in (0, 4):
                            slab(*rows(w["w_up"], k0, 4, i * (2 * NB) + b * NB, NB))
                for b in range(2):
                    for k0 in range(0, 32, 4):
                        slab(*rows(w["w_down"], k0, 4, b * NB, NB))
            for s in range(AHEAD):
                sp.wait_ge(lo_ready, q.next("slab"))
                sp.sem_inc(slab_in[s], 32)
            sp.wait_ge(acc_free, 2 + DEPTH * BLOCKS1 + DEPTH * BLOCKS2 - 2)
            sp.dma_start(gfin[:, :], bcast(t["g_final_2"], 0, D)).then_inc(x_in, 16)
            sp.wait_ge(out_ready, 1)
            sp.dma_start(out.rearrange("b (r p) d -> p (b r) d", p=P), outrow[:, :, :]).then_inc(out_done, 16)
            sp.wait_ge(out_done, 16)

        def hold(e):
            e.sem_inc(held, 1)

        def rows_of(r):
            return slice(r * P, (r + 1) * P)

        @block.tensor
        def _(pe):
            q = Place(pe)
            pe.sem_inc(slab_used, RING)
            pe.wait_ge(consts_in, 16)

            def open_block():
                pe.wait_ge(acc_free, q.next("blk"))
                return acc[(q.index("blk") - 1) % 2]

            def read_out(blk):
                pe.wait_ge(acc_free, blk + 2)

            def slab_product(a, hi, lo, kts, cols, first, last):
                pe.wait_ge(lo_ready, q.next("slab") + RING)
                s = (q.index("slab") - 1) % RING
                for j, kt in enumerate(kts):
                    for r in range(R):
                        begin, end = first and j == 0, last and j == len(kts) - 1
                        o = a[r][:, 0:cols]
                        pe.matmul(o, hi[:, kt, rows_of(r)], w_hi[:, s, j, 0:cols], start=begin, stop=False)
                        pe.matmul(o, hi[:, kt, rows_of(r)], w_lo[:, s, j, 0:cols], start=False, stop=False)
                        mm = pe.matmul(o, lo[:, kt, rows_of(r)], w_hi[:, s, j, 0:cols], start=False, stop=end)
                mm.then_inc(slab_used, 1)

            def wide_block(cols=NB):
                a = open_block()
                slab_product(a, hT_hi, hT_lo, range(0, 4), cols, True, False)
                slab_product(a, hT_hi, hT_lo, range(4, 8), cols, False, True)

            def turn_group(pieces, skip=0):
                pe.wait_ge(turn_free, q.next("turn"))
                b = turn[(q.index("turn") - 1) % 2]
                for src, col in pieces:
                    n, m = src.shape[0], src.shape[1]
                    tr = pe.transpose(b[0:m, col:col + n], src, ident[0:n, 0:n])
                tr.then_inc(turned, 1 + skip)
                q.next("turn", skip)
                return q.now("turn")

            def all_turned():
                pe.wait_ge(turn_free, q.now("turn") + 2)

            def turn_model(src, groups, skip=0):
                for g in groups:
                    turn_group([(src[:, r, kt * P:(kt + 1) * P], (kt % 2) * SEQ + r * P)
                                for kt in (2 * g, 2 * g + 1) for r in range(R)], skip if g == 3 else 0)

            def turn_x(b, skip=0):
                turn_model(x, (2 * b, 2 * b + 1), skip)

            def turn_pair(qsrc, ksrc):
                return turn_group([(qsrc(0), 0), (qsrc(1), P), (ksrc(0), 2 * P), (ksrc(1), 3 * P)])

            def score_bank():
                pe.wait_ge(scores_out, q.next("scores"))
                return score[(q.index("scores") - 1) % 2]

            pe.wait_ge(small_in, 16 * SMALL_LOADS)
            turn_group([(grows[:, :], 0)])
            turn_group([(crows[0:65, l, :], l * 65) for l in range(DEPTH)])
            pe.wait_ge(x_in, 16)
            turn_model(x, range(4))

            for l in q.rounds(DEPTH, dict(slab=len(KTS1), blk=BLOCKS1, turn=TURNS1, scores=16, pool=3, dve=4)):
                all_turned()
                wide_block()
                for _i in q.rounds(3, dict(slab=4, blk=2)):
                    wide_block()
                    wide_block()
                read_out(q.now("blk"))
                group = [turn_pair(lambda r, j=j: proj1[:, r, RQ + j * P:RQ + (j + 1) * P],
                                   lambda r, j=j: proj1[:, r, RK + j * P:RK + (j + 1) * P]) for j in range(4)]
                o = open_block()

                def ret_scores(h):
                    b, e, j = score_bank(), h % 2, h // 2
                    pe.wait_ge(turn_free, group[j] + 2)
                    for st in range(R):
                        mm = pe.matmul(b[:, st * SEQ:(st + 1) * SEQ],
                                       qkT1[64 * e:64 * e + 64, j, SEQ + st * P:SEQ + (st + 1) * P],
                                       qkT1[64 * e:64 * e + 64, j, 0:SEQ], start=True, stop=True)
                    mm.then_inc(scores, 1)
                    return q.now("scores")

                def ret_values(h, item):
                    pe.wait_ge(scores_out, item + 2)
                    for r in range(R):
                        for st in range(R):
                            mm = pe.matmul(o[r][:, h * HD:(h + 1) * HD],
                                           ret_p[:, h % 2, st * SEQ + r * P:st * SEQ + (r + 1) * P],
                                           proj1[:, st, RV + h * HD:RV + (h + 1) * HD],
                                           start=st == 0, stop=st == R - 1)
                    return mm

                item = ret_scores(0)
                for h in range(1, RH + 1):
                    last = item
                    if h < RH:
                        item = ret_scores(h)
                    mm = ret_values(h - 1, last)
                    if 3 < h < RH:
                        if h == 4:
                            pe.wait_ge(pool_ready, q.next("pool"))
                        c = (h - 4) * P
                        group.append(turn_pair(lambda r: proj1[:, r, DQ + c:DQ + c + P],
                                               lambda r: proj1[:, r, DK + c:DK + c + P]))
                mm.then_inc(heads_out, 1)
                o = open_block()

                def diff_scores(h):
                    for m in range(2):
                        b = score_bank()
                        pe.wait_ge(turn_free, group[4 + h] + 2)
                        for r in range(R):
                            mm = pe.matmul(b[:, r * SEQ:(r + 1) * SEQ],
                                           qkT1[64 * m:64 * m + 64, 4 + h, rows_of(r)],
                                           qkT1[64 * m:64 * m + 64, 4 + h, SEQ:2 * SEQ], start=True, stop=True)
                        mm.then_inc(scores, 1)

                diff_scores(0)
                for h in range(DH):
                    if h + 1 < DH:
                        diff_scores(h + 1)
                    pe.wait_ge(dve_ready, q.next("dve"))
                    n = turn_group([(comb1[:, r, kt * P:(kt + 1) * P], kt * SEQ + r * P)
                                    for kt in range(R) for r in range(R)])
                    pe.wait_ge(turn_free, n + 2)
                    for r in range(R):
                        for kt in range(R):
                            mm = pe.matmul(o[r][:, h * DVD:(h + 1) * DVD], combT1[:, kt, rows_of(r)],
                                           proj1[:, kt, DV + h * DVD:DV + (h + 1) * DVD],
                                           start=kt == 0, stop=kt == R - 1)
                mm.then_inc(heads_out, 1)
                for half in range(2):
                    pe.wait_ge(pool_ready, q.next("pool"))
                    turn_model(mixed1, (2 * half, 2 * half + 1))
                all_turned()
                wide_block()
                wide_block()
                read_out(q.now("blk"))
                turn_model(x, range(4))
                def turn_hid1(blk):
                    read_out(blk)
                    turn_group([(hid1[:, r, c * P:(c + 1) * P], c * SEQ + r * P)
                                for c in range(2) for r in range(R)])

                all_turned()
                wide_block()
                for _i in q.rounds(5, dict(slab=4, blk=2, turn=2)):
                    for _ in range(2):
                        wide_block()
                        turn_hid1(q.now("blk") - 1)
                turn_hid1(q.now("blk"))
                all_turned()
                for b in range(2):
                    a = open_block()
                    for n in range(6):
                        kts = range(4 * n, min(4 * n + 4, FF1 // P))
                        slab_product(a, hid1T_hi, hid1T_lo, kts, NB, n == 0, n == 5)
                        if b == 1 and n == 1:
                            read_out(q.now("blk") - 1)
                            turn_x(0)
                read_out(q.now("blk"))
                turn_x(1, skip=1)
            q.next("probs", DEPTH * DH)
            for l in q.rounds(DEPTH, dict(slab=len(KTS2), blk=BLOCKS2, turn=TURNS2, scores=12, pool=2, dve=5,
                                          layer_in=64, probs=12, conv=1)):
                all_turned()
                for b in range(5):
                    wide_block(min(NB, PROJ2 - b * NB))
                projected = q.now("blk")
                pe.wait_ge(layer_in, q.next("layer_in", 64))
                for g in range(2):
                    pe.wait_ge(turn_free, q.next("turn"))
                    for h in (2 * g, 2 * g + 1):
                        mm = pe.matmul(turn[(q.index("turn") - 1) % 2][:, (h % 2) * SEQ:(h % 2 + 1) * SEQ],
                                       cst[:, C_ANTI:C_ANTI + P], hankel[:, h, :], start=True, stop=True)
                    mm.then_inc(turned, 1)
                read_out(projected)
                turn_group([(proj2[:, r, QL + kt * P:QL + (kt + 1) * P], kt * SEQ + r * P)
                            for kt in range(2) for r in range(R)])
                lat = turn_group([(proj2[:, r, KL:KL + P], r * P) for r in range(R)])
                pe.wait_ge(turn_free, lat + 2)
                slab_product(open_block(), lat_hi, lat_lo, (0, 1), 384, True, True)
                slab_product(open_block(), lat_hi, lat_lo, (2,), 512, True, True)
                latent = q.now("blk")
                pe.wait_ge(dve_ready, q.next("dve"))
                turn_group([(proj2[:, r, DVAL + c * P:DVAL + (c + 1) * P], c * SEQ + r * P)
                            for c in range(2) for r in range(R)])
                pe.wait_ge(dve_ready, q.next("dve"))
                pe.wait_ge(turn_free, q.next("turn"))
                b = turn[(q.index("turn") - 1) % 2]
                logf = stat[:, S_LF:S_LF + 8].rearrange("p (r h) -> p r h", r=R)
                tri, ones = cst[:, C_TRI:C_TRI + P], cst[:, C_ONE:C_ONE + P]
                pe.matmul(b[:, 0:4], tri, logf[:, 0, :], start=True, stop=True)
                pe.matmul(b[:, 4:8], ones, logf[:, 0, :], start=True, stop=False)
                pe.matmul(b[:, 4:8], tri, logf[:, 1, :], start=False, stop=True).then_inc(turned, 1)
                group = {}

                def turn_head(g):
                    if g < 2:
                        group[g] = turn_pair(lambda r: proj2[:, r, AQ + g * P:AQ + (g + 1) * P],
                                             lambda r: proj2[:, r, AK + g * P:AK + (g + 1) * P])
                    elif g < 6:
                        if g == 2:
                            pe.wait_ge(pool_ready, q.next("pool"))
                            pe.wait_ge(dve_ready, q.next("dve"))
                        group[g] = turn_pair(lambda r: cqa[:, r, g - 2, :], lambda r: cka[:, r, g - 2, :])
                    else:
                        if g == 6:
                            read_out(latent)
                            pe.wait_ge(pool_ready, q.next("pool"))
                        group[g] = turn_pair(lambda r: qB[:, r, g - 6, :], lambda r: kB[:, r, g - 6, :])

                def head_scores(h):
                    g = h // 2 if h < 4 else h - 2
                    b = score_bank()
                    pe.wait_ge(turn_free, group[g] + 2)
                    at, d = (64 * (h % 2), HD) if h < 4 else (0, CAD) if h < 8 else (0, BQD)
                    s = qkT2[at:at + d, g % 3, :]
                    pe.matmul(b[:, 0:P], s[:, 0:P], s[:, 2 * P:3 * P], start=True, stop=True)
                    pe.matmul(b[:, P:3 * P], s[:, P:2 * P], s[:, 2 * P:4 * P], start=True, stop=True).then_inc(scores, 1)

                def head_values(h, o):
                    pe.wait_ge(probs, q.next("probs"))
                    s = soft2[:, h % 2, :]
                    n = turn_group([(s[:, k * P:(k + 1) * P], k * P) for k in range(3)])
                    pe.wait_ge(turn_free, n + 2)
                    s = softT2[:, h % 2, :]

                    def v(kt):
                        if h < 4:
                            return proj2[:, kt, AV + h * HD:AV + (h + 1) * HD]
                        if h < 8:
                            return proj2[:, kt, CV + (h - 4) * HD:CV + (h - 3) * HD]
                        return kvB[:, kt, (h - 8) * P + HD:(h - 7) * P]
                    c = (h % 8) * HD
                    pe.matmul(o[0][:, c:c + HD], s[:, 0:P], v(0), start=True, stop=True)
                    pe.matmul(o[1][:, c:c + HD], s[:, P:2 * P], v(0), start=True, stop=False)
                    return pe.matmul(o[1][:, c:c + HD], s[:, 2 * P:3 * P], v(1), start=False, stop=True)

                turn_head(0)
                turn_head(1)
                o = open_block()
                for h in range(13):
                    if h < 12:
                        head_scores(h)
                        if 2 <= h < 10:
                            turn_head(h)
                    if h == 9:
                        o = open_block()
                    if h >= 1:
                        mm = head_values(h - 1, o)
                        if h in (8, 12):
                            mm.then_inc(heads_out, 1)
                pe.wait_ge(dve_ready, q.next("dve"))
                turn_group([(yT[:, c, rows_of(r)], r * 256 + c * P) for r in range(R) for c in range(2)])
                read_out(q.now("blk"))
                pe.wait_ge(conv_out, q.next("conv"))
                turn_model(branches, range(4))
                all_turned()
                for b in range(2):
                    for n in range(NBR):
                        wide_block()
                        slab_product(open_block(), obT_hi, obT_lo, (2 * n, 2 * n + 1), NB, True, True)
                pe.wait_ge(dve_ready, q.next("dve"))
                turn_model(mix2, range(4))
                all_turned()
                wide_block()
                wide_block()
                read_out(q.now("blk"))
                turn_model(x, range(4))
                def turn_hid2(blk):
                    read_out(blk)
                    for g in range(2):
                        turn_group([(hid2[:, r, c * P:(c + 1) * P], (c % 2) * SEQ + r * P)
                                    for c in (2 * g, 2 * g + 1) for r in range(R)])

                all_turned()
                wide_block()
                for _i in q.rounds(3, dict(slab=4, blk=2, turn=4)):
                    for _ in range(2):
                        wide_block()
                        turn_hid2(q.now("blk") - 1)
                wide_block()
                turn_hid2(q.now("blk") - 1)
                turn_hid2(q.now("blk"))
                all_turned()
                for b in range(2):
                    a = open_block()
                    for n in range(8):
                        slab_product(a, hid2T_hi, hid2T_lo, range(4 * n, 4 * n + 4), NB, n == 0, n == 7)
                        if b == 1 and n == 1:
                            read_out(q.now("blk") - 1)
                            turn_x(0)
                read_out(q.now("blk"))
                turn_x(1, skip=1)
                q.next("blk")

        @block.scalar
        def _(act):
            q = Place(act)

            def load(dst, src):
                act.dma_start(dst, src).then_inc(small_in, 16)

            for l in range(DEPTH):
                for n, name in enumerate(("attn_norm_g", "ffn_norm_g")):
                    at = 8 * (2 * l + n)
                    load(grows[at:at + 8, :], t[name][l].rearrange("(k p) -> k p", p=P))
                    load(grows[32 + at:40 + at, :], t[("g_mix_2", "g_ffn_2")[n]][l].rearrange("(k p) -> k p", p=P))
                load(crows[0:62, l, :], t["w_dw_2"][l].rearrange("k (c p) -> (k c) p", p=P))
                load(crows[62:64, l, :], t["g_q_lat_2"][l].rearrange("(k p) -> k p", p=P))
                load(crows[64:65, l, :], t["g_kv_lat_2"][l].rearrange("(k p) -> k p", p=P))
            for at, name, n in ((B_RG, "ret_norm_g", HD), (B_DG, "diff_norm_g", DVD), (B_QG, "dq_norm_g", HD),
                                (B_KG, "dk_norm_g", HD), (B_DF, "ret_decay_fwd", RH), (B_DB, "ret_decay_bwd", RH),
                                (B_FB, "b_forget_2", 4)):
                load(small[:, at:at + DEPTH * n], bcast(t[name], 0, DEPTH * n))
            for n, name in enumerate(("lambda_q1", "lambda_k1", "lambda_q2", "lambda_k2")):
                load(lrows[:, n, :], bcast(t[name], 0, DEPTH * HD))
            load(grows[64:72, :], t["g_final_2"].rearrange("(k p) -> k p", p=P))
            for r in range(R):
                load(pos_i[:, r:r + 1], bass.AP(t["positions_2"].tensor, r * P, [[1, P], [1, 1]]))

            def step(ins):
                ins.then_inc(act_step, 1)
                act.wait_ge(act_step, q.next("step"))

            def split_hi(kts=4):
                s = q.index("slab") % RING
                q.next("slab")
                act.wait_ge(slab_in[s], q.next(f"in{s}", 32))
                act.wait_ge(slab_used, q.now("slab"))
                act.copy(w_hi[:, s, 0:kts, :], w_raw[:, s, 0:kts, :]).then_inc(hi_ready, 1)

            def used(n):
                act.wait_ge(slab_used, q.next("used", n) + RING)

            def block_of():
                q.next("blk")
                return acc[(q.index("blk") - 1) % 2]

            def read_out(blk):
                act.wait_ge(acc_free, blk + 2)

            def next_turn(skip=0):
                act.wait_ge(turned, q.next("turn") + skip)
                b = turn[(q.index("turn") - 1) % 2]
                q.next("turn", skip)
                return b

            def take_hi(dst):
                b = next_turn()
                n = dst.shape[1] * dst.shape[2]
                act.copy(dst, b[:, 0:n].rearrange("p (c n) -> p c n", n=SEQ)).then_inc(turn_hi, 1)

            def take_model(src_tiles, gain=None, skip=0):
                b = next_turn(skip)
                for j, kt in enumerate(src_tiles):
                    g = gcols[:, bass.ds(gain + kt, 1)]
                    ins = act.activation(hT_hi[:, kt, :], b[:, j * SEQ:(j + 1) * SEQ], ACT.Copy, scale=g)
                ins.then_inc(turn_hi, 1)

            def square_x(b):
                for r in range(R):
                    ins = act.activation(junk[:, :], x[:, r, b * NB:(b + 1) * NB], ACT.Square,
                                         accum_out=stat[:, S_X + 2 * b + r:S_X + 2 * b + r + 1])
                    step(ins) if r == 0 else ins.then_inc(squares, 1)
                act.wait_ge(squares, q.next("squares"))

            rstd = [stat[:, S_XR + r:S_XR + r + 1] for r in range(R)]

            act.wait_ge(small_in, 16 * SMALL_LOADS)
            act.wait_ge(x_in, 16)
            square_x(0)
            square_x(1)
            act.wait_ge(turned, 1)
            act.activation(small[:, B_DF:B_DF + 32], small[:, B_DF:B_DF + 32], ACT.Exp).then_inc(act_done, 1)
            act.wait_ge(act_job, q.next("act_job"))
            act.activation(lam[:, :], lam[:, :], ACT.Exp).then_inc(act_done, 1)
            act.wait_ge(act_job, q.next("act_job"))
            act.activation(rope[:, :, :, :], rope[:, :, :, :], ACT.Sin).then_inc(act_done, 1)
            q.next("turn", 2)
            for g in range(4):
                take_model((2 * g, 2 * g + 1), 0)
            for _ in range(AHEAD):
                split_hi()

            per = dict(slab=len(KTS1), used=len(KTS1), blk=BLOCKS1, turn=TURNS1,
                       decay=RH, heads=2, soft=DH, rstd=5, squares=7,
                       **{f"in{s}": 32 * len(KTS1) // RING for s in range(RING)})
            per1 = dict(per, step=STEPS_ACT1)
            loop4 = dict(slab=4, used=4, blk=2, **{f"in{s}": 32 for s in range(RING)})
            for l in q.rounds(DEPTH, per1):
                ahead = iter(KTS1[AHEAD:] + KTS1[:AHEAD])

                def splits(n):
                    for _ in range(n):
                        split_hi(next(ahead))

                splits(2)
                for _i in q.rounds(3, loop4):
                    for _ in range(2):
                        used(2)
                        block_of()
                        split_hi()
                        split_hi()
                for _ in range(12):
                    next(ahead)
                used(2)
                block_of()
                q.next("rstd")
                read_out(q.now("blk"))
                act.activation(sq1[:, :, :], proj1[:, :, DQ:DQ + D], ACT.Square).then_inc(squares, 1)
                q.next("squares", 3)
                act.activation(proj1[:, :, RG:RG + RETW], proj1[:, :, RG:RG + RETW], ACT.Silu).then_inc(act_done, 1)
                for h in range(RH):
                    act.wait_ge(decay_arg, q.next("decay"))
                    act.activation(decay[:, h % 2, :], decay[:, h % 2, :], ACT.Exp).then_inc(decay_ready, 1)
                q.next("turn", 8)
                act.wait_ge(heads_out, q.next("heads"))
                o = block_of()
                for r in range(R):
                    ins = act.activation(sq1[:, r, 0:NB], o[r][:, :], ACT.Square)
                ins.then_inc(squares, 1)
                for h in range(DH):
                    act.wait_ge(soft_ready, q.next("soft"))
                    for m in range(2):
                        for r in range(R):
                            n = 4 * (h % 2) + 2 * m + r
                            ins = act.activation(soft1[:, h % 2, m, r * SEQ:(r + 1) * SEQ],
                                                 soft1[:, h % 2, m, r * SEQ:(r + 1) * SEQ], ACT.Exp,
                                                 scale=HD ** -0.5, bias=stat[:, S_NM + n:S_NM + n + 1],
                                                 accum_out=stat[:, S_RS + n:S_RS + n + 1])
                    ins.then_inc(probs, 1)
                q.next("turn", 4)
                act.wait_ge(heads_out, q.next("heads"))
                o = block_of()
                for r in range(R):
                    ins = act.activation(sq1[:, r, NB:D], o[r][:, :], ACT.Square)
                ins.then_inc(squares, 1)
                for g in range(4):
                    take_hi(hT_hi[:, 2 * g:2 * g + 2, :])
                for b in range(2):
                    splits(2)
                    used(2)
                    block_of()
                    read_out(q.now("blk"))
                    square_x(b)
                for g in range(4):
                    take_model((2 * g, 2 * g + 1), l * 16 + 8)
                def gate(first=False):
                    used(2)
                    a = block_of()
                    for r in range(R):
                        ins = act.activation(gate1[:, r, :], a[r][:, 0:HALF], ACT.Silu, scale=rstd[r])
                    ins.then_inc(act_done, 1)

                splits(2)
                act.wait_ge(rstd_ready, q.next("rstd", 4))
                for i in q.rounds(5, dict(loop4, turn=2)):
                    for j in range(2):
                        gate()
                        split_hi()
                        split_hi()
                        take_hi(hid1T_hi[:, bass.ds(i * 4 + 2 * j, 2), :])
                for _ in range(20):
                    next(ahead)
                gate()
                take_hi(hid1T_hi[:, 20:22, :])
                splits(6)
                splits(2)
                used(6)
                block_of()
                read_out(q.now("blk"))
                square_x(0)
                for g in range(2):
                    take_model((2 * g, 2 * g + 1), l * 16 + 16)
                splits(4)
                used(6)
                block_of()
                read_out(q.now("blk"))
                square_x(1)
                take_model((4, 5), l * 16 + 16)
                take_model((6, 7), l * 16 + 16, skip=1)

            per2 = dict(slab=len(KTS2), used=len(KTS2), blk=BLOCKS2, turn=TURNS2, soft=12, act_job=1,
                        rstd=4, squares=5, conv=1, step=STEPS_ACT2,
                        **{f"in{s}": 32 * len(KTS2) // RING for s in range(RING)})
            for l in q.rounds(DEPTH, per2):
                ahead = iter(KTS2[AHEAD:] + KTS2[:AHEAD])

                def splits(n):
                    for _ in range(n):
                        split_hi(next(ahead))

                splits(10)
                used(10)
                for _ in range(5):
                    block_of()
                read_out(q.now("blk"))
                n = 0
                for at, width in ((QL, 256), (KL, P)):
                    for r in range(R):
                        ins = act.activation(junk[:, 0:width], proj2[:, r, at:at + width], ACT.Square,
                                             accum_out=stat[:, S_L + n:S_L + n + 1])
                        n += 1
                        step(ins) if n < 4 else ins.then_inc(squares, 1)
                q.next("squares")
                act.activation(proj2[:, :, DGATE:DGATE + 256], proj2[:, :, DGATE:DGATE + 256],
                               ACT.Sigmoid).then_inc(act_done, 1)
                q.next("turn", 2)
                b = next_turn()
                for c in range(2):
                    ins = act.activation(lat_hi[:, c, :], b[:, c * SEQ:(c + 1) * SEQ], ACT.Copy,
                                         scale=ccols[:, bass.ds(l * 65 + 62 + c, 1)])
                ins.then_inc(turn_hi, 1)
                b = next_turn()
                act.activation(lat_hi[:, 2, :], b[:, 0:SEQ], ACT.Copy,
                               scale=ccols[:, bass.ds(l * 65 + 64, 1)]).then_inc(turn_hi, 1)
                splits(2)
                used(2)
                block_of()
                block_of()
                act.wait_ge(act_job, q.next("act_job"))
                step(act.activation(stat[:, S_A:S_A + 8], stat[:, S_A:S_A + 8], ACT.Exp))
                act.activation(stat[:, S_A:S_A + 8], stat[:, S_A:S_A + 8], ACT.Ln, bias=1.0).then_inc(act_done, 1)
                for h in range(12):
                    act.wait_ge(soft_ready, q.next("soft"))
                    for r, (a, z) in enumerate(((0, P), (P, 3 * P))):
                        n = 2 * (h % 2) + r
                        ins = act.activation(soft2[:, h % 2, a:z], soft2[:, h % 2, a:z], ACT.Exp,
                                             bias=stat[:, S_NM2 + n:S_NM2 + n + 1],
                                             accum_out=stat[:, S_RS2 + 12 * r + h:S_RS2 + 12 * r + h + 1])
                    ins.then_inc(probs, 1)
                q.next("turn", 1 + 1 + 10 + 12 + 1)
                block_of()
                block_of()
                read_out(q.now("blk"))
                act.dma_start(bgate[:, :, :], bass.AP(t["b_gate_2"].tensor, l * (NBR * D), [[0, P], [1, NBR * D]])
                              ).then_inc(bgate_in, 16)
                act.wait_ge(conv_in, q.next("conv"))
                act.activation(branches[:, :, 3 * BW:4 * BW], conv_y[:, :, :], ACT.Silu).then_inc(conv_out, 1)
                for g in range(4):
                    take_hi(obT_hi[:, 2 * g:2 * g + 2, :])
                for b in range(2):
                    for n in range(NBR):
                        splits(2)
                        used(2)
                        block_of()
                        read_out(q.now("blk"))
                        act.activation(gate2[:, :, :], term2[:, :, :], ACT.Sigmoid).then_inc(act_done, 1)
                        splits(1)
                        used(1)
                        block_of()
                for g in range(4):
                    take_hi(hT_hi[:, 2 * g:2 * g + 2, :])
                for b in range(2):
                    splits(2)
                    used(2)
                    block_of()
                    read_out(q.now("blk"))
                    square_x(b)
                for g in range(4):
                    take_model((2 * g, 2 * g + 1), l * 16 + 40)
                def rectify():
                    used(2)
                    a = block_of()
                    for r in range(R):
                        ins = act.activation(relu[r][:, :], a[r][:, :], ACT.Relu, scale=rstd[r])
                    ins.then_inc(act_done, 1)

                splits(2)
                act.wait_ge(rstd_ready, q.next("rstd", 4))
                for i in q.rounds(3, dict(loop4, turn=4)):
                    for j in range(2):
                        rectify()
                        split_hi()
                        split_hi()
                        for g in range(2):
                            take_hi(hid2T_hi[:, bass.ds(i * 8 + 4 * j + 2 * g, 2), :])
                for _ in range(12):
                    next(ahead)
                rectify()
                splits(2)
                for g in range(2):
                    take_hi(hid2T_hi[:, 24 + 2 * g:26 + 2 * g, :])
                rectify()
                for g in range(2):
                    take_hi(hid2T_hi[:, 28 + 2 * g:30 + 2 * g, :])
                splits(8)
                splits(2)
                used(8)
                block_of()
                read_out(q.now("blk"))
                square_x(0)
                for g in range(2):
                    take_model((2 * g, 2 * g + 1), l * 16 + 48)
                splits(6)
                used(8)
                block_of()
                read_out(q.now("blk"))
                square_x(1)
                take_model((4, 5), l * 16 + 48)
                take_model((6, 7), l * 16 + 48, skip=1)
                q.next("blk")

        @block.vector
        def _(dve):
            q = Place(dve)
            dve.sem_inc(lo_ready, RING)
            dve.sem_inc(acc_free, 2)
            dve.sem_inc(turn_free, 2)
            dve.sem_inc(scores_out, 2)

            def step(ins):
                ins.then_inc(dve_step, 1)
                dve.wait_ge(dve_step, q.next("step"))

            def split_lo(kts=4):
                s = q.index("slab") % RING
                dve.wait_ge(hi_ready, q.next("slab"))
                dve.tensor_tensor(w_lo[:, s, 0:kts, :], w_raw[:, s, 0:kts, :],
                                  w_hi[:, s, 0:kts, :].bitcast(F32), ALU.subtract).then_inc(lo_ready, 1)

            def used(n):
                dve.wait_ge(slab_used, q.next("used", n) + RING)

            def block_of():
                q.next("blk")
                return acc[(q.index("blk") - 1) % 2]

            def next_turn(skip=0):
                dve.wait_ge(turned, q.next("turn") + skip)
                b = turn[(q.index("turn") - 1) % 2]
                q.next("turn", skip)
                return b

            def next_hi():
                q.next("turn")
                dve.wait_ge(turn_hi, q.next("turn_hi"))
                return turn[(q.index("turn") - 1) % 2]

            def take_lo(dst, hi):
                b = next_hi()
                n = dst.shape[1] * dst.shape[2]
                dve.tensor_tensor(dst, b[:, 0:n].rearrange("p (c n) -> p c n", n=SEQ), hi.bitcast(F32),
                                  ALU.subtract).then_inc(turn_free, 1)

            def lo_with_gain(lo, hi, src, gain):
                return dve.scalar_tensor_tensor(lo, src, gain, hi.bitcast(F32), ALU.mult, ALU.subtract)

            def take_model(tiles, gain, skip=0):
                b = next_hi()
                for j, kt in enumerate(tiles):
                    ins = lo_with_gain(hT_lo[:, kt, :], hT_hi[:, kt, :], b[:, j * SEQ:(j + 1) * SEQ],
                                       gcols[:, bass.ds(gain + kt, 1)])
                ins.then_inc(turn_free, 1 + skip)
                q.next("turn", skip)

            def add_x(b):
                a = block_of()
                for r in range(R):
                    ins = dve.tensor_tensor(x[:, r, b * NB:(b + 1) * NB], x[:, r, b * NB:(b + 1) * NB],
                                            a[r][:, :], ALU.add)
                ins.then_inc(acc_free, 1)

            def mean(dst, src, n):
                dve.tensor_scalar(dst, src, 1.0 / n, EPS, ALU.mult, ALU.add).then_inc(mean_ready, 1)

            def mean_x():
                dve.wait_ge(squares, q.next("squares", 2))
                step(dve.tensor_tensor(stat[:, S_XM:S_XM + 2], stat[:, S_X:S_X + 2], stat[:, S_X + 2:S_X + 4], ALU.add))
                mean(stat[:, S_XM:S_XM + 2], stat[:, S_XM:S_XM + 2], D)

            def root():
                dve.wait_ge(rstd_ready, q.next("rstd"))

            def per_head(at, r, heads, width):
                return stat[:, at + r * heads:at + (r + 1) * heads].unsqueeze(2).to_broadcast([P, heads, width])

            rstd = [stat[:, S_XR + r:S_XR + r + 1] for r in range(R)]

            dve.wait_ge(consts_in, 16)
            dve.wait_ge(small_in, 16 * SMALL_LOADS)
            for n in range(2):
                step(dve.tensor_tensor(lprod[:, n, :], lrows[:, 2 * n, :], lrows[:, 2 * n + 1, :], ALU.mult))
            dve.tensor_reduce(lam[:, :], lprod[:, :, :].rearrange("p n (l d) -> p (n l) d", l=DEPTH), AX.X,
                              ALU.add).then_inc(act_job, 1)
            posf = ropet[:, 5, :, 0]
            step(dve.tensor_copy(posf, pos_i[:, :]))
            for r in range(R):
                step(dve.tensor_scalar(ropet[:, 0, r, :], cst[:, C_INV:C_INV + 16], ropet[:, 5, r, 0:1], None, ALU.mult))
            ang, turns, red = ropet[:, 0], ropet[:, 1], ropet[:, 2]
            step(dve.tensor_scalar(turns, ang, 1.0 / (2 * np.pi), 12582912.0, ALU.mult, ALU.add))
            step(dve.tensor_scalar(turns, turns, 12582912.0, None, ALU.subtract))
            parts = (6.28125, 0.0019350051879882812, 3.0199159819e-07)
            step(dve.scalar_tensor_tensor(red, turns, -parts[0], ang, ALU.mult, ALU.add))
            step(dve.scalar_tensor_tensor(red, turns, -parts[1], red, ALU.mult, ALU.add))
            step(dve.scalar_tensor_tensor(red, turns, -parts[2], red, ALU.mult, ALU.add))
            step(dve.tensor_scalar(rope[:, 1], red, 3.1415925, -3.1415925, ALU.min, ALU.max))
            step(dve.tensor_scalar(ropet[:, 3], rope[:, 1], -1.0, None, ALU.mult))
            step(dve.tensor_tensor(ropet[:, 3], ropet[:, 3], rope[:, 1], ALU.max))
            dve.tensor_scalar(rope[:, 0], ropet[:, 3], -1.0, float(np.pi / 2), ALU.mult, ALU.add).then_inc(act_job, 1)
            b = next_turn()
            dve.tensor_copy(gcols[:, :], b[:, 0:72]).then_inc(turn_free, 1)
            b = next_turn()
            dve.tensor_copy(ccols[:, :], b[:, 0:DEPTH * 65]).then_inc(turn_free, 1)
            mean_x()
            dve.wait_ge(act_done, q.next("act_done", 3))
            dve.tensor_scalar(small[:, B_DF:B_DF + 32], small[:, B_DF:B_DF + 32], -1.0, None,
                              ALU.mult).then_inc(pool_job, 1)
            step(dve.tensor_tensor(lam[:, 0:DEPTH], lam[:, 0:DEPTH], lam[:, DEPTH:2 * DEPTH], ALU.subtract))
            step(dve.tensor_tensor(lam[:, 0:DEPTH], lam[:, 0:DEPTH], cst[:, C_LI:C_LI + DEPTH], ALU.add))
            step(dve.tensor_scalar(lam[:, 0:DEPTH], lam[:, 0:DEPTH], -1.0, None, ALU.mult))
            for g in range(4):
                take_model((2 * g, 2 * g + 1), 0)
            for _ in range(AHEAD):
                split_lo()

            loop4 = dict(slab=4, used=4, blk=2)
            for l in q.rounds(DEPTH, dict(slab=len(KTS1), used=len(KTS1), blk=BLOCKS1, turn=TURNS1,
                                          turn_hi=TURNS1 - 13, squares=7, rstd=5, act_done=12, scores=16,
                                          decay=RH, probs=DH, step=STEPS_DVE1)):
                ahead = iter(KTS1[AHEAD:] + KTS1[:AHEAD])

                def splits(n):
                    for _ in range(n):
                        split_lo(next(ahead))

                def take_proj(at):
                    used(2)
                    a = block_of()
                    for r in range(R):
                        ins = dve.tensor_scalar(proj1[:, r, bass.ds(at, NB)], a[r][:, :], rstd[r], None, ALU.mult)
                    ins.then_inc(acc_free, 1)

                splits(2)
                root()
                hold(dve)
                for i in q.rounds(3, loop4):
                    for j in range(2):
                        take_proj(i * (2 * NB) + j * NB)
                        split_lo()
                        split_lo()
                for _ in range(12):
                    next(ahead)
                take_proj(6 * NB)
                dve.wait_ge(squares, q.next("squares"))
                step(dve.tensor_reduce(stat[:, S_Q:S_Q + 32], sq1[:, :, :].rearrange("p r (h d) -> p (r h) d", d=HD),
                                       AX.X, ALU.add))
                mean(stat[:, S_Q:S_Q + 32], stat[:, S_Q:S_Q + 32], HD)
                for j in range(4):
                    b = next_turn()
                    dve.tensor_copy(qkT1[:, j, :], b[:, :]).then_inc(turn_free, 1)
                root()
                for r in range(R):
                    v = proj1[:, r, DQ:DQ + D].rearrange("p (h d) -> p h d", d=HD)
                    ins = dve.tensor_tensor(v, v, per_head(S_QR, r, 16, HD), ALU.mult)
                ins.then_inc(pool_job, 1)
                for h in range(RH):
                    dve.wait_ge(scores, q.next("scores"))
                    dve.wait_ge(decay_ready, q.next("decay"))
                    dve.scalar_tensor_tensor(ret_p[:, h % 2, :], score[h % 2][:, :], HD ** -0.5, decay[:, h % 2, :],
                                             ALU.mult, ALU.mult).then_inc(scores_out, 1)
                    if h > 3:
                        b = next_turn()
                        dve.tensor_copy(qkT1[:, h, :], b[:, :]).then_inc(turn_free, 1)
                dve.wait_ge(act_done, q.next("act_done"))
                o = block_of()
                dve.wait_ge(squares, q.next("squares"))
                step(dve.tensor_reduce(stat[:, S_O:S_O + 16], sq1[:, :, 0:NB].rearrange("p r (h d) -> p r h d", d=HD),
                                       AX.X, ALU.add))
                mean(stat[:, S_O:S_O + 16], stat[:, S_O:S_O + 16], HD)
                root()
                for r in range(R):
                    ins = dve.tensor_tensor(mixed1[:, r, 0:NB].rearrange("p (h d) -> p h d", d=HD),
                                            o[r][:, :].rearrange("p (h d) -> p h d", d=HD),
                                            per_head(S_OR, r, RH, HD), ALU.mult)
                ins.then_inc(acc_free, 1)
                def soften(h):
                    for m in range(2):
                        dve.wait_ge(scores, q.next("scores"))
                        slope = 2.0 ** (-8.0 * (h + 1) / DH)
                        dve.scalar_tensor_tensor(soft1[:, h % 2, m, :], cst[:, C_DA:C_DA + R * SEQ],
                                                 -slope * HD ** 0.5, score[m][:, :], ALU.mult, ALU.add
                                                 ).then_inc(scores_out, 1)
                    dve.wait_ge(scores_out, q.now("scores") + 2)
                    at = S_NM + 4 * (h % 2)
                    step(dve.tensor_reduce(stat[:, at:at + 4], soft1[:, h % 2].rearrange("p m (r k) -> p (m r) k", r=R),
                                           AX.X, ALU.max))
                    dve.tensor_scalar(stat[:, at:at + 4], stat[:, at:at + 4], -HD ** -0.5, None,
                                      ALU.mult).then_inc(soft_ready, 1)

                def combine(h):
                    dve.wait_ge(probs, q.next("probs"))
                    at, rs = S_RC + 4 * (h % 2), S_RS + 4 * (h % 2)
                    step(dve.reciprocal(stat[:, at:at + 4], stat[:, rs:rs + 4]))
                    step(dve.tensor_scalar(stat[:, at + 2:at + 4], stat[:, at + 2:at + 4], lam[:, bass.ds(l, 1)], None, ALU.mult))
                    for r in range(R):
                        step(dve.tensor_scalar(comb1[:, r, :], soft1[:, h % 2, 1, r * SEQ:(r + 1) * SEQ],
                                               stat[:, at + 2 + r:at + 3 + r], None, ALU.mult))
                    for r in range(R):
                        ins = dve.scalar_tensor_tensor(comb1[:, r, :], soft1[:, h % 2, 0, r * SEQ:(r + 1) * SEQ],
                                                       stat[:, at + r:at + r + 1], comb1[:, r, :], ALU.mult, ALU.add)
                    ins.then_inc(dve_ready, 1)
                    b = next_turn()
                    dve.tensor_copy(combT1[:, :, :].rearrange("p r k -> p (r k)"), b[:, :]).then_inc(turn_free, 1)

                soften(0)
                for h in range(DH):
                    if h + 1 < DH:
                        soften(h + 1)
                    combine(h)
                o = block_of()
                dve.wait_ge(squares, q.next("squares"))
                step(dve.tensor_reduce(stat[:, S_P:S_P + 8], sq1[:, :, NB:D].rearrange("p r (h d) -> p r h d", d=DVD),
                                       AX.X, ALU.add))
                mean(stat[:, S_P:S_P + 8], stat[:, S_P:S_P + 8], DVD)
                root()
                step(dve.tensor_scalar(stat[:, S_PR:S_PR + 8], stat[:, S_PR:S_PR + 8],
                                       cst[:, bass.ds(l + C_OML, 1)], None, ALU.mult))
                for r in range(R):
                    ins = dve.tensor_tensor(mixed1[:, r, NB:D].rearrange("p (h d) -> p h d", d=DVD),
                                            o[r][:, :].rearrange("p (h d) -> p h d", d=DVD),
                                            per_head(S_PR, r, DH, DVD), ALU.mult)
                ins.then_inc(acc_free, 1)
                for g in range(4):
                    take_lo(hT_lo[:, 2 * g:2 * g + 2, :], hT_hi[:, 2 * g:2 * g + 2, :])
                for b in range(2):
                    splits(2)
                    used(2)
                    add_x(b)
                mean_x()
                for g in range(4):
                    take_model((2 * g, 2 * g + 1), l * 16 + 8)
                def up():
                    used(2)
                    a = block_of()
                    dve.wait_ge(act_done, q.next("act_done"))
                    for r in range(R):
                        ins = dve.scalar_tensor_tensor(hid1[:, r, :], a[r][:, HALF:NB], rstd[r], gate1[:, r, :],
                                                       ALU.mult, ALU.mult)
                    ins.then_inc(acc_free, 1)

                splits(2)
                root()
                hold(dve)
                for i in q.rounds(5, dict(loop4, turn=2, turn_hi=2, act_done=2)):
                    for j in range(2):
                        up()
                        split_lo()
                        split_lo()
                        take_lo(hid1T_lo[:, bass.ds(i * 4 + 2 * j, 2), :], hid1T_hi[:, bass.ds(i * 4 + 2 * j, 2), :])
                for _ in range(20):
                    next(ahead)
                up()
                take_lo(hid1T_lo[:, 20:22, :], hid1T_hi[:, 20:22, :])
                splits(8)
                used(6)
                add_x(0)
                for g in range(2):
                    take_model((2 * g, 2 * g + 1), l * 16 + 16)
                splits(4)
                used(6)
                add_x(1)
                mean_x()
                take_model((4, 5), l * 16 + 16)
                take_model((6, 7), l * 16 + 16, skip=1)

            q.next("heads", DEPTH * 2)
            for l in q.rounds(DEPTH, dict(slab=len(KTS2), used=len(KTS2), blk=BLOCKS2, turn=TURNS2,
                                          turn_hi=2 + 4 + 4 + 4 + 16 + 4, squares=5, rstd=4, act_done=18, scores=12,
                                          heads=2, layer_in=64, bgate=16, step=STEPS_DVE2)):
                ahead = iter(KTS2[AHEAD:] + KTS2[:AHEAD])

                def splits(n):
                    for _ in range(n):
                        split_lo(next(ahead))

                def take_proj(b):
                    used(2)
                    a = block_of()
                    n = min(NB, PROJ2 - b * NB)
                    for r in range(R):
                        ins = dve.tensor_scalar(proj2[:, r, b * NB:b * NB + n], a[r][:, 0:n], rstd[r], None, ALU.mult)
                    ins.then_inc(acc_free, 1)

                splits(2)
                root()
                for b in range(4):
                    take_proj(b)
                    splits(2)
                take_proj(4)
                dve.wait_ge(layer_in, q.next("layer_in", 64))
                for g in range(2):
                    b = next_turn()
                    v = b[:, :].rearrange("p (h k) -> p h k", h=2)
                    dve.tensor_tensor(abias[:, 2 * g:2 * g + 2, 0:P], v[:, :, P:2 * P],
                                      cst[:, C_MCH:C_MCH + P].unsqueeze(1).to_broadcast([P, 2, P]), ALU.add)
                    dve.tensor_tensor(abias[:, 2 * g:2 * g + 2, P:3 * P], v,
                                      cst[:, C_MCH + P:C_MCH + 3 * P].unsqueeze(1).to_broadcast([P, 2, SEQ]),
                                      ALU.add).then_inc(turn_free, 1)
                dve.wait_ge(squares, q.next("squares"))
                step(dve.tensor_scalar(stat[:, S_L:S_L + 2], stat[:, S_L:S_L + 2], 1.0 / 256, EPS, ALU.mult, ALU.add))
                mean(stat[:, S_L + 2:S_L + 4], stat[:, S_L + 2:S_L + 4], P)
                b = next_hi()
                for c in range(2):
                    ins = lo_with_gain(lat_lo[:, c, :], lat_hi[:, c, :], b[:, c * SEQ:(c + 1) * SEQ],
                                       ccols[:, bass.ds(l * 65 + 62 + c, 1)])
                ins.then_inc(turn_free, 1)
                b = next_hi()
                lo_with_gain(lat_lo[:, 2, :], lat_hi[:, 2, :], b[:, 0:SEQ],
                             ccols[:, bass.ds(l * 65 + 64, 1)]).then_inc(turn_free, 1)
                splits(2)
                dve.wait_ge(act_done, q.next("act_done"))
                dve.tensor_tensor(proj2[:, :, DVAL:DVAL + 256], proj2[:, :, DVAL:DVAL + 256],
                                  proj2[:, :, DGATE:DGATE + 256], ALU.mult).then_inc(dve_ready, 1)
                z, m, a8, lf = (stat[:, s:s + 8] for s in (S_Z, S_M, S_A, S_LF))
                for r in range(R):
                    step(dve.tensor_tensor(z[:, 4 * r:4 * r + 4], proj2[:, r, CF:CF + 4],
                                           small[:, bass.ds(l * 4 + B_FB, 4)], ALU.add))
                step(dve.tensor_scalar(m, z, -1.0, None, ALU.mult))
                dve.tensor_tensor(a8, m, z, ALU.min).then_inc(act_job, 1)
                step(dve.tensor_scalar(z, z, 0.0, None, ALU.min))
                root()
                used(1)
                a = block_of()
                for r in range(R):
                    ins = dve.tensor_scalar(qB[:, r].rearrange("p h d -> p (h d)"), a[r][:, 0:384],
                                            stat[:, S_LR + r:S_LR + r + 1], None, ALU.mult)
                ins.then_inc(acc_free, 1)
                used(1)
                a = block_of()
                for r in range(R):
                    ins = dve.tensor_scalar(kvB[:, r, :], a[r][:, :], stat[:, S_LR + 2 + r:S_LR + 3 + r], None, ALU.mult)
                ins.then_inc(acc_free, 1)
                dve.wait_ge(act_done, q.next("act_done"))
                dve.tensor_tensor(lf, z, a8, ALU.subtract).then_inc(dve_ready, 1)
                step(dve.memset(uT[:, :, 0:TAPS - 1], 0.0))
                b = next_turn()
                step(dve.tensor_copy(uT[:, :, TAPS - 1:], b[:, :].rearrange("p (c n) -> p c n", c=2)))
                dve.sem_inc(turn_free, 1)
                b = next_turn()
                sums = b[:, 0:8].rearrange("p (r h) -> p r h", r=R)
                dve.tensor_scalar(cqa[:, :, :, HD], sums, HD ** 0.5, None, ALU.mult)
                dve.tensor_scalar(cka[:, :, :, HD + 1], sums, -HD ** 0.5, None, ALU.mult).then_inc(turn_free, 1)
                one = cst[:, C_ONE:C_ONE + 8].rearrange("p (r h) -> p r h", r=R)
                dve.tensor_copy(cka[:, :, :, HD], one)
                dve.tensor_copy(cqa[:, :, :, HD + 1], one).then_inc(dve_ready, 1)

                def take_group(g):
                    b = next_turn()
                    n = P if g < 2 else CAD if g < 6 else BQD
                    dve.tensor_copy(qkT2[0:n, g % 3, :], b[0:n, :]).then_inc(turn_free, 1)

                def take_probs(h):
                    b = next_turn()
                    dve.tensor_copy(softT2[:, h % 2, :], b[:, 0:3 * P]).then_inc(turn_free, 1)

                take_group(0)
                take_group(1)
                for h in range(13):
                    if h < 12:
                        dve.wait_ge(scores, q.next("scores"))
                        bias = abias[:, h, :] if h < 4 else cst[:, C_MCA:C_MCA + 384] if h < 8 else cst[:, C_MCH:C_MCH + 384]
                        dve.scalar_tensor_tensor(soft2[:, h % 2, :], score[h % 2][:, 0:384],
                                                 HD ** -0.5 if h < 8 else BQD ** -0.5, bias, ALU.mult, ALU.add
                                                 ).then_inc(scores_out, 1)
                        dve.wait_ge(scores_out, q.now("scores") + 2)
                        n = S_NM2 + 2 * (h % 2)
                        dve.tensor_reduce(stat[:, n:n + 1], soft2[:, h % 2, 0:P], AX.X, ALU.max, negate=True)
                        dve.tensor_reduce(stat[:, n + 1:n + 2], soft2[:, h % 2, P:3 * P], AX.X, ALU.max,
                                          negate=True).then_inc(soft_ready, 1)
                        if 2 <= h < 10:
                            take_group(h)
                    if h >= 1:
                        take_probs(h - 1)
                for k in range(TAPS):
                    for c in range(2):
                        w = ccols[:, bass.ds(l * 65 + 2 * k + c, 1)]
                        src = uT[:, c, k:k + SEQ]
                        if k == 0:
                            ins = dve.tensor_scalar(yT[:, c, :], src, w, None, ALU.mult)
                        else:
                            dve.wait_ge(dve_step, q.now("step") - 1)
                            ins = dve.scalar_tensor_tensor(yT[:, c, :], src, w, yT[:, c, :], ALU.mult, ALU.add)
                        if k == TAPS - 1 and c == 1:
                            ins.then_inc(dve_ready, 1)
                        else:
                            ins.then_inc(dve_step, 1)
                            q.next("step")
                dve.wait_ge(heads_out, q.next("heads"))
                dve.wait_ge(heads_out, q.next("heads"))
                step(dve.reciprocal(stat[:, S_RC2:S_RC2 + 24], stat[:, S_RS2:S_RS2 + 24]))
                for part in range(2):
                    o = block_of()
                    for n, dst in ((0, 0), (1, 2)) if part == 0 else ((2, 1),):
                        for r in range(R):
                            at = S_RC2 + 12 * r + 4 * n
                            ins = dve.tensor_tensor(
                                branches[:, r, dst * BW:(dst + 1) * BW].rearrange("p (h d) -> p h d", d=HD),
                                o[r][:, (n % 2) * 256:(n % 2) * 256 + 256].rearrange("p (h d) -> p h d", d=HD),
                                stat[:, at:at + 4].unsqueeze(2).to_broadcast([P, 4, HD]), ALU.mult)
                    ins.then_inc(acc_free, 1)
                b = next_turn()
                step(dve.tensor_tensor(conv_y[:, :, :], b[:, :].rearrange("p (r n) -> p r n", r=R),
                                       convrow[:, 0, :].unsqueeze(1).to_broadcast([P, R, 256]), ALU.add))
                dve.sem_inc(turn_free, 1)
                for r in range(R):
                    ins = dve.bn_stats(stat[:, S_BN + 6 * r:S_BN + 6 * r + 6], conv_y[:, r, :])
                step(ins)
                hold(dve)
                for r in range(R):
                    ins = dve.bn_aggr(stat[:, S_MV + 2 * r:S_MV + 2 * r + 2], stat[:, S_BN + 6 * r:S_BN + 6 * r + 6])
                step(ins)
                dve.tensor_scalar(stat[:, S_VR:S_VR + 2], stat[:, S_MV:S_MV + 4].rearrange("p (r n) -> p r n", n=2)[:, :, 1],
                                  EPS, None, ALU.add).then_inc(mean_ready, 1)
                root()
                for r in range(R):
                    step(dve.tensor_scalar(conv_y[:, r, :], conv_y[:, r, :], stat[:, S_MV + 2 * r:S_MV + 2 * r + 1],
                                           stat[:, S_VR + r:S_VR + r + 1], ALU.subtract, ALU.mult))
                step(dve.tensor_tensor(conv_y[:, :, :], conv_y[:, :, :],
                                       convrow[:, 1, :].unsqueeze(1).to_broadcast([P, R, 256]), ALU.mult))
                dve.tensor_tensor(conv_y[:, :, :], conv_y[:, :, :],
                                  convrow[:, 2, :].unsqueeze(1).to_broadcast([P, R, 256]), ALU.add).then_inc(conv_in, 1)
                for g in range(4):
                    take_lo(obT_lo[:, 2 * g:2 * g + 2, :], obT_hi[:, 2 * g:2 * g + 2, :])
                dve.wait_ge(bgate_in, q.next("bgate", 16))
                for b in range(2):
                    cols = slice(b * NB, (b + 1) * NB)
                    for n in range(NBR):
                        splits(2)
                        used(2)
                        a = block_of()
                        for r in range(R):
                            ins = dve.scalar_tensor_tensor(term2[:, r, :], a[r][:, :], rstd[r], bgate[:, n, cols],
                                                           ALU.mult, ALU.add)
                        ins.then_inc(acc_free, 1)
                        splits(1)
                        used(1)
                        a = block_of()
                        dve.wait_ge(act_done, q.next("act_done"))
                        for r in range(R):
                            dst = mix2[:, r, cols] if n == 0 else term2[:, r, :]
                            ins = dve.tensor_tensor(dst, gate2[:, r, :], a[r][:, :], ALU.mult)
                        ins.then_inc(acc_free, 1)
                        if n:
                            dve.wait_ge(acc_free, q.now("blk") + 2)
                            ins = dve.tensor_tensor(mix2[:, :, cols], mix2[:, :, cols], term2[:, :, :], ALU.add)
                            if b == 1 and n == NBR - 1:
                                ins.then_inc(dve_ready, 1)
                            else:
                                step(ins)
                for g in range(4):
                    take_lo(hT_lo[:, 2 * g:2 * g + 2, :], hT_hi[:, 2 * g:2 * g + 2, :])
                for b in range(2):
                    splits(2)
                    used(2)
                    add_x(b)
                mean_x()
                for g in range(4):
                    take_model((2 * g, 2 * g + 1), l * 16 + 40)
                def up():
                    used(2)
                    a = block_of()
                    dve.wait_ge(act_done, q.next("act_done"))
                    for r in range(R):
                        ins = dve.scalar_tensor_tensor(hid2[:, r, :], a[r][:, :], rstd[r], relu[r][:, :],
                                                       ALU.mult, ALU.mult)
                    ins.then_inc(acc_free, 1)

                splits(2)
                root()
                hold(dve)
                for i in q.rounds(3, dict(loop4, turn=4, turn_hi=4, act_done=2)):
                    for j in range(2):
                        up()
                        split_lo()
                        split_lo()
                        for g in range(2):
                            at = i * 8 + 4 * j + 2 * g
                            take_lo(hid2T_lo[:, bass.ds(at, 2), :], hid2T_hi[:, bass.ds(at, 2), :])
                for _ in range(12):
                    next(ahead)
                up()
                splits(2)
                for at in (24, 26):
                    take_lo(hid2T_lo[:, at:at + 2, :], hid2T_hi[:, at:at + 2, :])
                up()
                for at in (28, 30):
                    take_lo(hid2T_lo[:, at:at + 2, :], hid2T_hi[:, at:at + 2, :])
                splits(10)
                used(8)
                add_x(0)
                for g in range(2):
                    take_model((2 * g, 2 * g + 1), l * 16 + 48)
                splits(6)
                used(8)
                a = block_of()
                for r in range(R):
                    ins = dve.tensor_tensor(x[:, r, NB:D], x[:, r, NB:D], a[r][:, :], ALU.add)
                ins.then_inc(acc_free, 2)
                q.next("blk")
                mean_x()
                take_model((4, 5), l * 16 + 48)
                take_model((6, 7), l * 16 + 48, skip=1)
            root()
            dve.wait_ge(x_in, 32)
            for r in range(R):
                ins = dve.scalar_tensor_tensor(outrow[:, r, :], x[:, r, :], rstd[r], gfin[:, :], ALU.mult, ALU.mult)
            ins.then_inc(out_ready, 1)

        @block.gpsimd
        def _(pool):
            q = Place(pool)
            half = cst[:, C_NEG:C_NEG + 32]

            def root(dst, src, n):
                pool.wait_ge(mean_ready, q.next("mean"))
                pool.tensor_tensor(dst, src, half[:, 0:n], ALU.pow).then_inc(rstd_ready, 1)

            def root_x():
                root(stat[:, S_XR:S_XR + 2], stat[:, S_XM:S_XM + 2], 2)

            def step(ins):
                ins.then_inc(pool_step, 1)
                pool.wait_ge(pool_step, q.next("step"))

            pool.wait_ge(consts_in, 16)
            root_x()
            pool.wait_ge(pool_job, q.next("pool_job"))
            q.next("act_done", 3)
            for l in q.rounds(DEPTH, dict(mean=5, pool_job=1, act_done=12, scores=16, decay=RH, blk=BLOCKS1,
                                          step=STEPS_POOL1)):
                q.next("blk", 7)

                def exponent(h):
                    if h >= 2:
                        pool.wait_ge(scores_out, q.next("scores") + 2)
                    hold(pool)
                    pool.tensor_tensor(decay[:, h % 2, :], cst[:, C_DF:C_DF + 512],
                                       small[:, bass.ds(l * 8 + B_DF + h, 1)].to_broadcast([P, 512]), ALU.mult)
                    step(pool.tensor_tensor(pooltmp[:, :], cst[:, C_DB:C_DB + 512],
                                            small[:, bass.ds(l * 8 + B_DB + h, 1)].to_broadcast([P, 512]), ALU.mult))
                    pool.tensor_tensor(decay[:, h % 2, :], decay[:, h % 2, :], pooltmp[:, :],
                                       ALU.add).then_inc(decay_arg, 1)
                    pool.wait_ge(decay_arg, q.next("decay"))

                pool.wait_ge(acc_free, q.now("blk") + 2)
                exponent(0)
                exponent(1)
                root(stat[:, S_QR:S_QR + 32], stat[:, S_Q:S_Q + 32], 32)
                pool.wait_ge(pool_job, q.next("pool_job"))
                hold(pool)
                for r in range(R):
                    for at, g in ((DQ, B_QG), (DK, B_KG)):
                        v = proj1[:, r, at:at + 512].rearrange("p (h d) -> p h d", d=HD)
                        ins = pool.tensor_tensor(v, v, small[:, bass.ds(l * HD + g, HD)].unsqueeze(1)
                                                 .to_broadcast([P, 8, HD]), ALU.mult)
                ins.then_inc(pool_ready, 1)
                for h in range(2, RH):
                    exponent(h)
                q.next("scores", 2)
                pool.wait_ge(act_done, q.next("act_done"))
                hold(pool)
                for r in range(R):
                    v = proj1[:, r, RG:RG + RETW].rearrange("p (h d) -> p h d", d=HD)
                    ins = pool.tensor_tensor(v, v, small[:, bass.ds(l * HD + B_RG, HD)].unsqueeze(1)
                                             .to_broadcast([P, RH, HD]), ALU.mult)
                step(ins)
                root(stat[:, S_OR:S_OR + 16], stat[:, S_O:S_O + 16], 16)
                pool.wait_ge(acc_free, q.next("blk") + 2)
                pool.tensor_tensor(mixed1[:, :, 0:NB], mixed1[:, :, 0:NB], proj1[:, :, RG:RG + RETW],
                                   ALU.mult).then_inc(pool_ready, 1)
                root(stat[:, S_PR:S_PR + 8], stat[:, S_P:S_P + 8], 8)
                pool.wait_ge(acc_free, q.next("blk") + 2)
                hold(pool)
                for r in range(R):
                    v = mixed1[:, r, NB:D].rearrange("p (h d) -> p h d", d=DVD)
                    ins = pool.tensor_tensor(v, v, small[:, bass.ds(l * DVD + B_DG, DVD)].unsqueeze(1)
                                             .to_broadcast([P, DH, DVD]), ALU.mult)
                ins.then_inc(pool_ready, 1)
                root_x()
                root_x()
                q.next("act_done", 11)
                q.next("scores", 8)
                q.next("blk", BLOCKS1 - 9)
            for l in q.rounds(DEPTH, dict(mean=4, blk=BLOCKS2, step=STEPS_POOL2)):
                pool.wait_ge(acc_free, q.next("blk", 5) + 2)
                hold(pool)
                for r in range(R):
                    pool.tensor_copy(cqa[:, r, :, 0:HD], proj2[:, r, CQ:CQ + 256].rearrange("p (h d) -> p h d", d=HD))
                    ins = pool.tensor_copy(cka[:, r, :, 0:HD], proj2[:, r, CK:CK + 256].rearrange("p (h d) -> p h d", d=HD))
                ins.then_inc(pool_ready, 1)
                root(stat[:, S_LR:S_LR + 4], stat[:, S_L:S_L + 4], 4)
                def rotate(r, a, b, da, db, spread):
                    cos, sin = (rope[:, n, r, :] if not spread else
                                rope[:, n, r, :].unsqueeze(1).to_broadcast([P, 4, 16]) for n in range(2))
                    tmp = [ropetmp[:, n, 0:64].rearrange("p (h d) -> p h d", h=4) if spread else ropetmp[:, n, 0:16]
                           for n in range(4)]
                    for n, (u, v) in enumerate(((a, cos), (b, sin), (b, cos), (a, sin))):
                        step(pool.tensor_tensor(tmp[n], u, v, ALU.mult))
                    step(pool.tensor_tensor(da, tmp[0], tmp[1], ALU.subtract))
                    step(pool.tensor_tensor(db, tmp[2], tmp[3], ALU.add))

                for r in range(R):
                    a, b = proj2[:, r, KR:KR + 16], proj2[:, r, KR + 16:KR + 32]
                    rotate(r, a, b, a, b, False)
                pool.wait_ge(acc_free, q.next("blk", 2) + 2)
                for r in range(R):
                    a, b = qB[:, r, :, 64:80], qB[:, r, :, 80:96]
                    rotate(r, a, b, a, b, True)
                    hold(pool)
                    pool.tensor_copy(kB[:, r, :, 0:64], kvB[:, r, :].rearrange("p (h d) -> p h d", d=P)[:, :, 0:64])
                    ins = pool.tensor_copy(kB[:, r, :, 64:96], proj2[:, r, KR:KR + 32].unsqueeze(1)
                                           .to_broadcast([P, 4, 32]))
                ins.then_inc(pool_ready, 1)
                root(stat[:, S_VR:S_VR + 2], stat[:, S_VR:S_VR + 2], 2)
                root_x()
                root_x()
                q.next("blk", BLOCKS2 - 7)


_NAMES = [
    "x", "attn_norm_g", "w_in", "ret_decay_fwd", "ret_decay_bwd", "ret_norm_g", "dq_norm_g", "dk_norm_g",
    "lambda_q1", "lambda_k1", "lambda_q2", "lambda_k2", "diff_norm_g", "w_out", "ffn_norm_g", "w_gate", "w_up",
    "w_down", "positions_2", "g_mix_2", "w_in_2", "w_gate_2", "b_gate_2", "g_q_lat_2", "w_uq_2",
    "g_kv_lat_2", "w_ukv_2", "b_forget_2", "w_dw_2", "b_dw_2", "g_conv_ln_2", "b_conv_ln_2", "w_branch_2",
    "w_o_2", "g_ffn_2", "w_up_2", "w_down_2", "g_final_2"]


def kernel(**inputs):
    import concourse.bacc as bacc
    from concourse.bass_utils import run_bass_kernel_spmd

    nc = bacc.Bacc("TRN2", target_bir_lowering=False, num_devices=1)
    arrays = {name: np.ascontiguousarray(inputs[name]) for name in _NAMES}
    arrays["consts"] = shape_constants()
    falling = 2 * 128 - np.maximum(np.arange(384) - 127, 0)
    arrays["rel_ext"] = np.ascontiguousarray(inputs["rel_bias_2"][:, :, falling])
    t = {name: nc.dram_tensor(f"in_{name}", a.shape, mybir.dt.from_np(a.dtype), kind="ExternalInput").ap()
         for name, a in arrays.items()}
    out = nc.dram_tensor("out", (1, SEQ, D), F32, kind="ExternalOutput").ap()
    build(nc, t, out)
    r = run_bass_kernel_spmd(nc, [{f"in_{name}": a for name, a in arrays.items()}], core_ids=[0])
    return r.results[0]["out"]
```

```python
from contextlib import ExitStack

import numpy as np
import concourse.bass as bass
from concourse import mybir

F32 = mybir.dt.float32
F32R = mybir.dt.float32r
I32 = mybir.dt.int32
ALU = mybir.AluOpType
ACT = mybir.ActivationFunctionType
AX = mybir.AxisListType

P = 128
SEQ = 256
R = SEQ // P
D = 1024
KT = D // P
DEPTH = 2
EPS = 1e-6
NB = 512
RING = 4
AHEAD = 3

RETW, HD = 512, 64
RH = RETW // HD
DH, DVD = 4, 128
PROJ1 = 4 * RETW + 3 * 512
RQ, RK, RV, RG, DQ, DK, DV = (i * 512 for i in range(7))
FF1 = 2816
HALF = NB // 2
PROJ2 = 2468
AQ, AK, AV, QL, KL, KR, CQ, CK, CV, CF, DVAL, DGATE = (
    0, 256, 512, 768, 1024, 1152, 1184, 1440, 1696, 1952, 1956, 2212)
NBR, BW = 4, 256
FF2 = 4096
TAPS = 31
BQD = 96
CAD = 66
MASKED = -1e30

KTS1 = [4] * 14 + [4] * 4 + [4] * 22 + [4, 4, 4, 4, 4, 2] * 2
KTS2 = [4] * 10 + [2, 1] + [4, 4, 2] * 8 + [4] * 4 + [4] * 16 + [4] * 16
assert len(KTS1) % RING == 0 and len(KTS2) % RING == 0
BLOCKS1, BLOCKS2 = 7 + 1 + 1 + 2 + 11 + 2, 5 + 2 + 16 + 2 + 8 + 2 + 1
TURNS1, TURNS2 = 8 + 4 + 4 + 4 + 11 + 4 + 1, 2 + 1 + 2 + 1 + 10 + 12 + 4 + 1 + 4 + 4 + 16 + 4 + 1
assert not (BLOCKS1 % 2 or BLOCKS2 % 2 or TURNS1 % 2 or TURNS2 % 2)

COLS2 = ((DVAL, 512), (AQ, 512), (AV, 512), (KL, 512), (KL + 512, DVAL - KL - 512))
ORDER = (0, 2, 1, 3)
PLAN2 = {2: 1, 3: 1, 4: 1, 5: 1, 6: 1, 7: 1, 8: 2, 9: 1, 10: 1, 11: 1, 12: 1, 13: 1, 14: 1, 15: 1, 16: 1,
         17: 1, 18: 2, 19: 2, 20: 1, 21: 1, 22: 1, 23: 1, 24: 2, 25: 1, 27: 1, 30: 1, 34: 1, 36: 1}
TAPS_FROM, TAPS_EACH = 6, 3

C_ID, C_TRI, C_ANTI, C_DF, C_DB, C_DA = 0, 128, 256, 384, 896, 1408
C_MCH, C_MCA, C_INV, C_NEG, C_LI, C_OML, C_ONE = 1920, 2304, 2688, 2704, 2736, 2738, 2740
C_W = 2740 + 128


def shape_constants():
    c = np.zeros((P, C_W), np.float32)
    p = np.arange(P)
    c[:, C_ID:C_ID + P] = np.eye(P)
    c[:, C_TRI:C_TRI + P] = p[:, None] <= p[None, :]
    c[:, C_ANTI:C_ANTI + P] = np.eye(P)[::-1]
    t = np.arange(SEQ)
    for s in range(R):
        d = t[None, :] - (s * P + p)[:, None]
        c[:, C_DF + s * SEQ:C_DF + (s + 1) * SEQ] = np.maximum(d, 0)
        c[:, C_DB + s * SEQ:C_DB + (s + 1) * SEQ] = np.maximum(-d, 0)
        c[:, C_DA + s * SEQ:C_DA + (s + 1) * SEQ] = np.abs(d)
    for at, unit in ((C_MCH, 64), (C_MCA, 1)):
        k = np.arange(P)
        c[:, at:at + P] = np.where(k[None, :] // unit <= p[:, None] // unit, 0.0, MASKED)
        q = P + p
        c[:, at + P:at + P + SEQ] = np.where(t[None, :] // unit <= q[:, None] // unit, 0.0, MASKED)
    c[:, C_INV:C_INV + 16] = 1.0 / (np.float32(10000.0) ** (np.arange(16, dtype=np.float32) / np.float32(16)))
    c[:, C_NEG:C_NEG + 32] = -0.5
    for l in range(DEPTH):
        li = 0.8 - 0.6 * np.exp(-0.3 * l)
        c[:, C_LI + l] = li
        c[:, C_OML + l] = 1.0 - li
    c[:, C_ONE:C_ONE + P] = 1.0
    return c


S_X, S_XM, S_XR = 0, 4, 6
S_Q, S_QR = 8, 40
S_NM, S_RS, S_RC = 72, 80, 88
S_O, S_OR, S_P, S_PR = 96, 112, 128, 136
S_L, S_LR = 144, 148
S_Z, S_M, S_A, S_LF = 152, 160, 168, 176
S_NM2, S_RS2, S_RC2 = 184, 188, 212
S_BN, S_MV, S_VR = 236, 248, 252
STEPS_ACT1, STEPS_ACT2 = 4, 8
STEPS_DVE1, STEPS_DVE2 = 26, 85
STEPS_POOL1, STEPS_POOL2 = 9, 24
SMALL_LOADS = 8 + 6 + 7 + 4 + 3

B_RG, B_DG, B_QG, B_KG = 0, 128, 384, 512
B_DF, B_DB, B_FB = 640, 656, 672
B_W = 680


class Place:

    def __init__(self, e):
        self.e, self.base, self.k = e, {}, {}

    def now(self, name):
        return self.base.get(name, 0) + self.k.get(name, 0)

    def next(self, name, n=1):
        self.k[name] = self.k.get(name, 0) + n
        return self.now(name)

    def index(self, name):
        return self.k.get(name, 0)

    def rounds(self, n, per):
        base, k = dict(self.base), dict(self.k)
        with self.e.Fori(0, n) as i:
            for name, by in per.items():
                self.base[name] = i * by + base.get(name, 0)
            yield i
            grown = {x: self.k[x] - k.get(x, 0) for x in self.k if self.k[x] != k.get(x, 0)}
            assert grown == {x: y for x, y in per.items() if y}, (self.e, grown, per)
        self.base = base
        self.k = {x: k.get(x, 0) + n * per.get(x, 0) for x in {*k, *per}}


def bcast(row, at, n):
    return bass.AP(row.tensor, at, [[0, P], [1, n]])


def build(nc, t, out):
    with ExitStack() as ctx:
        def sb(name, shape, dt=F32):
            return ctx.enter_context(nc.sbuf_tensor(name, shape, dt))

        def sem(name):
            return ctx.enter_context(nc.semaphore(name))

        w_raw = sb("w_raw", [P, RING, 4, NB])
        w_hi = sb("w_hi", [P, RING, 4, NB], F32R)
        w_lo = sb("w_lo", [P, RING, 4, NB], F32R)
        x = sb("x", [P, R, D])
        hT_hi = sb("hT_hi", [P, KT, SEQ], F32R)
        hT_lo = sb("hT_lo", [P, KT, SEQ], F32R)
        cst = sb("cst", [P, C_W])
        small = sb("small", [P, B_W])
        gcols = sb("gcols", [P, 72])
        ccols = sb("ccols", [P, DEPTH * 65])
        rope = sb("rope", [P, 2, R, 16])
        stat = sb("stat", [P, 256])
        lam = sb("lam", [P, 4])

        arena_bytes = 68 * 1024
        base_at = -(-nc.sbuf_base // 32) * 32
        arena = sb("arena", [P, arena_bytes // 4 + 8])

        def over(name, shape, kb, dt=F32):
            n = 4
            for s in shape[1:]:
                n *= s
            at = int(kb * 1024)
            assert at + n <= arena_bytes, (name, at + n)
            return nc.alloc_sbuf_tensor_at(name, shape, dt, offset=base_at + at)

        proj1 = over("proj1", [P, R, PROJ1], 0)
        mixed1 = proj1[:, :, 0:D]
        qkT1 = over("qkT1", [P, 8, 512], 28)
        sq1 = over("sq1", [P, R, D], 44)
        decay = over("decay", [P, 2, R * SEQ], 52)
        ret_p = over("ret_p", [P, 2, R * SEQ], 56)
        soft1 = over("soft1", [P, 2, 2, R * SEQ], 52)
        comb1 = over("comb1", [P, R, SEQ], 60)
        combT1 = over("combT1", [P, R, SEQ], 62)
        pooltmp = over("pooltmp", [P, 2 * SEQ], 64)
        hid1T_hi = over("hid1T_hi", [P, FF1 // P, SEQ], 0, F32R)
        hid1T_lo = over("hid1T_lo", [P, FF1 // P, SEQ], 22, F32R)
        gate1 = over("gate1", [P, R, HALF], 44)
        hid1 = over("hid1", [P, R, HALF], 46)
        p_conv = over("p_conv", [P, R, 512], 0)
        p_a = over("p_a", [P, R, 512], 4)
        lat_hi = over("lat_hi", [P, 3, SEQ], 0, F32R)
        lat_lo = over("lat_lo", [P, 3, SEQ], 3, F32R)
        gate2 = over("gate2", [P, R, NB], 0)
        term2 = over("term2", [P, R, NB], 4)
        p_b = over("p_b", [P, R, 512], 8)
        p_c = over("p_c", [P, R, DVAL - KL], 12)
        mix2 = over("mix2", [P, R, D], 19.5)
        obT_hi = over("obT_hi", [P, 2, SEQ], 27.5, F32R)
        obT_lo = over("obT_lo", [P, 2, SEQ], 29.5, F32R)
        branch = over("branch", [P, R, BW], 31.5)
        bgate = over("bgate", [P, 2, NB], 33.5)
        qkT2 = over("qkT2", [P, 3, 512], 37.5)
        soft2 = over("soft2", [P, 2, 384], 43.5)
        softT2 = over("softT2", [P, 2, 384], 46.5)
        abias = over("abias", [P, 4, 384], 49.5)
        qB = over("qB", [P, R, 4, BQD], 49.5)
        kB = over("kB", [P, R, 4, BQD], 52.5)
        kvB = over("kvB", [P, R, 512], 55.5)
        hankel = over("hankel", [P, 4, SEQ], 55.5)
        cqa = over("cqa", [P, R, 4, CAD], 59.5)
        cka = over("cka", [P, R, 4, CAD], 61.5625)
        uT = over("uT", [P, 2, SEQ + TAPS - 1], 63.625)
        yT = over("yT", [P, 2, SEQ], 65.9375)
        convrow = cst[:, C_DF:C_DF + 768].rearrange("p (n c) -> p n c", n=3)
        ropetmp = cst[:, C_DF + 768:C_DF + 1024].rearrange("p (n c) -> p n c", n=4)
        hid2T_hi = over("hid2T_hi", [P, FF2 // P, SEQ], 0, F32R)
        hid2T_lo = over("hid2T_lo", [P, FF2 // P, SEQ], 32, F32R)
        hid2 = over("hid2", [P, R, NB], 64)
        grows = over("grows", [72, P], 0)
        crows = over("crows", [P, DEPTH, P], 1)
        lrows = over("lrows", [P, 4, DEPTH * HD], 3)
        lprod = over("lprod", [P, 2, DEPTH * HD], 5)
        pos_i = over("pos_i", [P, R], 7, I32)
        ropet = over("ropet", [P, 6, R, 16], 8)
        gfin = over("gfin", [P, D], 64)
        outrow = over("outrow", [P, R, D], 32)

        ident = cst[:, C_ID:C_ID + P]
        junk = sb("junk", [P, NB])
        relu = [junk, cst[:, C_DB:C_DB + NB]]

        bank = [ctx.enter_context(nc.psum_tensor(f"bank{i}", [P, NB], F32)) for i in range(8)]
        acc, turn, score = [bank[0:2], bank[2:4]], bank[4:6], bank[6:8]

        consts_in = sem("consts_in")
        small_in = sem("small_in")
        x_in = sem("x_in")
        slab_in = [sem(f"slab_in{i}") for i in range(RING)]
        hi_ready = sem("hi_ready")
        lo_ready = sem("lo_ready")
        slab_used = sem("slab_used")
        acc_free = sem("acc_free")
        turned = sem("turned")
        turn_hi = sem("turn_hi")
        turn_free = sem("turn_free")
        scores = sem("scores")
        scores_out = sem("scores_out")
        soft_ready = sem("soft_ready")
        probs = sem("probs")
        heads_out = sem("heads_out")
        decay_arg = sem("decay_arg")
        decay_ready = sem("decay_ready")
        squares = sem("squares")
        mean_ready = sem("mean_ready")
        rstd_ready = sem("rstd_ready")
        out_free = sem("out_free")
        act_done = sem("act_done")
        dve_ready = sem("dve_ready")
        pool_ready = sem("pool_ready")
        pool_job = sem("pool_job")
        conv_in = sem("conv_in")
        act_job = sem("act_job")
        conv_out = sem("conv_out")
        act_step = sem("act_step")
        dve_step = sem("dve_step")
        pool_step = sem("pool_step")
        held = sem("held")
        layer_in = sem("layer_in")
        bgate_in = [sem(f"bgate_in{i}") for i in range(2)]
        out_ready = sem("out_ready")
        out_done = sem("out_done")
        block = ctx.enter_context(nc.Block())

        def hold(e):
            e.sem_inc(held, 1)

        def rows_of(r):
            return slice(r * P, (r + 1) * P)

        @block.sync
        def _(sp):
            q = Place(sp)
            sp.dma_start(x[:, :, :], t["x"].rearrange("b (r p) d -> p (b r) d", p=P)).then_inc(x_in, 16)
            sp.dma_start(cst[:, :], t["consts"]).then_inc(consts_in, 16)

            def slab(*parts):
                assert len(parts) == 2
                sp.wait_ge(lo_ready, q.next("slab"))
                hold(sp)
                for dst, src in parts:
                    s = (q.index("slab") - 1) % RING
                    sp.dma_start(dst(w_raw[:, s]), src).then_inc(slab_in[s], 16)

            def rows(w, k0, n, c0, cols):
                def part(a, b):
                    src = w[(k0 + a) * P:(k0 + b) * P, bass.ds(c0, cols)]
                    return lambda s: s[:, a:b, 0:cols], src.rearrange("(c p) n -> p c n", p=P)
                if n == 1:
                    h = cols // 2
                    src = w[k0 * P:(k0 + 1) * P, :]
                    return [(lambda s: s[:, 0, 0:h], src[:, c0:c0 + h]),
                            (lambda s: s[:, 0, h:cols], src[:, c0 + h:c0 + cols])]
                return [part(0, n // 2), part(n // 2, n)]

            def halves(w, k0, c0):
                src = w[k0 * P:(k0 + 4) * P, bass.ds(c0, HALF)]
                return src.rearrange("(c p) n -> p c n", p=P)

            for l in q.rounds(DEPTH, dict(slab=len(KTS1))):
                w = {n: t[n][bass.ds(l, 1)].rearrange("o k n -> (o k) n") for n in ("w_in", "w_out", "w_gate", "w_up", "w_down")}
                for i in q.rounds(3, dict(slab=4)):
                    for b in range(2):
                        for k0 in (0, 4):
                            slab(*rows(w["w_in"], k0, 4, i * (2 * NB) + b * NB, NB))
                for k0 in (0, 4):
                    slab(*rows(w["w_in"], k0, 4, 6 * NB, NB))
                for b in range(2):
                    for k0 in (0, 4):
                        slab(*rows(w["w_out"], k0, 4, b * NB, NB))

                def gate_up(c0):
                    for k0 in (0, 4):
                        slab((lambda s: s[:, :, 0:HALF], halves(w["w_gate"], k0, c0)),
                             (lambda s: s[:, :, HALF:NB], halves(w["w_up"], k0, c0)))

                gate_up(0)
                for i in q.rounds(5, dict(slab=4)):
                    gate_up(i * (2 * HALF) + HALF)
                    gate_up(i * (2 * HALF) + 2 * HALF)
                for b in range(2):
                    for k0 in range(0, 22, 4):
                        slab(*rows(w["w_down"], k0, min(4, 22 - k0), b * NB, NB))

            for l in q.rounds(DEPTH, dict(slab=len(KTS2))):
                w = {n: t[n + "_2"][bass.ds(l, 1)].rearrange("o k n -> (o k) n")
                     for n in ("w_in", "w_gate", "w_uq", "w_ukv", "w_o", "w_up", "w_down")}
                w["w_branch"] = t["w_branch_2"][bass.ds(l, 1)].rearrange("o b k n -> (o b k) n")
                for n, (c0, cols) in enumerate(COLS2):
                    if n == 4:
                        sp.dma_start(hankel[:, :, :], bass.AP(
                            t["rel_ext"].tensor, l * (4 * 384), [[1, P], [384, 4], [1, SEQ]])).then_inc(layer_in, 16)
                        for row, name in enumerate(("b_dw_2", "g_conv_ln_2", "b_conv_ln_2")):
                            sp.dma_start(convrow[:, row, :], bcast(t[name], l * 256, 256)).then_inc(layer_in, 16)
                    for k0 in (0, 4):
                        slab(*rows(w["w_in"], k0, 4, c0, cols))
                slab(*rows(w["w_uq"], 0, 2, 0, 384))
                slab(*rows(w["w_ukv"], 0, 1, 0, 512))
                for n in ORDER:
                    for b in range(2):
                        for k0 in (0, 4):
                            slab(*rows(w["w_gate"], k0, 4, n * D + b * NB, NB))
                        slab(*rows(w["w_branch"], 2 * n, 2, b * NB, NB))
                for k0 in (0, 4):
                    for b in range(2):
                        slab(*rows(w["w_o"], k0, 4, b * NB, NB))
                for i in q.rounds(4, dict(slab=4)):
                    for b in range(2):
                        for k0 in (0, 4):
                            slab(*rows(w["w_up"], k0, 4, i * (2 * NB) + b * NB, NB))
                for b in range(2):
                    for k0 in range(0, 32, 4):
                        slab(*rows(w["w_down"], k0, 4, b * NB, NB))
            for s in range(AHEAD):
                sp.wait_ge(lo_ready, q.next("slab"))
                sp.sem_inc(slab_in[s], 32)
            sp.wait_ge(acc_free, 2 + DEPTH * BLOCKS1 + DEPTH * BLOCKS2 - 2)
            sp.dma_start(gfin[:, :], bcast(t["g_final_2"], 0, D)).then_inc(x_in, 16)
            sp.wait_ge(out_ready, 1)
            sp.dma_start(out.rearrange("b (r p) d -> p (b r) d", p=P), outrow[:, :, :]).then_inc(out_done, 16)
            sp.wait_ge(out_done, 16)

        @block.tensor
        def _(pe):
            q = Place(pe)
            pe.sem_inc(slab_used, RING)
            pe.wait_ge(consts_in, 16)

            def open_block():
                pe.wait_ge(acc_free, q.next("blk"))
                return acc[(q.index("blk") - 1) % 2]

            def read_out(blk):
                pe.wait_ge(acc_free, blk + 2)

            def slab_product(a, hi, lo, kts, cols, first, last):
                pe.wait_ge(lo_ready, q.next("slab") + RING)
                s = (q.index("slab") - 1) % RING
                for j, kt in enumerate(kts):
                    for r in range(R):
                        begin, end = first and j == 0, last and j == len(kts) - 1
                        o = a[r][:, 0:cols]
                        pe.matmul(o, hi[:, kt, rows_of(r)], w_hi[:, s, j, 0:cols], start=begin, stop=False)
                        pe.matmul(o, hi[:, kt, rows_of(r)], w_lo[:, s, j, 0:cols], start=False, stop=False)
                        mm = pe.matmul(o, lo[:, kt, rows_of(r)], w_hi[:, s, j, 0:cols], start=False, stop=end)
                mm.then_inc(slab_used, 1)

            def wide_block(cols=NB):
                a = open_block()
                slab_product(a, hT_hi, hT_lo, range(0, 4), cols, True, False)
                slab_product(a, hT_hi, hT_lo, range(4, 8), cols, False, True)

            def turn_group(pieces, skip=0):
                pe.wait_ge(turn_free, q.next("turn"))
                b = turn[(q.index("turn") - 1) % 2]
                for src, col in pieces:
                    n, m = src.shape[0], src.shape[1]
                    tr = pe.transpose(b[0:m, col:col + n], src, ident[0:n, 0:n])
                tr.then_inc(turned, 1 + skip)
                q.next("turn", skip)
                return q.now("turn")

            def all_turned():
                pe.wait_ge(turn_free, q.now("turn") + 2)

            def turn_model(src, groups, skip=0):
                for g in groups:
                    turn_group([(src[:, r, kt * P:(kt + 1) * P], (kt % 2) * SEQ + r * P)
                                for kt in (2 * g, 2 * g + 1) for r in range(R)], skip if g == 3 else 0)

            def turn_x(b, skip=0):
                turn_model(x, (2 * b, 2 * b + 1), skip)

            def turn_pair(qsrc, ksrc):
                return turn_group([(qsrc(0), 0), (qsrc(1), P), (ksrc(0), 2 * P), (ksrc(1), 3 * P)])

            def score_bank():
                pe.wait_ge(scores_out, q.next("scores"))
                return score[(q.index("scores") - 1) % 2]

            pe.wait_ge(small_in, 16 * SMALL_LOADS)
            turn_group([(grows[:, :], 0)])
            turn_group([(crows[0:65, l, :], l * 65) for l in range(DEPTH)])
            pe.wait_ge(x_in, 16)
            turn_model(x, range(4))

            for l in q.rounds(DEPTH, dict(slab=len(KTS1), blk=BLOCKS1, turn=TURNS1, scores=16, pool=3, dve=4)):
                all_turned()
                wide_block()
                for _i in q.rounds(3, dict(slab=4, blk=2)):
                    wide_block()
                    wide_block()
                read_out(q.now("blk"))
                group = [turn_pair(lambda r, j=j: proj1[:, r, RQ + j * P:RQ + (j + 1) * P],
                                   lambda r, j=j: proj1[:, r, RK + j * P:RK + (j + 1) * P]) for j in range(4)]
                o = open_block()

                def ret_scores(h):
                    b, e, j = score_bank(), h % 2, h // 2
                    pe.wait_ge(turn_free, group[j] + 2)
                    for st in range(R):
                        mm = pe.matmul(b[:, st * SEQ:(st + 1) * SEQ],
                                       qkT1[64 * e:64 * e + 64, j, SEQ + st * P:SEQ + (st + 1) * P],
                                       qkT1[64 * e:64 * e + 64, j, 0:SEQ], start=True, stop=True)
                    mm.then_inc(scores, 1)
                    return q.now("scores")

                def ret_values(h, item):
                    pe.wait_ge(scores_out, item + 2)
                    for r in range(R):
                        for st in range(R):
                            mm = pe.matmul(o[r][:, h * HD:(h + 1) * HD],
                                           ret_p[:, h % 2, st * SEQ + r * P:st * SEQ + (r + 1) * P],
                                           proj1[:, st, RV + h * HD:RV + (h + 1) * HD],
                                           start=st == 0, stop=st == R - 1)
                    return mm

                item = ret_scores(0)
                for h in range(1, RH + 1):
                    last = item
                    if h < RH:
                        item = ret_scores(h)
                    mm = ret_values(h - 1, last)
                    if 3 < h < RH:
                        if h == 4:
                            pe.wait_ge(pool_ready, q.next("pool"))
                        c = (h - 4) * P
                        group.append(turn_pair(lambda r: proj1[:, r, DQ + c:DQ + c + P],
                                               lambda r: proj1[:, r, DK + c:DK + c + P]))
                mm.then_inc(heads_out, 1)
                o = open_block()

                def diff_scores(h):
                    for m in range(2):
                        b = score_bank()
                        pe.wait_ge(turn_free, group[4 + h] + 2)
                        for r in range(R):
                            mm = pe.matmul(b[:, r * SEQ:(r + 1) * SEQ],
                                           qkT1[64 * m:64 * m + 64, 4 + h, rows_of(r)],
                                           qkT1[64 * m:64 * m + 64, 4 + h, SEQ:2 * SEQ], start=True, stop=True)
                        mm.then_inc(scores, 1)

                diff_scores(0)
                for h in range(DH):
                    if h + 1 < DH:
                        diff_scores(h + 1)
                    pe.wait_ge(dve_ready, q.next("dve"))
                    n = turn_group([(comb1[:, r, kt * P:(kt + 1) * P], kt * SEQ + r * P)
                                    for kt in range(R) for r in range(R)])
                    pe.wait_ge(turn_free, n + 2)
                    for r in range(R):
                        for kt in range(R):
                            mm = pe.matmul(o[r][:, h * DVD:(h + 1) * DVD], combT1[:, kt, rows_of(r)],
                                           proj1[:, kt, DV + h * DVD:DV + (h + 1) * DVD],
                                           start=kt == 0, stop=kt == R - 1)
                mm.then_inc(heads_out, 1)
                for half in range(2):
                    pe.wait_ge(pool_ready, q.next("pool"))
                    turn_model(mixed1, (2 * half, 2 * half + 1))
                all_turned()
                wide_block()
                wide_block()
                read_out(q.now("blk"))
                turn_model(x, range(4))
                def turn_hid1(blk):
                    read_out(blk)
                    turn_group([(hid1[:, r, c * P:(c + 1) * P], c * SEQ + r * P)
                                for c in range(2) for r in range(R)])

                all_turned()
                wide_block()
                for _i in q.rounds(5, dict(slab=4, blk=2, turn=2)):
                    for _ in range(2):
                        wide_block()
                        turn_hid1(q.now("blk") - 1)
                turn_hid1(q.now("blk"))
                all_turned()
                for b in range(2):
                    a = open_block()
                    for n in range(6):
                        kts = range(4 * n, min(4 * n + 4, FF1 // P))
                        slab_product(a, hid1T_hi, hid1T_lo, kts, NB, n == 0, n == 5)
                        if b == 1 and n == 1:
                            read_out(q.now("blk") - 1)
                            turn_x(0)
                read_out(q.now("blk"))
                turn_x(1, skip=1)
            q.next("probs", DEPTH * DH)
            for l in q.rounds(DEPTH, dict(slab=len(KTS2), blk=BLOCKS2, turn=TURNS2, scores=12, pool=2, dve=6,
                                          layer_in=64, probs=12, conv=1, out=3)):
                projection = [q.now("blk") + n for n in range(len(COLS2) + 3)]
                group = {}

                def turn_head(g):
                    if g < 2:
                        group[g] = turn_pair(lambda r: p_a[:, r, g * P:(g + 1) * P],
                                             lambda r: p_a[:, r, AK + g * P:AK + (g + 1) * P])
                    elif g < 6:
                        group[g] = turn_pair(lambda r: cqa[:, r, g - 2, :], lambda r: cka[:, r, g - 2, :])
                    else:
                        if g == 6:
                            pe.wait_ge(pool_ready, q.next("pool"))
                        group[g] = turn_pair(lambda r: qB[:, r, g - 6, :], lambda r: kB[:, r, g - 6, :])

                def head_scores(h):
                    g = h // 2 if h < 4 else h - 2
                    pe.wait_ge(scores_out, q.next("scores") + 1)
                    pe.wait_ge(turn_free, group[g] + 2)
                    at, d = (64 * (h % 2), HD) if h < 4 else (0, CAD) if h < 8 else (0, BQD)
                    b, s = score[0], qkT2[at:at + d, g % 3, :]
                    pe.matmul(b[:, 0:P], s[:, 0:P], s[:, 2 * P:3 * P], start=True, stop=True)
                    pe.matmul(b[:, P:3 * P], s[:, P:2 * P], s[:, 2 * P:4 * P], start=True, stop=True).then_inc(scores, 1)

                def turn_probs(h):
                    pe.wait_ge(probs, q.next("probs"))
                    s = soft2[:, h % 2, :]
                    group["probs", h] = turn_group([(s[:, k * P:(k + 1) * P], k * P) for k in range(3)])

                def head_values(h):
                    pe.wait_ge(turn_free, group["probs", h] + 2)
                    if h % 4 == 0:
                        pe.wait_ge(out_free, q.next("out"))
                    if h == 0:
                        read_out(projection[3])
                    s = softT2[:, h % 2, :]

                    def v(kt):
                        if h < 4:
                            return p_b[:, kt, h * HD:(h + 1) * HD]
                        if h < 8:
                            return p_c[:, kt, CV - KL + (h - 4) * HD:CV - KL + (h - 3) * HD]
                        return kvB[:, kt, (h - 8) * P + HD:(h - 7) * P]
                    o = [score[1][:, r * BW + (h % 4) * HD:r * BW + (h % 4 + 1) * HD] for r in range(R)]
                    pe.matmul(o[0], s[:, 0:P], v(0), start=True, stop=True)
                    pe.matmul(o[1], s[:, P:2 * P], v(0), start=True, stop=False)
                    mm = pe.matmul(o[1], s[:, 2 * P:3 * P], v(1), start=False, stop=True)
                    if h % 4 == 3:
                        mm.then_inc(heads_out, 1)

                def turn_branch():
                    group["branch"] = turn_group([(branch[:, r, c * P:(c + 1) * P], c * SEQ + r * P)
                                for c in range(2) for r in range(R)])

                def four_heads(first):
                    for h in range(first, first + 6):
                        if h < first + 4:
                            head_scores(h)
                            if 4 <= h < 10:
                                turn_head(h)
                        if first < h < first + 5:
                            turn_probs(h - 1)
                        if h >= first + 2:
                            head_values(h - 2)
                        if h == 3:
                            yield
                            read_out(projection[4])
                            turn_group([(p_b[:, r, QL - AV + kt * P:QL - AV + (kt + 1) * P], kt * SEQ + r * P)
                                        for kt in range(2) for r in range(R)])
                            turn_group([(p_c[:, r, 0:P], r * P) for r in range(R)])
                            group["latents"] = q.now("turn")
                        yield

                def side():
                    yield
                    pe.wait_ge(dve_ready, q.next("dve"))
                    turn_group([(p_conv[:, r, c * P:(c + 1) * P], c * SEQ + r * P) for c in range(2) for r in range(R)])
                    yield
                    pe.wait_ge(layer_in, q.next("layer_in", 64))
                    for g in range(2):
                        pe.wait_ge(turn_free, q.next("turn"))
                        for h in (2 * g, 2 * g + 1):
                            mm = pe.matmul(turn[(q.index("turn") - 1) % 2][:, (h % 2) * SEQ:(h % 2 + 1) * SEQ],
                                           cst[:, C_ANTI:C_ANTI + P], hankel[:, h, :], start=True, stop=True)
                        mm.then_inc(turned, 1)
                    read_out(projection[2])
                    turn_head(0)
                    turn_head(1)
                    yield
                    yield from four_heads(0)
                    pe.wait_ge(dve_ready, q.next("dve"))
                    pe.wait_ge(turn_free, q.next("turn"))
                    b = turn[(q.index("turn") - 1) % 2]
                    logf = stat[:, S_LF:S_LF + 8].rearrange("p (r h) -> p r h", r=R)
                    tri, ones = cst[:, C_TRI:C_TRI + P], cst[:, C_ONE:C_ONE + P]
                    pe.matmul(b[:, 0:4], tri, logf[:, 0, :], start=True, stop=True)
                    pe.matmul(b[:, 4:8], ones, logf[:, 0, :], start=True, stop=False)
                    pe.matmul(b[:, 4:8], tri, logf[:, 1, :], start=False, stop=True).then_inc(turned, 1)
                    yield
                    pe.wait_ge(out_free, q.now("out") + 1)
                    turn_branch()
                    pe.wait_ge(pool_ready, q.next("pool"))
                    pe.wait_ge(dve_ready, q.next("dve"))
                    turn_head(2)
                    turn_head(3)
                    yield
                    for first in (4, 8):
                        yield from four_heads(first)
                        yield
                        pe.wait_ge(out_free, q.now("out") + 1)
                        turn_branch()
                        yield
                    pe.wait_ge(dve_ready, q.next("dve"))
                    turn_group([(yT[:, c, rows_of(r)], r * 256 + c * P) for r in range(R) for c in range(2)])
                    yield
                    pe.wait_ge(conv_out, q.next("conv"))
                    turn_branch()
                    yield
                    for half in range(2):
                        pe.wait_ge(dve_ready, q.next("dve"))
                        turn_model(mix2, (2 * half, 2 * half + 1))
                        yield

                attention, slabs = side(), iter(range(40))

                def product(*args):
                    slab_product(*args)
                    for _ in range(PLAN2.get(next(slabs), 0)):
                        next(attention)

                def model_block(cols=NB):
                    a = open_block()
                    product(a, hT_hi, hT_lo, range(0, 4), cols, True, False)
                    product(a, hT_hi, hT_lo, range(4, 8), cols, False, True)

                all_turned()
                for _c0, cols in COLS2:
                    model_block(cols)
                pe.wait_ge(turn_free, group["latents"] + 2)
                product(open_block(), lat_hi, lat_lo, (0, 1), 384, True, True)
                product(open_block(), lat_hi, lat_lo, (2,), 512, True, True)
                for u in range(2 * NBR):
                    model_block()
                    pe.wait_ge(turn_free, group["branch"] + 2)
                    product(open_block(), obT_hi, obT_lo, (0, 1), NB, True, True)
                a = [open_block(), open_block()]
                for k0 in (0, 4):
                    all_turned()
                    for b in range(2):
                        product(a[b], hT_hi, hT_lo, range(k0, k0 + 4), NB, k0 == 0, k0 == 4)
                assert next(attention, None) is None and next(slabs, None) is None
                read_out(q.now("blk") - 1)
                turn_x(0)
                read_out(q.now("blk"))
                turn_x(1)
                def turn_hid2(blk):
                    read_out(blk)
                    for g in range(2):
                        turn_group([(hid2[:, r, c * P:(c + 1) * P], (c % 2) * SEQ + r * P)
                                    for c in (2 * g, 2 * g + 1) for r in range(R)])

                all_turned()
                wide_block()
                for _i in q.rounds(3, dict(slab=4, blk=2, turn=4)):
                    for _ in range(2):
                        wide_block()
                        turn_hid2(q.now("blk") - 1)
                wide_block()
                turn_hid2(q.now("blk") - 1)
                turn_hid2(q.now("blk"))
                all_turned()
                for b in range(2):
                    a = open_block()
                    for n in range(8):
                        slab_product(a, hid2T_hi, hid2T_lo, range(4 * n, 4 * n + 4), NB, n == 0, n == 7)
                        if b == 1 and n == 1:
                            read_out(q.now("blk") - 1)
                            turn_x(0)
                read_out(q.now("blk"))
                turn_x(1, skip=1)
                q.next("blk")

        @block.scalar
        def _(act):
            q = Place(act)

            def load(dst, src):
                act.dma_start(dst, src).then_inc(small_in, 16)

            for l in range(DEPTH):
                for n, name in enumerate(("attn_norm_g", "ffn_norm_g")):
                    at = 8 * (2 * l + n)
                    load(grows[at:at + 8, :], t[name][l].rearrange("(k p) -> k p", p=P))
                    load(grows[32 + at:40 + at, :], t[("g_mix_2", "g_ffn_2")[n]][l].rearrange("(k p) -> k p", p=P))
                load(crows[0:62, l, :], t["w_dw_2"][l].rearrange("k (c p) -> (k c) p", p=P))
                load(crows[62:64, l, :], t["g_q_lat_2"][l].rearrange("(k p) -> k p", p=P))
                load(crows[64:65, l, :], t["g_kv_lat_2"][l].rearrange("(k p) -> k p", p=P))
            for at, name, n in ((B_RG, "ret_norm_g", HD), (B_DG, "diff_norm_g", DVD), (B_QG, "dq_norm_g", HD),
                                (B_KG, "dk_norm_g", HD), (B_DF, "ret_decay_fwd", RH), (B_DB, "ret_decay_bwd", RH),
                                (B_FB, "b_forget_2", 4)):
                load(small[:, at:at + DEPTH * n], bcast(t[name], 0, DEPTH * n))
            for n, name in enumerate(("lambda_q1", "lambda_k1", "lambda_q2", "lambda_k2")):
                load(lrows[:, n, :], bcast(t[name], 0, DEPTH * HD))
            load(grows[64:72, :], t["g_final_2"].rearrange("(k p) -> k p", p=P))
            for r in range(R):
                load(pos_i[:, r:r + 1], bass.AP(t["positions_2"].tensor, r * P, [[1, P], [1, 1]]))

            def step(ins):
                ins.then_inc(act_step, 1)
                act.wait_ge(act_step, q.next("step"))

            def split_hi(kts=4):
                s = q.index("slab") % RING
                q.next("slab")
                act.wait_ge(slab_in[s], q.next(f"in{s}", 32))
                act.wait_ge(slab_used, q.now("slab"))
                act.copy(w_hi[:, s, 0:kts, :], w_raw[:, s, 0:kts, :]).then_inc(hi_ready, 1)

            def used(n):
                act.wait_ge(slab_used, q.next("used", n) + RING)

            def block_of():
                q.next("blk")
                return acc[(q.index("blk") - 1) % 2]

            def read_out(blk):
                act.wait_ge(acc_free, blk + 2)

            def next_turn(skip=0):
                act.wait_ge(turned, q.next("turn") + skip)
                b = turn[(q.index("turn") - 1) % 2]
                q.next("turn", skip)
                return b

            def take_hi(dst):
                b = next_turn()
                n = dst.shape[1] * dst.shape[2]
                act.copy(dst, b[:, 0:n].rearrange("p (c n) -> p c n", n=SEQ)).then_inc(turn_hi, 1)

            def take_model(src_tiles, gain=None, skip=0):
                b = next_turn(skip)
                for j, kt in enumerate(src_tiles):
                    g = gcols[:, bass.ds(gain + kt, 1)]
                    ins = act.activation(hT_hi[:, kt, :], b[:, j * SEQ:(j + 1) * SEQ], ACT.Copy, scale=g)
                ins.then_inc(turn_hi, 1)

            def square_x(b):
                for r in range(R):
                    ins = act.activation(junk[:, :], x[:, r, b * NB:(b + 1) * NB], ACT.Square,
                                         accum_out=stat[:, S_X + 2 * b + r:S_X + 2 * b + r + 1])
                    step(ins) if r == 0 else ins.then_inc(squares, 1)
                act.wait_ge(squares, q.next("squares"))

            rstd = [stat[:, S_XR + r:S_XR + r + 1] for r in range(R)]

            act.wait_ge(small_in, 16 * SMALL_LOADS)
            act.wait_ge(x_in, 16)
            square_x(0)
            square_x(1)
            act.wait_ge(turned, 1)
            act.activation(small[:, B_DF:B_DF + 32], small[:, B_DF:B_DF + 32], ACT.Exp).then_inc(act_done, 1)
            act.wait_ge(act_job, q.next("act_job"))
            act.activation(lam[:, :], lam[:, :], ACT.Exp).then_inc(act_done, 1)
            act.wait_ge(act_job, q.next("act_job"))
            act.activation(rope[:, :, :, :], rope[:, :, :, :], ACT.Sin).then_inc(act_done, 1)
            q.next("turn", 2)
            for g in range(4):
                take_model((2 * g, 2 * g + 1), 0)
            for _ in range(AHEAD):
                split_hi()

            per = dict(slab=len(KTS1), used=len(KTS1), blk=BLOCKS1, turn=TURNS1,
                       decay=RH, heads=2, soft=DH, rstd=5, squares=7,
                       **{f"in{s}": 32 * len(KTS1) // RING for s in range(RING)})
            per1 = dict(per, step=STEPS_ACT1)
            loop4 = dict(slab=4, used=4, blk=2, **{f"in{s}": 32 for s in range(RING)})
            for l in q.rounds(DEPTH, per1):
                ahead = iter(KTS1[AHEAD:] + KTS1[:AHEAD])

                def splits(n):
                    for _ in range(n):
                        split_hi(next(ahead))

                splits(2)
                for _i in q.rounds(3, loop4):
                    for _ in range(2):
                        used(2)
                        block_of()
                        split_hi()
                        split_hi()
                for _ in range(12):
                    next(ahead)
                used(2)
                block_of()
                q.next("rstd")
                read_out(q.now("blk"))
                act.activation(sq1[:, :, :], proj1[:, :, DQ:DQ + D], ACT.Square).then_inc(squares, 1)
                q.next("squares", 3)
                act.activation(proj1[:, :, RG:RG + RETW], proj1[:, :, RG:RG + RETW], ACT.Silu).then_inc(act_done, 1)
                for h in range(RH):
                    act.wait_ge(decay_arg, q.next("decay"))
                    act.activation(decay[:, h % 2, :], decay[:, h % 2, :], ACT.Exp).then_inc(decay_ready, 1)
                q.next("turn", 8)
                act.wait_ge(heads_out, q.next("heads"))
                o = block_of()
                for r in range(R):
                    ins = act.activation(sq1[:, r, 0:NB], o[r][:, :], ACT.Square)
                ins.then_inc(squares, 1)
                for h in range(DH):
                    act.wait_ge(soft_ready, q.next("soft"))
                    for m in range(2):
                        for r in range(R):
                            n = 4 * (h % 2) + 2 * m + r
                            ins = act.activation(soft1[:, h % 2, m, r * SEQ:(r + 1) * SEQ],
                                                 soft1[:, h % 2, m, r * SEQ:(r + 1) * SEQ], ACT.Exp,
                                                 scale=HD ** -0.5, bias=stat[:, S_NM + n:S_NM + n + 1],
                                                 accum_out=stat[:, S_RS + n:S_RS + n + 1])
                    ins.then_inc(probs, 1)
                q.next("turn", 4)
                act.wait_ge(heads_out, q.next("heads"))
                o = block_of()
                for r in range(R):
                    ins = act.activation(sq1[:, r, NB:D], o[r][:, :], ACT.Square)
                ins.then_inc(squares, 1)
                for g in range(4):
                    take_hi(hT_hi[:, 2 * g:2 * g + 2, :])
                for b in range(2):
                    splits(2)
                    used(2)
                    block_of()
                    read_out(q.now("blk"))
                    square_x(b)
                for g in range(4):
                    take_model((2 * g, 2 * g + 1), l * 16 + 8)
                def gate(first=False):
                    used(2)
                    a = block_of()
                    for r in range(R):
                        ins = act.activation(gate1[:, r, :], a[r][:, 0:HALF], ACT.Silu, scale=rstd[r])
                    ins.then_inc(act_done, 1)

                splits(2)
                act.wait_ge(rstd_ready, q.next("rstd", 4))
                for i in q.rounds(5, dict(loop4, turn=2)):
                    for j in range(2):
                        gate()
                        split_hi()
                        split_hi()
                        take_hi(hid1T_hi[:, bass.ds(i * 4 + 2 * j, 2), :])
                for _ in range(20):
                    next(ahead)
                gate()
                take_hi(hid1T_hi[:, 20:22, :])
                splits(6)
                splits(2)
                used(6)
                block_of()
                read_out(q.now("blk"))
                square_x(0)
                for g in range(2):
                    take_model((2 * g, 2 * g + 1), l * 16 + 16)
                splits(4)
                used(6)
                block_of()
                read_out(q.now("blk"))
                square_x(1)
                take_model((4, 5), l * 16 + 16)
                take_model((6, 7), l * 16 + 16, skip=1)

            per2 = dict(slab=len(KTS2), used=len(KTS2), blk=BLOCKS2, turn=TURNS2, soft=12, act_job=1,
                        rstd=4, squares=5, conv=1, step=STEPS_ACT2,
                        **{f"in{s}": 32 * len(KTS2) // RING for s in range(RING)})
            for l in q.rounds(DEPTH, per2):
                ahead = iter(KTS2[AHEAD:] + KTS2[:AHEAD])

                def splits(n):
                    for _ in range(n):
                        split_hi(next(ahead))

                projection = [q.now("blk") + n for n in range(len(COLS2) + 3)]

                def ordered():
                    act.wait_ge(turn_free, q.now("turn") + 1)

                def take_block(dst, cols, scales, n):
                    used(n)
                    a = block_of()
                    act.wait_ge(acc_free, q.now("blk") + 1)
                    for r in range(R):
                        ins = act.activation(dst(r), a[r][:, 0:cols], ACT.Copy, scale=scales[r])
                    ins.then_inc(acc_free, 1)

                def load_gate_bias(u):
                    act.dma_start(bgate[:, u % 2, :], bcast(
                        t["b_gate_2"], l * (NBR * D) + ORDER[u // 2] * D + (u % 2) * NB, NB)).then_inc(bgate_in[u % 2], 16)

                def take_group(g):
                    b = next_turn()
                    ordered()
                    n = P if g < 2 else CAD if g < 6 else BQD
                    act.copy(qkT2[0:n, g % 3, :], b[0:n, :]).then_inc(turn_free, 1)

                def take_probs(h):
                    b = next_turn()
                    ordered()
                    act.copy(softT2[:, h % 2, :], b[:, 0:3 * P]).then_inc(turn_free, 1)

                def exponentials(h):
                    act.wait_ge(soft_ready, q.next("soft"))
                    for r, (a, z) in enumerate(((0, P), (P, 3 * P))):
                        n = 2 * (h % 2) + r
                        ins = act.activation(soft2[:, h % 2, a:z], soft2[:, h % 2, a:z], ACT.Exp,
                                             bias=stat[:, S_NM2 + n:S_NM2 + n + 1],
                                             accum_out=stat[:, S_RS2 + 12 * r + h:S_RS2 + 12 * r + h + 1])
                    ins.then_inc(probs, 1)

                def latents():
                    read_out(projection[4])
                    n = 0
                    for src in (p_b[:, :, QL - AV:QL - AV + 256], p_c[:, :, 0:P]):
                        for r in range(R):
                            ins = act.activation(junk[:, 0:src.shape[2]], src[:, r, :], ACT.Square,
                                                 accum_out=stat[:, S_L + n:S_L + n + 1])
                            n += 1
                            step(ins) if n < 4 else ins.then_inc(squares, 1)
                    q.next("squares")
                    b = next_turn()
                    for c in range(2):
                        ins = act.activation(lat_hi[:, c, :], b[:, c * SEQ:(c + 1) * SEQ], ACT.Copy,
                                             scale=ccols[:, bass.ds(l * 65 + 62 + c, 1)])
                    ins.then_inc(turn_hi, 1)
                    b = next_turn()
                    act.activation(lat_hi[:, 2, :], b[:, 0:SEQ], ACT.Copy,
                                   scale=ccols[:, bass.ds(l * 65 + 64, 1)]).then_inc(turn_hi, 1)

                def four_heads(first):
                    for h in range(first, first + 6):
                        if h < first + 4 and 4 <= h < 10:
                            take_group(h)
                        if first < h < first + 5:
                            take_probs(h - 1)
                        if h < first + 4:
                            exponentials(h)
                        if h == 3:
                            yield
                            latents()
                        if h == first + 5 == 5:
                            act.wait_ge(act_job, q.next("act_job"))
                            step(act.activation(stat[:, S_A:S_A + 8], stat[:, S_A:S_A + 8], ACT.Exp))
                            act.activation(stat[:, S_A:S_A + 8], stat[:, S_A:S_A + 8], ACT.Ln,
                                           bias=1.0).then_inc(act_done, 1)
                        yield

                def side():
                    read_out(projection[1])
                    act.activation(p_conv[:, :, 256:512], p_conv[:, :, 256:512], ACT.Sigmoid).then_inc(act_done, 1)
                    yield
                    q.next("turn")
                    yield
                    load_gate_bias(0)
                    load_gate_bias(1)
                    q.next("turn", 2)
                    take_group(0)
                    take_group(1)
                    yield
                    yield from four_heads(0)
                    q.next("turn")
                    yield
                    take_hi(obT_hi[:, :, :])
                    take_group(2)
                    take_group(3)
                    yield
                    for first in (4, 8):
                        yield from four_heads(first)
                        yield
                        take_hi(obT_hi[:, :, :])
                        yield
                    q.next("turn")
                    act.wait_ge(conv_in, q.next("conv"))
                    act.activation(branch[:, :, :], branch[:, :, :], ACT.Silu).then_inc(conv_out, 1)
                    yield
                    take_hi(obT_hi[:, :, :])
                    yield
                    for half in range(2):
                        for g in (2 * half, 2 * half + 1):
                            take_hi(hT_hi[:, 2 * g:2 * g + 2, :])
                        yield

                due, lat = {}, [[stat[:, S_LR + 2 * n + r:S_LR + 2 * n + r + 1] for r in range(R)] for n in range(2)]
                places = (lambda r: p_conv[:, r, :], lambda r: p_a[:, r, :], lambda r: p_b[:, r, :],
                          lambda r: p_c[:, r, 0:NB], lambda r: p_c[:, r, NB:DVAL - KL])
                for n, (_c0, cols) in enumerate(COLS2):
                    due[2 * n + 1] = lambda n=n, cols=cols: take_block(places[n], cols, rstd, 2)

                def latent_product(n):
                    if n == 0:
                        act.wait_ge(rstd_ready, q.next("rstd"))
                    dst = (lambda r: qB[:, r].rearrange("p h d -> p (h d)"), lambda r: kvB[:, r, :])[n]
                    take_block(dst, (384, 512)[n], lat[n], 1)

                def gate(u):
                    used(2)
                    block_of()
                    read_out(q.now("blk"))
                    act.activation(gate2[:, :, :], term2[:, :, :], ACT.Sigmoid).then_inc(act_done, 1)
                    if u + 2 < 2 * NBR:
                        load_gate_bias(u + 2)

                def branch_product():
                    used(1)
                    block_of()

                def added(b):
                    used(3 if b == 0 else 1)
                    block_of()
                    read_out(q.now("blk"))
                    square_x(b)

                for n in range(2):
                    due[10 + n] = lambda n=n: latent_product(n)
                for u in range(2 * NBR):
                    due[13 + 3 * u] = lambda u=u: gate(u)
                    due[14 + 3 * u] = branch_product
                for b in range(2):
                    due[38 + b] = lambda b=b: added(b)

                act.wait_ge(rstd_ready, q.next("rstd"))
                attention = side()
                for s in range(40):
                    splits(1)
                    if s in due:
                        due[s]()
                    for _ in range(PLAN2.get(s, 0)):
                        next(attention)
                assert next(attention, None) is None
                for g in range(4):
                    take_model((2 * g, 2 * g + 1), l * 16 + 40)
                def rectify():
                    used(2)
                    a = block_of()
                    for r in range(R):
                        ins = act.activation(relu[r][:, :], a[r][:, :], ACT.Relu, scale=rstd[r])
                    ins.then_inc(act_done, 1)

                splits(2)
                act.wait_ge(rstd_ready, q.next("rstd", 2))
                for i in q.rounds(3, dict(loop4, turn=4)):
                    for j in range(2):
                        rectify()
                        split_hi()
                        split_hi()
                        for g in range(2):
                            take_hi(hid2T_hi[:, bass.ds(i * 8 + 4 * j + 2 * g, 2), :])
                for _ in range(12):
                    next(ahead)
                rectify()
                splits(2)
                for g in range(2):
                    take_hi(hid2T_hi[:, 24 + 2 * g:26 + 2 * g, :])
                rectify()
                for g in range(2):
                    take_hi(hid2T_hi[:, 28 + 2 * g:30 + 2 * g, :])
                splits(8)
                splits(2)
                used(8)
                block_of()
                read_out(q.now("blk"))
                square_x(0)
                for g in range(2):
                    take_model((2 * g, 2 * g + 1), l * 16 + 48)
                splits(6)
                used(8)
                block_of()
                read_out(q.now("blk"))
                square_x(1)
                take_model((4, 5), l * 16 + 48)
                take_model((6, 7), l * 16 + 48, skip=1)
                q.next("blk")

        @block.vector
        def _(dve):
            q = Place(dve)
            dve.sem_inc(lo_ready, RING)
            dve.sem_inc(acc_free, 2)
            dve.sem_inc(turn_free, 2)
            dve.sem_inc(scores_out, 2)
            dve.sem_inc(out_free, 1)

            def step(ins):
                ins.then_inc(dve_step, 1)
                dve.wait_ge(dve_step, q.next("step"))

            def split_lo(kts=4):
                s = q.index("slab") % RING
                dve.wait_ge(hi_ready, q.next("slab"))
                dve.tensor_tensor(w_lo[:, s, 0:kts, :], w_raw[:, s, 0:kts, :],
                                  w_hi[:, s, 0:kts, :].bitcast(F32), ALU.subtract).then_inc(lo_ready, 1)

            def used(n):
                dve.wait_ge(slab_used, q.next("used", n) + RING)

            def block_of():
                q.next("blk")
                return acc[(q.index("blk") - 1) % 2]

            def next_turn(skip=0):
                dve.wait_ge(turned, q.next("turn") + skip)
                b = turn[(q.index("turn") - 1) % 2]
                q.next("turn", skip)
                return b

            def next_hi():
                q.next("turn")
                dve.wait_ge(turn_hi, q.next("turn_hi"))
                return turn[(q.index("turn") - 1) % 2]

            def take_lo(dst, hi):
                b = next_hi()
                n = dst.shape[1] * dst.shape[2]
                dve.tensor_tensor(dst, b[:, 0:n].rearrange("p (c n) -> p c n", n=SEQ), hi.bitcast(F32),
                                  ALU.subtract).then_inc(turn_free, 1)

            def lo_with_gain(lo, hi, src, gain):
                return dve.scalar_tensor_tensor(lo, src, gain, hi.bitcast(F32), ALU.mult, ALU.subtract)

            def take_model(tiles, gain, skip=0):
                b = next_hi()
                for j, kt in enumerate(tiles):
                    ins = lo_with_gain(hT_lo[:, kt, :], hT_hi[:, kt, :], b[:, j * SEQ:(j + 1) * SEQ],
                                       gcols[:, bass.ds(gain + kt, 1)])
                ins.then_inc(turn_free, 1 + skip)
                q.next("turn", skip)

            def add_x(b):
                a = block_of()
                for r in range(R):
                    ins = dve.tensor_tensor(x[:, r, b * NB:(b + 1) * NB], x[:, r, b * NB:(b + 1) * NB],
                                            a[r][:, :], ALU.add)
                ins.then_inc(acc_free, 1)

            def mean(dst, src, n):
                dve.tensor_scalar(dst, src, 1.0 / n, EPS, ALU.mult, ALU.add).then_inc(mean_ready, 1)

            def mean_x():
                dve.wait_ge(squares, q.next("squares", 2))
                step(dve.tensor_tensor(stat[:, S_XM:S_XM + 2], stat[:, S_X:S_X + 2], stat[:, S_X + 2:S_X + 4], ALU.add))
                mean(stat[:, S_XM:S_XM + 2], stat[:, S_XM:S_XM + 2], D)

            def root():
                dve.wait_ge(rstd_ready, q.next("rstd"))

            def per_head(at, r, heads, width):
                return stat[:, at + r * heads:at + (r + 1) * heads].unsqueeze(2).to_broadcast([P, heads, width])

            rstd = [stat[:, S_XR + r:S_XR + r + 1] for r in range(R)]

            dve.wait_ge(consts_in, 16)
            dve.wait_ge(small_in, 16 * SMALL_LOADS)
            for n in range(2):
                step(dve.tensor_tensor(lprod[:, n, :], lrows[:, 2 * n, :], lrows[:, 2 * n + 1, :], ALU.mult))
            dve.tensor_reduce(lam[:, :], lprod[:, :, :].rearrange("p n (l d) -> p (n l) d", l=DEPTH), AX.X,
                              ALU.add).then_inc(act_job, 1)
            posf = ropet[:, 5, :, 0]
            step(dve.tensor_copy(posf, pos_i[:, :]))
            for r in range(R):
                step(dve.tensor_scalar(ropet[:, 0, r, :], cst[:, C_INV:C_INV + 16], ropet[:, 5, r, 0:1], None, ALU.mult))
            ang, turns, red = ropet[:, 0], ropet[:, 1], ropet[:, 2]
            step(dve.tensor_scalar(turns, ang, 1.0 / (2 * np.pi), 12582912.0, ALU.mult, ALU.add))
            step(dve.tensor_scalar(turns, turns, 12582912.0, None, ALU.subtract))
            parts = (6.28125, 0.0019350051879882812, 3.0199159819e-07)
            step(dve.scalar_tensor_tensor(red, turns, -parts[0], ang, ALU.mult, ALU.add))
            step(dve.scalar_tensor_tensor(red, turns, -parts[1], red, ALU.mult, ALU.add))
            step(dve.scalar_tensor_tensor(red, turns, -parts[2], red, ALU.mult, ALU.add))
            step(dve.tensor_scalar(rope[:, 1], red, 3.1415925, -3.1415925, ALU.min, ALU.max))
            step(dve.tensor_scalar(ropet[:, 3], rope[:, 1], -1.0, None, ALU.mult))
            step(dve.tensor_tensor(ropet[:, 3], ropet[:, 3], rope[:, 1], ALU.max))
            dve.tensor_scalar(rope[:, 0], ropet[:, 3], -1.0, float(np.pi / 2), ALU.mult, ALU.add).then_inc(act_job, 1)
            b = next_turn()
            dve.tensor_copy(gcols[:, :], b[:, 0:72]).then_inc(turn_free, 1)
            b = next_turn()
            dve.tensor_copy(ccols[:, :], b[:, 0:DEPTH * 65]).then_inc(turn_free, 1)
            mean_x()
            dve.wait_ge(act_done, q.next("act_done", 3))
            dve.tensor_scalar(small[:, B_DF:B_DF + 32], small[:, B_DF:B_DF + 32], -1.0, None,
                              ALU.mult).then_inc(pool_job, 1)
            step(dve.tensor_tensor(lam[:, 0:DEPTH], lam[:, 0:DEPTH], lam[:, DEPTH:2 * DEPTH], ALU.subtract))
            step(dve.tensor_tensor(lam[:, 0:DEPTH], lam[:, 0:DEPTH], cst[:, C_LI:C_LI + DEPTH], ALU.add))
            step(dve.tensor_scalar(lam[:, 0:DEPTH], lam[:, 0:DEPTH], -1.0, None, ALU.mult))
            for g in range(4):
                take_model((2 * g, 2 * g + 1), 0)
            for _ in range(AHEAD):
                split_lo()

            loop4 = dict(slab=4, used=4, blk=2)
            for l in q.rounds(DEPTH, dict(slab=len(KTS1), used=len(KTS1), blk=BLOCKS1, turn=TURNS1,
                                          turn_hi=TURNS1 - 13, squares=7, rstd=5, act_done=12, scores=16,
                                          decay=RH, probs=DH, step=STEPS_DVE1)):
                ahead = iter(KTS1[AHEAD:] + KTS1[:AHEAD])

                def splits(n):
                    for _ in range(n):
                        split_lo(next(ahead))

                def take_proj(at):
                    used(2)
                    a = block_of()
                    for r in range(R):
                        ins = dve.tensor_scalar(proj1[:, r, bass.ds(at, NB)], a[r][:, :], rstd[r], None, ALU.mult)
                    ins.then_inc(acc_free, 1)

                splits(2)
                root()
                hold(dve)
                for i in q.rounds(3, loop4):
                    for j in range(2):
                        take_proj(i * (2 * NB) + j * NB)
                        split_lo()
                        split_lo()
                for _ in range(12):
                    next(ahead)
                take_proj(6 * NB)
                dve.wait_ge(squares, q.next("squares"))
                step(dve.tensor_reduce(stat[:, S_Q:S_Q + 32], sq1[:, :, :].rearrange("p r (h d) -> p (r h) d", d=HD),
                                       AX.X, ALU.add))
                mean(stat[:, S_Q:S_Q + 32], stat[:, S_Q:S_Q + 32], HD)
                for j in range(4):
                    b = next_turn()
                    dve.tensor_copy(qkT1[:, j, :], b[:, :]).then_inc(turn_free, 1)
                root()
                for r in range(R):
                    v = proj1[:, r, DQ:DQ + D].rearrange("p (h d) -> p h d", d=HD)
                    ins = dve.tensor_tensor(v, v, per_head(S_QR, r, 16, HD), ALU.mult)
                ins.then_inc(pool_job, 1)
                for h in range(RH):
                    dve.wait_ge(scores, q.next("scores"))
                    dve.wait_ge(decay_ready, q.next("decay"))
                    dve.scalar_tensor_tensor(ret_p[:, h % 2, :], score[h % 2][:, :], HD ** -0.5, decay[:, h % 2, :],
                                             ALU.mult, ALU.mult).then_inc(scores_out, 1)
                    if h > 3:
                        b = next_turn()
                        dve.tensor_copy(qkT1[:, h, :], b[:, :]).then_inc(turn_free, 1)
                dve.wait_ge(act_done, q.next("act_done"))
                o = block_of()
                dve.wait_ge(squares, q.next("squares"))
                step(dve.tensor_reduce(stat[:, S_O:S_O + 16], sq1[:, :, 0:NB].rearrange("p r (h d) -> p r h d", d=HD),
                                       AX.X, ALU.add))
                mean(stat[:, S_O:S_O + 16], stat[:, S_O:S_O + 16], HD)
                root()
                for r in range(R):
                    ins = dve.tensor_tensor(mixed1[:, r, 0:NB].rearrange("p (h d) -> p h d", d=HD),
                                            o[r][:, :].rearrange("p (h d) -> p h d", d=HD),
                                            per_head(S_OR, r, RH, HD), ALU.mult)
                ins.then_inc(acc_free, 1)
                def soften(h):
                    for m in range(2):
                        dve.wait_ge(scores, q.next("scores"))
                        slope = 2.0 ** (-8.0 * (h + 1) / DH)
                        dve.scalar_tensor_tensor(soft1[:, h % 2, m, :], cst[:, C_DA:C_DA + R * SEQ],
                                                 -slope * HD ** 0.5, score[m][:, :], ALU.mult, ALU.add
                                                 ).then_inc(scores_out, 1)
                    dve.wait_ge(scores_out, q.now("scores") + 2)
                    at = S_NM + 4 * (h % 2)
                    step(dve.tensor_reduce(stat[:, at:at + 4], soft1[:, h % 2].rearrange("p m (r k) -> p (m r) k", r=R),
                                           AX.X, ALU.max))
                    dve.tensor_scalar(stat[:, at:at + 4], stat[:, at:at + 4], -HD ** -0.5, None,
                                      ALU.mult).then_inc(soft_ready, 1)

                def combine(h):
                    dve.wait_ge(probs, q.next("probs"))
                    at, rs = S_RC + 4 * (h % 2), S_RS + 4 * (h % 2)
                    step(dve.reciprocal(stat[:, at:at + 4], stat[:, rs:rs + 4]))
                    step(dve.tensor_scalar(stat[:, at + 2:at + 4], stat[:, at + 2:at + 4], lam[:, bass.ds(l, 1)], None, ALU.mult))
                    for r in range(R):
                        step(dve.tensor_scalar(comb1[:, r, :], soft1[:, h % 2, 1, r * SEQ:(r + 1) * SEQ],
                                               stat[:, at + 2 + r:at + 3 + r], None, ALU.mult))
                    for r in range(R):
                        ins = dve.scalar_tensor_tensor(comb1[:, r, :], soft1[:, h % 2, 0, r * SEQ:(r + 1) * SEQ],
                                                       stat[:, at + r:at + r + 1], comb1[:, r, :], ALU.mult, ALU.add)
                    ins.then_inc(dve_ready, 1)
                    b = next_turn()
                    dve.tensor_copy(combT1[:, :, :].rearrange("p r k -> p (r k)"), b[:, :]).then_inc(turn_free, 1)

                soften(0)
                for h in range(DH):
                    if h + 1 < DH:
                        soften(h + 1)
                    combine(h)
                o = block_of()
                dve.wait_ge(squares, q.next("squares"))
                step(dve.tensor_reduce(stat[:, S_P:S_P + 8], sq1[:, :, NB:D].rearrange("p r (h d) -> p r h d", d=DVD),
                                       AX.X, ALU.add))
                mean(stat[:, S_P:S_P + 8], stat[:, S_P:S_P + 8], DVD)
                root()
                step(dve.tensor_scalar(stat[:, S_PR:S_PR + 8], stat[:, S_PR:S_PR + 8],
                                       cst[:, bass.ds(l + C_OML, 1)], None, ALU.mult))
                for r in range(R):
                    ins = dve.tensor_tensor(mixed1[:, r, NB:D].rearrange("p (h d) -> p h d", d=DVD),
                                            o[r][:, :].rearrange("p (h d) -> p h d", d=DVD),
                                            per_head(S_PR, r, DH, DVD), ALU.mult)
                ins.then_inc(acc_free, 1)
                for g in range(4):
                    take_lo(hT_lo[:, 2 * g:2 * g + 2, :], hT_hi[:, 2 * g:2 * g + 2, :])
                for b in range(2):
                    splits(2)
                    used(2)
                    add_x(b)
                mean_x()
                for g in range(4):
                    take_model((2 * g, 2 * g + 1), l * 16 + 8)
                def up():
                    used(2)
                    a = block_of()
                    dve.wait_ge(act_done, q.next("act_done"))
                    for r in range(R):
                        ins = dve.scalar_tensor_tensor(hid1[:, r, :], a[r][:, HALF:NB], rstd[r], gate1[:, r, :],
                                                       ALU.mult, ALU.mult)
                    ins.then_inc(acc_free, 1)

                splits(2)
                root()
                hold(dve)
                for i in q.rounds(5, dict(loop4, turn=2, turn_hi=2, act_done=2)):
                    for j in range(2):
                        up()
                        split_lo()
                        split_lo()
                        take_lo(hid1T_lo[:, bass.ds(i * 4 + 2 * j, 2), :], hid1T_hi[:, bass.ds(i * 4 + 2 * j, 2), :])
                for _ in range(20):
                    next(ahead)
                up()
                take_lo(hid1T_lo[:, 20:22, :], hid1T_hi[:, 20:22, :])
                splits(8)
                used(6)
                add_x(0)
                for g in range(2):
                    take_model((2 * g, 2 * g + 1), l * 16 + 16)
                splits(4)
                used(6)
                add_x(1)
                mean_x()
                take_model((4, 5), l * 16 + 16)
                take_model((6, 7), l * 16 + 16, skip=1)

            q.next("heads", DEPTH * 2)
            for l in q.rounds(DEPTH, dict(slab=len(KTS2), used=len(KTS2), blk=BLOCKS2, turn=TURNS2,
                                          turn_hi=2 + 4 + 4 + 4 + 16 + 4, squares=5, rstd=4, act_done=18, scores=12,
                                          heads=3, layer_in=64, bgate0=64, bgate1=64, step=STEPS_DVE2)):
                ahead = iter(KTS2[AHEAD:] + KTS2[:AHEAD])

                def splits(n):
                    for _ in range(n):
                        split_lo(next(ahead))

                projection = [q.now("blk") + n for n in range(len(COLS2) + 3)]
                z, m, a8, lf = (stat[:, s:s + 8] for s in (S_Z, S_M, S_A, S_LF))

                def ordered():
                    dve.wait_ge(turn_free, q.now("turn") + 1)

                def lo_of(dst, hi):
                    dve.wait_ge(turn_free, q.now("turn") + 2)
                    take_lo(dst, hi)

                def soften(h):
                    dve.wait_ge(scores, q.next("scores"))
                    bias = abias[:, h, :] if h < 4 else cst[:, C_MCA:C_MCA + 384] if h < 8 else cst[:, C_MCH:C_MCH + 384]
                    dve.scalar_tensor_tensor(soft2[:, h % 2, :], score[0][:, 0:384],
                                             HD ** -0.5 if h < 8 else BQD ** -0.5, bias, ALU.mult, ALU.add
                                             ).then_inc(scores_out, 1)
                    dve.wait_ge(scores_out, q.now("scores") + 2)
                    n = S_NM2 + 2 * (h % 2)
                    dve.tensor_reduce(stat[:, n:n + 1], soft2[:, h % 2, 0:P], AX.X, ALU.max, negate=True)
                    dve.tensor_reduce(stat[:, n + 1:n + 2], soft2[:, h % 2, P:3 * P], AX.X, ALU.max,
                                      negate=True).then_inc(soft_ready, 1)

                def normalise(n):
                    dve.wait_ge(heads_out, q.next("heads"))
                    rs, rc = (stat[:, at:at + 24].rearrange("p (r h) -> p r h", r=R)[:, :, 4 * n:4 * n + 4]
                              for at in (S_RS2, S_RC2))
                    step(dve.reciprocal(rc, rs))
                    for r in range(R):
                        at = S_RC2 + 12 * r + 4 * n
                        ins = dve.tensor_tensor(branch[:, r, :].rearrange("p (h d) -> p h d", d=HD),
                                                score[1][:, r * BW:(r + 1) * BW].rearrange("p (h d) -> p h d", d=HD),
                                                stat[:, at:at + 4].unsqueeze(2).to_broadcast([P, 4, HD]), ALU.mult)
                    ins.then_inc(out_free, 1)

                def latents():
                    dve.wait_ge(squares, q.next("squares"))
                    step(dve.tensor_scalar(stat[:, S_L:S_L + 2], stat[:, S_L:S_L + 2], 1.0 / 256, EPS, ALU.mult, ALU.add))
                    mean(stat[:, S_L + 2:S_L + 4], stat[:, S_L + 2:S_L + 4], P)
                    b = next_hi()
                    ordered()
                    for c in range(2):
                        ins = lo_with_gain(lat_lo[:, c, :], lat_hi[:, c, :], b[:, c * SEQ:(c + 1) * SEQ],
                                           ccols[:, bass.ds(l * 65 + 62 + c, 1)])
                    ins.then_inc(turn_free, 1)
                    b = next_hi()
                    lo_with_gain(lat_lo[:, 2, :], lat_hi[:, 2, :], b[:, 0:SEQ],
                                 ccols[:, bass.ds(l * 65 + 64, 1)]).then_inc(turn_free, 1)

                def four_heads(first):
                    for h in range(first, first + 6):
                        if h < first + 4:
                            soften(h)
                            q.next("turn", 1 if 4 <= h < 10 else 0)
                        if first < h < first + 5:
                            q.next("turn")
                        if h == 3:
                            yield
                            latents()
                        if h == first + 5 == 5:
                            dve.wait_ge(acc_free, projection[5] + 2)
                            for r in range(R):
                                step(dve.tensor_tensor(z[:, 4 * r:4 * r + 4], p_c[:, r, CF - KL:CF - KL + 4],
                                                       small[:, bass.ds(l * 4 + B_FB, 4)], ALU.add))
                            step(dve.tensor_scalar(m, z, -1.0, None, ALU.mult))
                            dve.tensor_tensor(a8, m, z, ALU.min).then_inc(act_job, 1)
                            step(dve.tensor_scalar(z, z, 0.0, None, ALU.min))
                        yield

                def side():
                    dve.wait_ge(act_done, q.next("act_done"))
                    dve.tensor_tensor(p_conv[:, :, 0:256], p_conv[:, :, 0:256], p_conv[:, :, 256:512],
                                      ALU.mult).then_inc(dve_ready, 1)
                    yield
                    step(dve.memset(uT[:, :, 0:TAPS - 1], 0.0))
                    b = next_turn()
                    step(dve.tensor_copy(uT[:, :, TAPS - 1:], b[:, :].rearrange("p (c n) -> p c n", c=2)))
                    dve.sem_inc(turn_free, 1)
                    yield
                    dve.wait_ge(layer_in, q.next("layer_in", 64))
                    for g in range(2):
                        b = next_turn()
                        v = b[:, :].rearrange("p (h k) -> p h k", h=2)
                        dve.tensor_tensor(abias[:, 2 * g:2 * g + 2, 0:P], v[:, :, P:2 * P],
                                          cst[:, C_MCH:C_MCH + P].unsqueeze(1).to_broadcast([P, 2, P]), ALU.add)
                        dve.tensor_tensor(abias[:, 2 * g:2 * g + 2, P:3 * P], v,
                                          cst[:, C_MCH + P:C_MCH + 3 * P].unsqueeze(1).to_broadcast([P, 2, SEQ]),
                                          ALU.add).then_inc(turn_free, 1)
                    q.next("turn", 2)
                    yield
                    yield from four_heads(0)
                    dve.wait_ge(act_done, q.next("act_done"))
                    dve.tensor_tensor(lf, z, a8, ALU.subtract).then_inc(dve_ready, 1)
                    normalise(0)
                    b = next_turn()
                    ordered()
                    sums = b[:, 0:8].rearrange("p (r h) -> p r h", r=R)
                    dve.tensor_scalar(cqa[:, :, :, HD], sums, HD ** 0.5, None, ALU.mult)
                    dve.tensor_scalar(cka[:, :, :, HD + 1], sums, -HD ** 0.5, None, ALU.mult).then_inc(turn_free, 1)
                    one = cst[:, C_ONE:C_ONE + 8].rearrange("p (r h) -> p r h", r=R)
                    dve.tensor_copy(cka[:, :, :, HD], one)
                    dve.tensor_copy(cqa[:, :, :, HD + 1], one).then_inc(dve_ready, 1)
                    yield
                    lo_of(obT_lo[:, :, :], obT_hi[:, :, :])
                    q.next("turn", 2)
                    yield
                    for n in (1, 2):
                        yield from four_heads(4 * n)
                        normalise(n)
                        yield
                        lo_of(obT_lo[:, :, :], obT_hi[:, :, :])
                        yield
                    b = next_turn()
                    rows3 = [convrow[:, n, :].unsqueeze(1).to_broadcast([P, R, 256]) for n in range(3)]
                    step(dve.tensor_tensor(branch[:, :, :], b[:, :].rearrange("p (r n) -> p r n", r=R), rows3[0], ALU.add))
                    dve.sem_inc(turn_free, 1)
                    for r in range(R):
                        ins = dve.bn_stats(stat[:, S_BN + 6 * r:S_BN + 6 * r + 6], branch[:, r, :])
                    step(ins)
                    hold(dve)
                    for r in range(R):
                        ins = dve.bn_aggr(stat[:, S_MV + 2 * r:S_MV + 2 * r + 2], stat[:, S_BN + 6 * r:S_BN + 6 * r + 6])
                    step(ins)
                    dve.tensor_scalar(stat[:, S_VR:S_VR + 2], stat[:, S_MV:S_MV + 4].rearrange("p (r n) -> p r n", n=2)[:, :, 1],
                                      EPS, None, ALU.add).then_inc(mean_ready, 1)
                    root()
                    for r in range(R):
                        step(dve.tensor_scalar(branch[:, r, :], branch[:, r, :], stat[:, S_MV + 2 * r:S_MV + 2 * r + 1],
                                               stat[:, S_VR + r:S_VR + r + 1], ALU.subtract, ALU.mult))
                    step(dve.tensor_tensor(branch[:, :, :], branch[:, :, :], rows3[1], ALU.mult))
                    dve.tensor_tensor(branch[:, :, :], branch[:, :, :], rows3[2], ALU.add).then_inc(conv_in, 1)
                    yield
                    take_lo(obT_lo[:, :, :], obT_hi[:, :, :])
                    yield
                    for half in range(2):
                        for g in (2 * half, 2 * half + 1):
                            take_lo(hT_lo[:, 2 * g:2 * g + 2, :], hT_hi[:, 2 * g:2 * g + 2, :])
                        yield

                def taps():
                    for k in range(TAPS):
                        for c in range(2):
                            w = ccols[:, bass.ds(l * 65 + 2 * k + c, 1)]
                            src = uT[:, c, k:k + SEQ]
                            if k == 0:
                                ins = dve.tensor_scalar(yT[:, c, :], src, w, None, ALU.mult)
                            else:
                                dve.wait_ge(dve_step, q.now("step") - 1)
                                ins = dve.scalar_tensor_tensor(yT[:, c, :], src, w, yT[:, c, :], ALU.mult, ALU.add)
                            if k == TAPS - 1 and c == 1:
                                ins.then_inc(dve_ready, 1)
                            else:
                                ins.then_inc(dve_step, 1)
                                q.next("step")
                            yield

                def others(n):
                    used(n)
                    block_of()

                def latent_product(n):
                    if n == 0:
                        root()
                    others(1)

                def gate(u):
                    used(2)
                    a = block_of()
                    dve.wait_ge(acc_free, q.now("blk") + 1)
                    dve.wait_ge(bgate_in[u % 2], q.next(f"bgate{u % 2}", 16))
                    for r in range(R):
                        ins = dve.scalar_tensor_tensor(term2[:, r, :], a[r][:, :], rstd[r], bgate[:, u % 2, :],
                                                       ALU.mult, ALU.add)
                    ins.then_inc(acc_free, 1)

                def branch_product(u):
                    used(1)
                    a = block_of()
                    dve.wait_ge(act_done, q.next("act_done"))
                    cols = slice((u % 2) * NB, (u % 2 + 1) * NB)
                    for r in range(R):
                        dst = mix2[:, r, cols] if u < 2 else term2[:, r, :]
                        ins = dve.tensor_tensor(dst, gate2[:, r, :], a[r][:, :], ALU.mult)
                    ins.then_inc(acc_free, 1)
                    if u >= 2:
                        dve.wait_ge(acc_free, q.now("blk") + 2)
                        step(dve.tensor_tensor(mix2[:, :, cols], mix2[:, :, cols], term2[:, :, :], ALU.add))
                        if u >= 6:
                            dve.sem_inc(dve_ready, 1)

                due = {2 * n + 1: lambda: others(2) for n in range(len(COLS2))}
                for n in range(2):
                    due[10 + n] = lambda n=n: latent_product(n)
                for u in range(2 * NBR):
                    due[13 + 3 * u] = lambda u=u: gate(u)
                    due[14 + 3 * u] = lambda u=u: branch_product(u)

                def add_half(b):
                    used(3 if b == 0 else 1)
                    add_x(b)

                for b in range(2):
                    due[38 + b] = lambda b=b: add_half(b)

                root()
                attention, convolution = side(), taps()
                for s in range(40):
                    splits(1)
                    if s in due:
                        due[s]()
                    for _ in range(PLAN2.get(s, 0)):
                        next(attention)
                    if s >= TAPS_FROM:
                        for _ in range(TAPS_EACH):
                            next(convolution, None)
                assert next(attention, None) is None and next(convolution, None) is None
                mean_x()
                for g in range(4):
                    take_model((2 * g, 2 * g + 1), l * 16 + 40)
                def up():
                    used(2)
                    a = block_of()
                    dve.wait_ge(act_done, q.next("act_done"))
                    for r in range(R):
                        ins = dve.scalar_tensor_tensor(hid2[:, r, :], a[r][:, :], rstd[r], relu[r][:, :],
                                                       ALU.mult, ALU.mult)
                    ins.then_inc(acc_free, 1)

                splits(2)
                root()
                hold(dve)
                for i in q.rounds(3, dict(loop4, turn=4, turn_hi=4, act_done=2)):
                    for j in range(2):
                        up()
                        split_lo()
                        split_lo()
                        for g in range(2):
                            at = i * 8 + 4 * j + 2 * g
                            take_lo(hid2T_lo[:, bass.ds(at, 2), :], hid2T_hi[:, bass.ds(at, 2), :])
                for _ in range(12):
                    next(ahead)
                up()
                splits(2)
                for at in (24, 26):
                    take_lo(hid2T_lo[:, at:at + 2, :], hid2T_hi[:, at:at + 2, :])
                up()
                for at in (28, 30):
                    take_lo(hid2T_lo[:, at:at + 2, :], hid2T_hi[:, at:at + 2, :])
                splits(10)
                used(8)
                add_x(0)
                for g in range(2):
                    take_model((2 * g, 2 * g + 1), l * 16 + 48)
                splits(6)
                used(8)
                a = block_of()
                for r in range(R):
                    ins = dve.tensor_tensor(x[:, r, NB:D], x[:, r, NB:D], a[r][:, :], ALU.add)
                ins.then_inc(acc_free, 2)
                q.next("blk")
                mean_x()
                take_model((4, 5), l * 16 + 48)
                take_model((6, 7), l * 16 + 48, skip=1)
            root()
            dve.wait_ge(x_in, 32)
            for r in range(R):
                ins = dve.scalar_tensor_tensor(outrow[:, r, :], x[:, r, :], rstd[r], gfin[:, :], ALU.mult, ALU.mult)
            ins.then_inc(out_ready, 1)

        @block.gpsimd
        def _(pool):
            q = Place(pool)
            half = cst[:, C_NEG:C_NEG + 32]

            def root(dst, src, n):
                pool.wait_ge(mean_ready, q.next("mean"))
                pool.tensor_tensor(dst, src, half[:, 0:n], ALU.pow).then_inc(rstd_ready, 1)

            def root_x():
                root(stat[:, S_XR:S_XR + 2], stat[:, S_XM:S_XM + 2], 2)

            def step(ins):
                ins.then_inc(pool_step, 1)
                pool.wait_ge(pool_step, q.next("step"))

            pool.wait_ge(consts_in, 16)
            root_x()
            pool.wait_ge(pool_job, q.next("pool_job"))
            q.next("act_done", 3)
            for l in q.rounds(DEPTH, dict(mean=5, pool_job=1, act_done=12, scores=16, decay=RH, blk=BLOCKS1,
                                          step=STEPS_POOL1)):
                q.next("blk", 7)

                def exponent(h):
                    if h >= 2:
                        pool.wait_ge(scores_out, q.next("scores") + 2)
                    hold(pool)
                    pool.tensor_tensor(decay[:, h % 2, :], cst[:, C_DF:C_DF + 512],
                                       small[:, bass.ds(l * 8 + B_DF + h, 1)].to_broadcast([P, 512]), ALU.mult)
                    step(pool.tensor_tensor(pooltmp[:, :], cst[:, C_DB:C_DB + 512],
                                            small[:, bass.ds(l * 8 + B_DB + h, 1)].to_broadcast([P, 512]), ALU.mult))
                    pool.tensor_tensor(decay[:, h % 2, :], decay[:, h % 2, :], pooltmp[:, :],
                                       ALU.add).then_inc(decay_arg, 1)
                    pool.wait_ge(decay_arg, q.next("decay"))

                pool.wait_ge(acc_free, q.now("blk") + 2)
                exponent(0)
                exponent(1)
                root(stat[:, S_QR:S_QR + 32], stat[:, S_Q:S_Q + 32], 32)
                pool.wait_ge(pool_job, q.next("pool_job"))
                hold(pool)
                for r in range(R):
                    for at, g in ((DQ, B_QG), (DK, B_KG)):
                        v = proj1[:, r, at:at + 512].rearrange("p (h d) -> p h d", d=HD)
                        ins = pool.tensor_tensor(v, v, small[:, bass.ds(l * HD + g, HD)].unsqueeze(1)
                                                 .to_broadcast([P, 8, HD]), ALU.mult)
                ins.then_inc(pool_ready, 1)
                for h in range(2, RH):
                    exponent(h)
                q.next("scores", 2)
                pool.wait_ge(act_done, q.next("act_done"))
                hold(pool)
                for r in range(R):
                    v = proj1[:, r, RG:RG + RETW].rearrange("p (h d) -> p h d", d=HD)
                    ins = pool.tensor_tensor(v, v, small[:, bass.ds(l * HD + B_RG, HD)].unsqueeze(1)
                                             .to_broadcast([P, RH, HD]), ALU.mult)
                step(ins)
                root(stat[:, S_OR:S_OR + 16], stat[:, S_O:S_O + 16], 16)
                pool.wait_ge(acc_free, q.next("blk") + 2)
                pool.tensor_tensor(mixed1[:, :, 0:NB], mixed1[:, :, 0:NB], proj1[:, :, RG:RG + RETW],
                                   ALU.mult).then_inc(pool_ready, 1)
                root(stat[:, S_PR:S_PR + 8], stat[:, S_P:S_P + 8], 8)
                pool.wait_ge(acc_free, q.next("blk") + 2)
                hold(pool)
                for r in range(R):
                    v = mixed1[:, r, NB:D].rearrange("p (h d) -> p h d", d=DVD)
                    ins = pool.tensor_tensor(v, v, small[:, bass.ds(l * DVD + B_DG, DVD)].unsqueeze(1)
                                             .to_broadcast([P, DH, DVD]), ALU.mult)
                ins.then_inc(pool_ready, 1)
                root_x()
                root_x()
                q.next("act_done", 11)
                q.next("scores", 8)
                q.next("blk", BLOCKS1 - 9)
            for l in q.rounds(DEPTH, dict(mean=4, blk=BLOCKS2, step=STEPS_POOL2)):
                pool.wait_ge(acc_free, q.next("blk", 5) + 2)
                hold(pool)
                for r in range(R):
                    pool.tensor_copy(cqa[:, r, :, 0:HD], p_c[:, r, CQ - KL:CQ - KL + 256].rearrange("p (h d) -> p h d", d=HD))
                    ins = pool.tensor_copy(cka[:, r, :, 0:HD], p_c[:, r, CK - KL:CK - KL + 256].rearrange("p (h d) -> p h d", d=HD))
                ins.then_inc(pool_ready, 1)
                root(stat[:, S_LR:S_LR + 4], stat[:, S_L:S_L + 4], 4)
                def rotate(r, a, b, da, db, spread):
                    cos, sin = (rope[:, n, r, :] if not spread else
                                rope[:, n, r, :].unsqueeze(1).to_broadcast([P, 4, 16]) for n in range(2))
                    tmp = [ropetmp[:, n, 0:64].rearrange("p (h d) -> p h d", h=4) if spread else ropetmp[:, n, 0:16]
                           for n in range(4)]
                    for n, (u, v) in enumerate(((a, cos), (b, sin), (b, cos), (a, sin))):
                        step(pool.tensor_tensor(tmp[n], u, v, ALU.mult))
                    step(pool.tensor_tensor(da, tmp[0], tmp[1], ALU.subtract))
                    step(pool.tensor_tensor(db, tmp[2], tmp[3], ALU.add))

                for r in range(R):
                    a, b = p_c[:, r, P:P + 16], p_c[:, r, P + 16:P + 32]
                    rotate(r, a, b, a, b, False)
                pool.wait_ge(acc_free, q.next("blk", 2) + 2)
                for r in range(R):
                    a, b = qB[:, r, :, 64:80], qB[:, r, :, 80:96]
                    rotate(r, a, b, a, b, True)
                    hold(pool)
                    pool.tensor_copy(kB[:, r, :, 0:64], kvB[:, r, :].rearrange("p (h d) -> p h d", d=P)[:, :, 0:64])
                    ins = pool.tensor_copy(kB[:, r, :, 64:96], p_c[:, r, P:P + 32].unsqueeze(1)
                                           .to_broadcast([P, 4, 32]))
                ins.then_inc(pool_ready, 1)
                root(stat[:, S_VR:S_VR + 2], stat[:, S_VR:S_VR + 2], 2)
                root_x()
                root_x()
                q.next("blk", BLOCKS2 - 7)


_NAMES = [
    "x", "attn_norm_g", "w_in", "ret_decay_fwd", "ret_decay_bwd", "ret_norm_g", "dq_norm_g", "dk_norm_g",
    "lambda_q1", "lambda_k1", "lambda_q2", "lambda_k2", "diff_norm_g", "w_out", "ffn_norm_g", "w_gate", "w_up",
    "w_down", "positions_2", "g_mix_2", "w_in_2", "w_gate_2", "b_gate_2", "g_q_lat_2", "w_uq_2",
    "g_kv_lat_2", "w_ukv_2", "b_forget_2", "w_dw_2", "b_dw_2", "g_conv_ln_2", "b_conv_ln_2", "w_branch_2",
    "w_o_2", "g_ffn_2", "w_up_2", "w_down_2", "g_final_2"]


def kernel(**inputs):
    import concourse.bacc as bacc
    from concourse.bass_utils import run_bass_kernel_spmd

    nc = bacc.Bacc("TRN2", target_bir_lowering=False, num_devices=1)
    arrays = {name: np.ascontiguousarray(inputs[name]) for name in _NAMES}
    arrays["consts"] = shape_constants()
    falling = 2 * 128 - np.maximum(np.arange(384) - 127, 0)
    arrays["rel_ext"] = np.ascontiguousarray(inputs["rel_bias_2"][:, :, falling])
    t = {name: nc.dram_tensor(f"in_{name}", a.shape, mybir.dt.from_np(a.dtype), kind="ExternalInput").ap()
         for name, a in arrays.items()}
    out = nc.dram_tensor("out", (1, SEQ, D), F32, kind="ExternalOutput").ap()
    build(nc, t, out)
    r = run_bass_kernel_spmd(nc, [{f"in_{name}": a for name, a in arrays.items()}], core_ids=[0])
    return r.results[0]["out"]
```

```python
from contextlib import ExitStack

import numpy as np
import concourse.bass as bass
from concourse import mybir

F32 = mybir.dt.float32
F32R = mybir.dt.float32r
I32 = mybir.dt.int32
ALU = mybir.AluOpType
ACT = mybir.ActivationFunctionType
AX = mybir.AxisListType

P = 128
SEQ = 256
R = SEQ // P
D = 1024
KT = D // P
DEPTH = 2
EPS = 1e-6
NB = 512
RING = 4
AHEAD = 3

RETW, HD = 512, 64
RH = RETW // HD
DH, DVD = 4, 128
PROJ1 = 4 * RETW + 3 * 512
RQ, RK, RV, RG, DQ, DK, DV = (i * 512 for i in range(7))
FF1 = 2816
HALF = NB // 2
PROJ2 = 2468
AQ, AK, AV, QL, KL, KR, CQ, CK, CV, CF, DVAL, DGATE = (
    0, 256, 512, 768, 1024, 1152, 1184, 1440, 1696, 1952, 1956, 2212)
NBR, BW = 4, 256
FF2 = 4096
TAPS = 31
BQD = 96
CAD = 66
MASKED = -1e30

KTS1 = [4] * 14 + [4] * 4 + [4] * 22 + [4, 4, 4, 4, 4, 2] * 2
assert len(KTS1) % RING == 0
BLOCKS1, BLOCKS2 = 7 + 2 + 11 + 2, 5 + 2 + 16 + 2 + 8 + 2 + 1
TURNS1, TURNS2 = 4 + 4 + 4 + 4 + 4 + 4 + 4 + 11 + 4 + 1, 2 + 1 + 2 + 1 + 10 + 12 + 4 + 1 + 4 + 4 + 16 + 4 + 1
assert not (BLOCKS1 % 2 or BLOCKS2 % 2 or TURNS1 % 2 or TURNS2 % 2)

COLS2 = ((DVAL, 512), (AQ, 512), (AV, 512), (KL, 512), (KL + 512, DVAL - KL - 512))
ORDER = (0, 2, 1, 3)
OUT_OF = (0, 0, 1, 0)
PRODUCTS = ("G0", "U0", "U1", "G1", "B0", "G2", "B1", "G3", "B2", "G4", "B3", "G5", "B4", "G6", "B5", "B6", "G7", "B7")
KTS2 = [4] * 2 * len(COLS2)
for name in PRODUCTS:
    KTS2 += {"G": [4, 4], "B": [2]}.get(name[0], [1 if name == "U1" else 2])
KTS2 += [4] * (4 + 16 + 16)
assert len(KTS2) % RING == 0
PLAN2 = {2: 1, 3: 1, 4: 1, 5: 1, 6: 1, 7: 1, 8: 2, 9: 1, 10: 1, 11: 1, 12: 1, 13: 1, 14: 1, 15: 1,
         17: 1, 18: 1, 19: 1, 20: 1, 21: 1, 23: 1, 24: 1, 26: 2, 27: 1, 29: 1, 33: 1, 36: 1}
TAPS_FROM, TAPS_EACH = 4, 3
COLS1 = (DQ, DK, DV, RQ, RK, RV, RG)
PLAN1 = {2: 1, 4: 1, 5: 1, 6: 1, 7: 1, 8: 1, 9: 1, 10: 1, 11: 1, 12: 1, 13: 1, 14: 1, 15: 1}

C_ID, C_TRI, C_ANTI, C_DF, C_DB, C_DA = 0, 128, 256, 384, 896, 1408
C_MCH, C_MCA, C_INV, C_NEG, C_LI, C_OML, C_ONE = 1920, 2304, 2688, 2704, 2736, 2738, 2740
C_W = 2740 + 128


def shape_constants():
    c = np.zeros((P, C_W), np.float32)
    p = np.arange(P)
    c[:, C_ID:C_ID + P] = np.eye(P)
    c[:, C_TRI:C_TRI + P] = p[:, None] <= p[None, :]
    c[:, C_ANTI:C_ANTI + P] = np.eye(P)[::-1]
    t = np.arange(SEQ)
    for s in range(R):
        d = t[None, :] - (s * P + p)[:, None]
        c[:, C_DF + s * SEQ:C_DF + (s + 1) * SEQ] = np.maximum(d, 0)
        c[:, C_DB + s * SEQ:C_DB + (s + 1) * SEQ] = np.maximum(-d, 0)
        c[:, C_DA + s * SEQ:C_DA + (s + 1) * SEQ] = np.abs(d)
    for at, unit in ((C_MCH, 64), (C_MCA, 1)):
        k = np.arange(P)
        c[:, at:at + P] = np.where(k[None, :] // unit <= p[:, None] // unit, 0.0, MASKED)
        q = P + p
        c[:, at + P:at + P + SEQ] = np.where(t[None, :] // unit <= q[:, None] // unit, 0.0, MASKED)
    c[:, C_INV:C_INV + 16] = 1.0 / (np.float32(10000.0) ** (np.arange(16, dtype=np.float32) / np.float32(16)))
    c[:, C_NEG:C_NEG + 32] = -0.5
    for l in range(DEPTH):
        li = 0.8 - 0.6 * np.exp(-0.3 * l)
        c[:, C_LI + l] = li
        c[:, C_OML + l] = 1.0 - li
    c[:, C_ONE:C_ONE + P] = 1.0
    return c


S_X, S_XM, S_XR = 0, 4, 6
S_Q, S_QR = 8, 40
S_NM, S_RS, S_RC = 72, 80, 88
S_O, S_OR, S_P, S_PR = 96, 112, 128, 136
S_L, S_LR = 144, 148
S_Z, S_M, S_A, S_LF = 152, 160, 168, 176
S_NM2, S_RS2, S_RC2 = 184, 188, 212
S_BN, S_MV, S_VR = 236, 248, 252
STEPS_ACT1, STEPS_ACT2 = 4, 8
STEPS_DVE1, STEPS_DVE2 = 28, 85
STEPS_POOL1, STEPS_POOL2 = 11, 24
GAIN_LOADS, SMALL_LOADS = 9, 6 + 7 + 4 + 2

B_RG, B_DG, B_QG, B_KG = 0, 128, 384, 512
B_DF, B_DB, B_FB = 640, 656, 672
B_W = 680


class Place:

    def __init__(self, e):
        self.e, self.base, self.k = e, {}, {}

    def now(self, name):
        return self.base.get(name, 0) + self.k.get(name, 0)

    def next(self, name, n=1):
        self.k[name] = self.k.get(name, 0) + n
        return self.now(name)

    def index(self, name):
        return self.k.get(name, 0)

    def rounds(self, n, per):
        base, k = dict(self.base), dict(self.k)
        with self.e.Fori(0, n) as i:
            for name, by in per.items():
                self.base[name] = i * by + base.get(name, 0)
            yield i
            grown = {x: self.k[x] - k.get(x, 0) for x in self.k if self.k[x] != k.get(x, 0)}
            assert grown == {x: y for x, y in per.items() if y}, (self.e, grown, per)
        self.base = base
        self.k = {x: k.get(x, 0) + n * per.get(x, 0) for x in {*k, *per}}


def bcast(row, at, n):
    return bass.AP(row.tensor, at, [[0, P], [1, n]])


def build(nc, t, out):
    with ExitStack() as ctx:
        def sb(name, shape, dt=F32):
            return ctx.enter_context(nc.sbuf_tensor(name, shape, dt))

        def sem(name):
            return ctx.enter_context(nc.semaphore(name))

        w_raw = sb("w_raw", [P, RING, 4, NB])
        w_hi = sb("w_hi", [P, RING, 4, NB], F32R)
        w_lo = sb("w_lo", [P, RING, 4, NB], F32R)
        x = sb("x", [P, R, D])
        hT_hi = sb("hT_hi", [P, KT, SEQ], F32R)
        hT_lo = sb("hT_lo", [P, KT, SEQ], F32R)
        cst = sb("cst", [P, C_W])
        small = sb("small", [P, B_W])
        gcols = sb("gcols", [P, 72])
        ccols = sb("ccols", [P, DEPTH * 65])
        rope = sb("rope", [P, 2, R, 16])
        stat = sb("stat", [P, 256])
        lam = sb("lam", [P, 4])

        arena_bytes = 68 * 1024
        base_at = -(-nc.sbuf_base // 32) * 32
        arena = sb("arena", [P, arena_bytes // 4 + 8])

        def over(name, shape, kb, dt=F32):
            n = 4
            for s in shape[1:]:
                n *= s
            at = int(kb * 1024)
            assert at + n <= arena_bytes, (name, at + n)
            return nc.alloc_sbuf_tensor_at(name, shape, dt, offset=base_at + at)

        proj1 = over("proj1", [P, R, PROJ1], 0)
        sq1 = proj1[:, :, RV:RV + D]
        qkT1 = over("qkT1", [P, 4, 512], 28)
        decay01 = over("decay01", [P, 2, R * SEQ], 36)
        ret_p = over("ret_p", [P, 2, R * SEQ], 40)
        soft1 = over("soft1", [P, 2, 2, R * SEQ], 44)
        decay25 = over("decay25", [P, 4, R * SEQ], 44)
        comb1 = over("comb1", [P, 2, R, SEQ], 52)
        sqo = over("sqo", [P, R, NB], 52)
        combT1 = over("combT1", [P, 2, R, SEQ], 56)
        mixed1 = over("mixed1", [P, R, D], 60)
        decay = [decay01[:, h % 6] if h % 6 < 2 else decay25[:, h - 2] for h in range(RH)]
        hid1T_hi = over("hid1T_hi", [P, FF1 // P, SEQ], 0, F32R)
        hid1T_lo = over("hid1T_lo", [P, FF1 // P, SEQ], 22, F32R)
        gate1 = over("gate1", [P, R, HALF], 44)
        hid1 = over("hid1", [P, R, HALF], 46)
        p_conv = over("p_conv", [P, R, 512], 0)
        p_a = over("p_a", [P, R, 512], 4)
        gate2 = over("gate2", [P, 2, R, NB], 0)
        p_b = over("p_b", [P, R, 512], 8)
        term2 = over("term2", [P, R, NB], 8)
        p_c = over("p_c", [P, R, DVAL - KL], 12)
        lat_hi = over("lat_hi", [P, 3, SEQ], 19.5, F32R)
        lat_lo = over("lat_lo", [P, 3, SEQ], 22.5, F32R)
        mix2 = over("mix2", [P, R, D], 19.5)
        obT_hi, obT_lo = ([over(f"obT_{part}{n}", [P, 2, SEQ], at + kb, F32R) for n, at in enumerate((27.5, 12))]
                          for part, kb in (("hi", 0), ("lo", 2)))
        branch = over("branch", [P, R, BW], 31.5)
        bgate = over("bgate", [P, 2, NB], 33.5)
        qkT2 = over("qkT2", [P, 3, 512], 37.5)
        soft2 = over("soft2", [P, 2, 384], 43.5)
        softT2 = over("softT2", [P, 2, 384], 46.5)
        abias = over("abias", [P, 4, 384], 49.5)
        qB = over("qB", [P, R, 4, BQD], 49.5)
        kB = over("kB", [P, R, 4, BQD], 52.5)
        kvB = over("kvB", [P, R, 512], 55.5)
        hankel = over("hankel", [P, 4, SEQ], 55.5)
        cqa = over("cqa", [P, R, 4, CAD], 59.5)
        cka = over("cka", [P, R, 4, CAD], 61.5625)
        uT = over("uT", [P, 2, SEQ + TAPS - 1], 63.625)
        yT = over("yT", [P, 2, SEQ], 65.9375)
        convrow = cst[:, C_DF:C_DF + 768].rearrange("p (n c) -> p n c", n=3)
        ropetmp = cst[:, C_DF + 768:C_DF + 1024].rearrange("p (n c) -> p n c", n=4)
        hid2T_hi = over("hid2T_hi", [P, FF2 // P, SEQ], 0, F32R)
        hid2T_lo = over("hid2T_lo", [P, FF2 // P, SEQ], 32, F32R)
        hid2 = over("hid2", [P, R, NB], 64)
        grows = over("grows", [72, P], 0)
        crows = over("crows", [P, DEPTH, P], 1)
        lrows = over("lrows", [P, 4, DEPTH * HD], 3)
        lprod = over("lprod", [P, 2, DEPTH * HD], 5)
        pos_i = over("pos_i", [P, R], 7, I32)
        ropet = over("ropet", [P, 6, R, 16], 8)
        gfin = over("gfin", [P, D], 64)
        outrow = over("outrow", [P, R, D], 32)

        ident = cst[:, C_ID:C_ID + P]
        junk = sb("junk", [P, NB])
        relu = [junk, cst[:, C_DB:C_DB + NB]]

        bank = [ctx.enter_context(nc.psum_tensor(f"bank{i}", [P, NB], F32)) for i in range(8)]
        acc, turn, score = [bank[0:2], bank[2:4]], bank[4:6], bank[6:8]

        ident_in = sem("ident_in")
        consts_in = sem("consts_in")
        gains_in = sem("gains_in")
        small_in = sem("small_in")
        x_in = sem("x_in")
        slab_in = [sem(f"slab_in{i}") for i in range(RING)]
        hi_ready = sem("hi_ready")
        lo_ready = sem("lo_ready")
        slab_used = sem("slab_used")
        acc_free = sem("acc_free")
        turned = sem("turned")
        turn_hi = sem("turn_hi")
        turn_free = sem("turn_free")
        scores = sem("scores")
        scores_out = sem("scores_out")
        soft_ready = sem("soft_ready")
        probs = sem("probs")
        heads_out = sem("heads_out")
        decay_arg = sem("decay_arg")
        decay_ready = sem("decay_ready")
        squares = sem("squares")
        mean_ready = sem("mean_ready")
        rstd_ready = sem("rstd_ready")
        out_free = sem("out_free")
        act_done = sem("act_done")
        dve_ready = sem("dve_ready")
        pool_ready = sem("pool_ready")
        pool_job = sem("pool_job")
        conv_in = sem("conv_in")
        outputs_in = sem("outputs_in")
        act_job = sem("act_job")
        conv_out = sem("conv_out")
        act_step = sem("act_step")
        dve_step = sem("dve_step")
        pool_step = sem("pool_step")
        held = sem("held")
        layer_in = sem("layer_in")
        bgate_in = [sem(f"bgate_in{i}") for i in range(2)]
        out_ready = sem("out_ready")
        out_done = sem("out_done")
        block = ctx.enter_context(nc.Block())

        def hold(e):
            e.sem_inc(held, 1)

        def rows_of(r):
            return slice(r * P, (r + 1) * P)

        @block.sync
        def _(sp):
            q = Place(sp)
            sp.dma_start(ident, t["consts"][:, C_ID:C_ID + P]).then_inc(ident_in, 16)
            sp.dma_start(x[:, :, :], t["x"].rearrange("b (r p) d -> p (b r) d", p=P)).then_inc(x_in, 16)

            def slab(*parts):
                assert len(parts) == 2
                sp.wait_ge(lo_ready, q.next("slab"))
                hold(sp)
                for dst, src in parts:
                    s = (q.index("slab") - 1) % RING
                    sp.dma_start(dst(w_raw[:, s]), src).then_inc(slab_in[s], 16)

            def rows(w, k0, n, c0, cols):
                def part(a, b):
                    src = w[(k0 + a) * P:(k0 + b) * P, bass.ds(c0, cols)]
                    return lambda s: s[:, a:b, 0:cols], src.rearrange("(c p) n -> p c n", p=P)
                if n == 1:
                    h = cols // 2
                    src = w[k0 * P:(k0 + 1) * P, :]
                    return [(lambda s: s[:, 0, 0:h], src[:, c0:c0 + h]),
                            (lambda s: s[:, 0, h:cols], src[:, c0 + h:c0 + cols])]
                return [part(0, n // 2), part(n // 2, n)]

            def halves(w, k0, c0):
                src = w[k0 * P:(k0 + 4) * P, bass.ds(c0, HALF)]
                return src.rearrange("(c p) n -> p c n", p=P)

            for l in q.rounds(DEPTH, dict(slab=len(KTS1))):
                w = {n: t[n][bass.ds(l, 1)].rearrange("o k n -> (o k) n")
                     for n in ("w_in", "w_out", "w_gate", "w_up", "w_down")}
                for c0 in COLS1:
                    for k0 in (0, 4):
                        slab(*rows(w["w_in"], k0, 4, c0, NB))
                for k0 in (4, 0):
                    for b in range(2):
                        slab(*rows(w["w_out"], k0, 4, b * NB, NB))

                def gate_up(c0):
                    for k0 in (0, 4):
                        slab((lambda s: s[:, :, 0:HALF], halves(w["w_gate"], k0, c0)),
                             (lambda s: s[:, :, HALF:NB], halves(w["w_up"], k0, c0)))

                gate_up(0)
                for i in q.rounds(5, dict(slab=4)):
                    gate_up(i * (2 * HALF) + HALF)
                    gate_up(i * (2 * HALF) + 2 * HALF)
                for b in range(2):
                    for k0 in range(0, 22, 4):
                        slab(*rows(w["w_down"], k0, min(4, 22 - k0), b * NB, NB))

            for l in q.rounds(DEPTH, dict(slab=len(KTS2))):
                w = {n: t[n + "_2"][bass.ds(l, 1)].rearrange("o k n -> (o k) n")
                     for n in ("w_in", "w_gate", "w_uq", "w_ukv", "w_o", "w_up", "w_down")}
                w["w_branch"] = t["w_branch_2"][bass.ds(l, 1)].rearrange("o b k n -> (o b k) n")
                for n, (c0, cols) in enumerate(COLS2):
                    if n == 4:
                        sp.dma_start(hankel[:, :, :], bass.AP(
                            t["rel_ext"].tensor, l * (4 * 384), [[1, P], [384, 4], [1, SEQ]])).then_inc(layer_in, 16)
                        for row, name in enumerate(("b_dw_2", "g_conv_ln_2", "b_conv_ln_2")):
                            sp.dma_start(convrow[:, row, :], bcast(t[name], l * 256, 256)).then_inc(layer_in, 16)
                    for k0 in (0, 4):
                        slab(*rows(w["w_in"], k0, 4, c0, cols))
                for name in PRODUCTS:
                    if name == "U0":
                        slab(*rows(w["w_uq"], 0, 2, 0, 384))
                    elif name == "U1":
                        slab(*rows(w["w_ukv"], 0, 1, 0, 512))
                    else:
                        n, b = ORDER[int(name[1]) // 2], int(name[1]) % 2
                        if name[0] == "G":
                            for k0 in (0, 4):
                                slab(*rows(w["w_gate"], k0, 4, n * D + b * NB, NB))
                        else:
                            slab(*rows(w["w_branch"], 2 * n, 2, b * NB, NB))
                for k0 in (0, 4):
                    for b in range(2):
                        slab(*rows(w["w_o"], k0, 4, b * NB, NB))
                for i in q.rounds(4, dict(slab=4)):
                    for b in range(2):
                        for k0 in (0, 4):
                            slab(*rows(w["w_up"], k0, 4, i * (2 * NB) + b * NB, NB))
                for b in range(2):
                    for k0 in range(0, 32, 4):
                        slab(*rows(w["w_down"], k0, 4, b * NB, NB))
            for s in range(AHEAD):
                sp.wait_ge(lo_ready, q.next("slab"))
                sp.sem_inc(slab_in[s], 32)
            sp.wait_ge(acc_free, 2 + DEPTH * BLOCKS1 + DEPTH * BLOCKS2 - 2)
            sp.dma_start(gfin[:, :], bcast(t["g_final_2"], 0, D)).then_inc(x_in, 16)
            sp.wait_ge(out_ready, 1)
            sp.dma_start(out.rearrange("b (r p) d -> p (b r) d", p=P), outrow[:, :, :]).then_inc(out_done, 16)
            sp.wait_ge(out_done, 16)

        @block.tensor
        def _(pe):
            q = Place(pe)
            pe.sem_inc(slab_used, RING)
            pe.wait_ge(ident_in, 16)

            def open_block():
                pe.wait_ge(acc_free, q.next("blk"))
                return acc[(q.index("blk") - 1) % 2]

            def read_out(blk):
                pe.wait_ge(acc_free, blk + 2)

            def slab_product(a, hi, lo, kts, cols, first, last, halfway=None):
                pe.wait_ge(lo_ready, q.next("slab") + RING)
                s = (q.index("slab") - 1) % RING
                for j, kt in enumerate(kts):
                    for r in range(R):
                        begin, end = first and j == 0, last and j == len(kts) - 1
                        o = a[r][:, 0:cols]
                        pe.matmul(o, hi[:, kt, rows_of(r)], w_hi[:, s, j, 0:cols], start=begin, stop=False)
                        pe.matmul(o, hi[:, kt, rows_of(r)], w_lo[:, s, j, 0:cols], start=False, stop=False)
                        mm = pe.matmul(o, lo[:, kt, rows_of(r)], w_hi[:, s, j, 0:cols], start=False, stop=end)
                    if j == 1 and halfway:
                        halfway()
                mm.then_inc(slab_used, 1)

            def wide_block(cols=NB):
                a = open_block()
                slab_product(a, hT_hi, hT_lo, range(0, 4), cols, True, False)
                slab_product(a, hT_hi, hT_lo, range(4, 8), cols, False, True)

            def turn_group(pieces, skip=0):
                pe.wait_ge(turn_free, q.next("turn"))
                b = turn[(q.index("turn") - 1) % 2]
                for src, col in pieces:
                    n, m = src.shape[0], src.shape[1]
                    tr = pe.transpose(b[0:m, col:col + n], src, ident[0:n, 0:n])
                tr.then_inc(turned, 1 + skip)
                q.next("turn", skip)
                return q.now("turn")

            def all_turned():
                pe.wait_ge(turn_free, q.now("turn") + 2)

            def turn_model(src, groups, skip=0):
                for g in groups:
                    turn_group([(src[:, r, kt * P:(kt + 1) * P], (kt % 2) * SEQ + r * P)
                                for kt in (2 * g, 2 * g + 1) for r in range(R)], skip if g == groups[-1] else 0)

            def turn_x(b, skip=0):
                turn_model(x, (2 * b, 2 * b + 1), skip)

            def turn_added(skip=0):
                read_out(q.now("blk") - 1)
                turn_x(0, skip)

            def first_block(product, cols=NB):
                all_turned()
                a, last = open_block(), q.now("blk") - 1

                def turn_rest():
                    read_out(last)
                    turn_x(1)

                product(a, hT_hi, hT_lo, range(0, 4), cols, True, False, turn_rest)
                all_turned()
                product(a, hT_hi, hT_lo, range(4, 8), cols, False, True)

            def turn_pair(qsrc, ksrc):
                return turn_group([(qsrc(0), 0), (qsrc(1), P), (ksrc(0), 2 * P), (ksrc(1), 3 * P)])

            def score_bank():
                pe.wait_ge(scores_out, q.next("scores"))
                return score[(q.index("scores") - 1) % 2]

            pe.wait_ge(gains_in, 16 * GAIN_LOADS)
            turn_group([(grows[:, :], 0)])
            pe.wait_ge(x_in, 16)
            turn_x(0)
            pe.wait_ge(small_in, 16 * SMALL_LOADS)
            turn_group([(crows[0:65, l, :], l * 65) for l in range(DEPTH)])

            for l in q.rounds(DEPTH, dict(slab=len(KTS1), blk=BLOCKS1, turn=TURNS1, scores=16, pool=2, dve=7)):
                projection = [q.now("blk") + n for n in range(len(COLS1) + 1)]
                group, item = {}, {}

                def diff_scores(h):
                    for m in range(2):
                        b = score_bank()
                        pe.wait_ge(turn_free, group["diff", h] + 2)
                        for r in range(R):
                            mm = pe.matmul(b[:, r * SEQ:(r + 1) * SEQ], qkT1[64 * m:64 * m + 64, h, rows_of(r)],
                                           qkT1[64 * m:64 * m + 64, h, SEQ:2 * SEQ], start=True, stop=True)
                        mm.then_inc(scores, 1)

                def turn_combined(h):
                    pe.wait_ge(dve_ready, q.next("dve"))
                    group["comb", h] = turn_group([(comb1[:, h % 2, r, kt * P:(kt + 1) * P], kt * SEQ + r * P)
                                                   for kt in range(R) for r in range(R)])

                def diff_values(h):
                    pe.wait_ge(turn_free, group["comb", h] + 2)
                    if h == 0:
                        read_out(projection[3])
                    pe.wait_ge(turn_free, q.next("turn"))
                    o = turn[(q.index("turn") - 1) % 2]
                    for r in range(R):
                        for kt in range(R):
                            mm = pe.matmul(o[:, r * P:(r + 1) * P], combT1[:, h % 2, kt, rows_of(r)],
                                           proj1[:, kt, DV + h * DVD:DV + (h + 1) * DVD],
                                           start=kt == 0, stop=kt == R - 1)
                    mm.then_inc(turned, 1)

                def ret_scores(h):
                    b, e, j = score_bank(), h % 2, h // 2
                    pe.wait_ge(turn_free, group["ret", j] + 2)
                    for st in range(R):
                        mm = pe.matmul(b[:, st * SEQ:(st + 1) * SEQ],
                                       qkT1[64 * e:64 * e + 64, j, SEQ + st * P:SEQ + (st + 1) * P],
                                       qkT1[64 * e:64 * e + 64, j, 0:SEQ], start=True, stop=True)
                    mm.then_inc(scores, 1)
                    item[h] = q.now("scores")

                def ret_values(j):
                    if j == 0:
                        read_out(projection[6])
                    pe.wait_ge(turn_free, q.next("turn"))
                    o = turn[(q.index("turn") - 1) % 2]
                    for e in range(2):
                        h = 2 * j + e
                        pe.wait_ge(scores_out, item[h] + 2)
                        for r in range(R):
                            for st in range(R):
                                mm = pe.matmul(o[:, r * P + e * HD:r * P + (e + 1) * HD],
                                               ret_p[:, e, st * SEQ + r * P:st * SEQ + (r + 1) * P],
                                               proj1[:, st, RV + h * HD:RV + (h + 1) * HD],
                                               start=st == 0, stop=st == R - 1)
                    mm.then_inc(turned, 1)

                def side():
                    yield
                    yield
                    pe.wait_ge(pool_ready, q.next("pool"))
                    pe.wait_ge(dve_ready, q.next("dve"))
                    for h in range(DH):
                        group["diff", h] = turn_pair(lambda r: proj1[:, r, DQ + h * P:DQ + (h + 1) * P],
                                                     lambda r: proj1[:, r, DK + h * P:DK + (h + 1) * P])
                    yield
                    for h in range(DH + 3):
                        if h < DH:
                            diff_scores(h)
                        if 2 <= h < DH + 2:
                            turn_combined(h - 2)
                        if h >= 3:
                            diff_values(h - 3)
                        if h == DH:
                            read_out(projection[5])
                            for j in range(RH // 2):
                                group["ret", j] = turn_pair(lambda r: proj1[:, r, RQ + j * P:RQ + (j + 1) * P],
                                                            lambda r: proj1[:, r, RK + j * P:RK + (j + 1) * P])
                        if h == DH + 2:
                            ret_values(0)
                        if h > DH:
                            for e in range(2):
                                ret_scores(2 * (h - DH - 1) + e)
                        yield
                    for j in range(1, RH // 2):
                        if j == 3:
                            pe.wait_ge(dve_ready, q.next("dve"))
                            turn_model(mixed1, (0,))
                        ret_values(j)
                        if j < 3:
                            ret_scores(2 * j + 2)
                            ret_scores(2 * j + 3)
                        if j == 1:
                            pe.wait_ge(pool_ready, q.next("pool"))
                            turn_model(mixed1, (2, 3))
                        if j == 3:
                            pe.wait_ge(dve_ready, q.next("dve"))
                            turn_model(mixed1, (1,))
                        yield

                attention, slabs = side(), iter(range(18))

                def product(*args):
                    slab_product(*args)
                    for _ in range(PLAN1.get(next(slabs), 0)):
                        next(attention)

                first_block(product)
                for _ in COLS1[1:]:
                    a = open_block()
                    product(a, hT_hi, hT_lo, range(0, 4), NB, True, False)
                    product(a, hT_hi, hT_lo, range(4, 8), NB, False, True)
                a = []
                for k0 in (4, 0):
                    all_turned()
                    for b in range(2):
                        if k0 == 4:
                            a.append(open_block())
                        product(a[b], hT_hi, hT_lo, range(4 - k0, 8 - k0), NB, k0 == 4, k0 == 0,
                                turn_added if (k0, b) == (0, 1) else None)
                assert next(attention, None) is None and next(slabs, None) is None
                def turn_hid1(blk):
                    read_out(blk)
                    turn_group([(hid1[:, r, c * P:(c + 1) * P], c * SEQ + r * P)
                                for c in range(2) for r in range(R)])

                first_block(slab_product)
                for _i in q.rounds(5, dict(slab=4, blk=2, turn=2)):
                    for _ in range(2):
                        wide_block()
                        turn_hid1(q.now("blk") - 1)
                all_turned()
                last = q.now("blk")
                for b in range(2):
                    a = open_block()
                    for n in range(6):
                        kts = range(4 * n, min(4 * n + 4, FF1 // P))
                        if (b, n) == (0, 5):
                            all_turned()
                        slab_product(a, hid1T_hi, hid1T_lo, kts, NB, n == 0, n == 5)
                        if (b, n) == (0, 0):
                            turn_hid1(last)
                        if b == 1 and n == 1:
                            turn_added(skip=1)
            pe.wait_ge(consts_in, 16)
            q.next("probs", DEPTH * DH)
            for l in q.rounds(DEPTH, dict(slab=len(KTS2), blk=BLOCKS2, turn=TURNS2, scores=12, pool=2, dve=6,
                                          layer_in=64, probs=12, conv=1, out=3)):
                projection = [q.now("blk") + n for n in range(len(COLS2) + 3)]
                group = {}

                def turn_head(g):
                    if g < 2:
                        group[g] = turn_pair(lambda r: p_a[:, r, g * P:(g + 1) * P],
                                             lambda r: p_a[:, r, AK + g * P:AK + (g + 1) * P])
                    elif g < 6:
                        group[g] = turn_pair(lambda r: cqa[:, r, g - 2, :], lambda r: cka[:, r, g - 2, :])
                    else:
                        if g == 6:
                            pe.wait_ge(pool_ready, q.next("pool"))
                        group[g] = turn_pair(lambda r: qB[:, r, g - 6, :], lambda r: kB[:, r, g - 6, :])

                def head_scores(h):
                    g = h // 2 if h < 4 else h - 2
                    pe.wait_ge(scores_out, q.next("scores") + 1)
                    pe.wait_ge(turn_free, group[g] + 2)
                    at, d = (64 * (h % 2), HD) if h < 4 else (0, CAD) if h < 8 else (0, BQD)
                    b, s = score[0], qkT2[at:at + d, g % 3, :]
                    pe.matmul(b[:, 0:P], s[:, 0:P], s[:, 2 * P:3 * P], start=True, stop=True)
                    pe.matmul(b[:, P:3 * P], s[:, P:2 * P], s[:, 2 * P:4 * P], start=True, stop=True).then_inc(scores, 1)

                def turn_probs(h):
                    pe.wait_ge(probs, q.next("probs"))
                    s = soft2[:, h % 2, :]
                    group["probs", h] = turn_group([(s[:, k * P:(k + 1) * P], k * P) for k in range(3)])

                def head_values(h):
                    pe.wait_ge(turn_free, group["probs", h] + 2)
                    if h % 4 == 0:
                        pe.wait_ge(out_free, q.next("out"))
                    if h == 0:
                        read_out(projection[3])
                    s = softT2[:, h % 2, :]

                    def v(kt):
                        if h < 4:
                            return p_b[:, kt, h * HD:(h + 1) * HD]
                        if h < 8:
                            return p_c[:, kt, CV - KL + (h - 4) * HD:CV - KL + (h - 3) * HD]
                        return kvB[:, kt, (h - 8) * P + HD:(h - 7) * P]
                    o = [score[1][:, r * BW + (h % 4) * HD:r * BW + (h % 4 + 1) * HD] for r in range(R)]
                    pe.matmul(o[0], s[:, 0:P], v(0), start=True, stop=True)
                    pe.matmul(o[1], s[:, P:2 * P], v(0), start=True, stop=False)
                    mm = pe.matmul(o[1], s[:, 2 * P:3 * P], v(1), start=False, stop=True)
                    if h % 4 == 3:
                        mm.then_inc(heads_out, 1)

                def turn_branch(n):
                    pe.wait_ge(out_free, q.now("out") + 1)
                    group["branch", n] = turn_group([(branch[:, r, c * P:(c + 1) * P], c * SEQ + r * P)
                                for c in range(2) for r in range(R)])

                def heads(first, end):
                    for h in range(first, end + 2):
                        if h == 10:
                            turn_branch(1)
                        if h < end:
                            head_scores(h)
                            if 4 <= h < 10:
                                turn_head(h)
                        if first < h <= end:
                            turn_probs(h - 1)
                        if h >= first + 2:
                            head_values(h - 2)
                        if h == 3:
                            yield
                            read_out(projection[4])
                            turn_group([(p_b[:, r, QL - AV + kt * P:QL - AV + (kt + 1) * P], kt * SEQ + r * P)
                                        for kt in range(2) for r in range(R)])
                            turn_group([(p_c[:, r, 0:P], r * P) for r in range(R)])
                            group["latents"] = q.now("turn")
                        yield

                def side():
                    yield
                    pe.wait_ge(dve_ready, q.next("dve"))
                    turn_group([(p_conv[:, r, c * P:(c + 1) * P], c * SEQ + r * P) for c in range(2) for r in range(R)])
                    yield
                    pe.wait_ge(layer_in, q.next("layer_in", 64))
                    for g in range(2):
                        pe.wait_ge(turn_free, q.next("turn"))
                        for h in (2 * g, 2 * g + 1):
                            mm = pe.matmul(turn[(q.index("turn") - 1) % 2][:, (h % 2) * SEQ:(h % 2 + 1) * SEQ],
                                           cst[:, C_ANTI:C_ANTI + P], hankel[:, h, :], start=True, stop=True)
                        mm.then_inc(turned, 1)
                    read_out(projection[2])
                    turn_head(0)
                    turn_head(1)
                    yield
                    yield from heads(0, 4)
                    pe.wait_ge(dve_ready, q.next("dve"))
                    pe.wait_ge(turn_free, q.next("turn"))
                    b = turn[(q.index("turn") - 1) % 2]
                    logf = stat[:, S_LF:S_LF + 8].rearrange("p (r h) -> p r h", r=R)
                    tri, ones = cst[:, C_TRI:C_TRI + P], cst[:, C_ONE:C_ONE + P]
                    pe.matmul(b[:, 0:4], tri, logf[:, 0, :], start=True, stop=True)
                    pe.matmul(b[:, 4:8], ones, logf[:, 0, :], start=True, stop=False)
                    pe.matmul(b[:, 4:8], tri, logf[:, 1, :], start=False, stop=True).then_inc(turned, 1)
                    yield
                    turn_branch(0)
                    pe.wait_ge(pool_ready, q.next("pool"))
                    pe.wait_ge(dve_ready, q.next("dve"))
                    turn_head(2)
                    turn_head(3)
                    yield
                    yield from heads(4, 12)
                    turn_branch(2)
                    yield
                    pe.wait_ge(dve_ready, q.next("dve"))
                    turn_group([(yT[:, c, rows_of(r)], r * 256 + c * P) for r in range(R) for c in range(2)])
                    yield
                    yield
                    pe.wait_ge(conv_out, q.next("conv"))
                    turn_branch(3)
                    yield
                    for half in range(2):
                        pe.wait_ge(dve_ready, q.next("dve"))
                        turn_model(mix2, (2 * half, 2 * half + 1))
                        yield

                attention, slabs = side(), iter(range(40))

                def product(*args):
                    slab_product(*args)
                    for _ in range(PLAN2.get(next(slabs), 0)):
                        next(attention)

                def model_block(cols=NB):
                    a = open_block()
                    product(a, hT_hi, hT_lo, range(0, 4), cols, True, False)
                    product(a, hT_hi, hT_lo, range(4, 8), cols, False, True)

                first_block(product, COLS2[0][1])
                for _c0, cols in COLS2[1:]:
                    model_block(cols)
                for name in PRODUCTS:
                    n = int(name[1])
                    if name[0] == "G":
                        model_block()
                    elif name[0] == "U":
                        pe.wait_ge(turn_free, group["latents"] + 2)
                        product(open_block(), lat_hi, lat_lo, ((0, 1), (2,))[n], (384, 512)[n], True, True)
                    else:
                        pe.wait_ge(turn_free, group["branch", n // 2] + 2)
                        at = OUT_OF[n // 2]
                        product(open_block(), obT_hi[at], obT_lo[at], (0, 1), NB, True, True)
                a = []
                for k0 in (0, 4):
                    all_turned()
                    for b in range(2):
                        if k0 == 0:
                            a.append(open_block())
                        product(a[b], hT_hi, hT_lo, range(k0, k0 + 4), NB, k0 == 0, k0 == 4,
                                turn_added if (k0, b) == (4, 1) else None)
                assert next(attention, None) is None and next(slabs, None) is None
                def turn_hid2(blk):
                    read_out(blk)
                    for g in range(2):
                        turn_group([(hid2[:, r, c * P:(c + 1) * P], (c % 2) * SEQ + r * P)
                                    for c in (2 * g, 2 * g + 1) for r in range(R)])

                first_block(slab_product)
                for _i in q.rounds(3, dict(slab=4, blk=2, turn=4)):
                    for _ in range(2):
                        wide_block()
                        turn_hid2(q.now("blk") - 1)
                wide_block()
                earlier, last = q.now("turn"), q.now("blk")
                turn_hid2(last - 1)
                pe.wait_ge(turn_free, earlier + 2)
                for b in range(2):
                    a = open_block()
                    for n in range(8):
                        if (b, n) == (0, 6):
                            all_turned()
                        slab_product(a, hid2T_hi, hid2T_lo, range(4 * n, 4 * n + 4), NB, n == 0, n == 7)
                        if (b, n) == (0, 0):
                            turn_hid2(last)
                        if b == 1 and n == 1:
                            turn_added(skip=1)
                q.next("blk")

        @block.scalar
        def _(act):
            q = Place(act)

            def load(dst, src, signal=small_in):
                act.dma_start(dst, src).then_inc(signal, 16)

            for l in range(DEPTH):
                for n, name in enumerate(("attn_norm_g", "ffn_norm_g")):
                    at = 8 * (2 * l + n)
                    load(grows[at:at + 8, :], t[name][l].rearrange("(k p) -> k p", p=P), gains_in)
                    load(grows[32 + at:40 + at, :], t[("g_mix_2", "g_ffn_2")[n]][l].rearrange("(k p) -> k p", p=P), gains_in)
            load(grows[64:72, :], t["g_final_2"].rearrange("(k p) -> k p", p=P), gains_in)
            load(cst[:, P:C_W], t["consts"][:, P:C_W], consts_in)
            for l in range(DEPTH):
                load(crows[0:62, l, :], t["w_dw_2"][l].rearrange("k (c p) -> (k c) p", p=P))
                load(crows[62:64, l, :], t["g_q_lat_2"][l].rearrange("(k p) -> k p", p=P))
                load(crows[64:65, l, :], t["g_kv_lat_2"][l].rearrange("(k p) -> k p", p=P))
            for at, name, n in ((B_RG, "ret_norm_g", HD), (B_DG, "diff_norm_g", DVD), (B_QG, "dq_norm_g", HD),
                                (B_KG, "dk_norm_g", HD), (B_DF, "ret_decay_fwd", RH), (B_DB, "ret_decay_bwd", RH),
                                (B_FB, "b_forget_2", 4)):
                load(small[:, at:at + DEPTH * n], bcast(t[name], 0, DEPTH * n))
            for n, name in enumerate(("lambda_q1", "lambda_k1", "lambda_q2", "lambda_k2")):
                load(lrows[:, n, :], bcast(t[name], 0, DEPTH * HD))
            for r in range(R):
                load(pos_i[:, r:r + 1], bass.AP(t["positions_2"].tensor, r * P, [[1, P], [1, 1]]))

            def step(ins):
                ins.then_inc(act_step, 1)
                act.wait_ge(act_step, q.next("step"))

            def split_hi(kts=4):
                s = q.index("slab") % RING
                q.next("slab")
                act.wait_ge(slab_in[s], q.next(f"in{s}", 32))
                act.wait_ge(slab_used, q.now("slab"))
                act.copy(w_hi[:, s, 0:kts, :], w_raw[:, s, 0:kts, :]).then_inc(hi_ready, 1)

            def used(n):
                act.wait_ge(slab_used, q.next("used", n) + RING)

            def block_of():
                q.next("blk")
                return acc[(q.index("blk") - 1) % 2]

            def read_out(blk):
                act.wait_ge(acc_free, blk + 2)

            def next_turn(skip=0):
                act.wait_ge(turned, q.next("turn") + skip)
                b = turn[(q.index("turn") - 1) % 2]
                q.next("turn", skip)
                return b

            def take_hi(dst):
                b = next_turn()
                n = dst.shape[1] * dst.shape[2]
                act.copy(dst, b[:, 0:n].rearrange("p (c n) -> p c n", n=SEQ)).then_inc(turn_hi, 1)

            def take_model(src_tiles, gain=None, skip=0):
                b = next_turn(skip)
                for j, kt in enumerate(src_tiles):
                    g = gcols[:, bass.ds(gain + kt, 1)]
                    ins = act.activation(hT_hi[:, kt, :], b[:, j * SEQ:(j + 1) * SEQ], ACT.Copy, scale=g)
                ins.then_inc(turn_hi, 1)

            def square_x(b):
                for r in range(R):
                    ins = act.activation(junk[:, :], x[:, r, b * NB:(b + 1) * NB], ACT.Square,
                                         accum_out=stat[:, S_X + 2 * b + r:S_X + 2 * b + r + 1])
                    step(ins) if r == 0 else ins.then_inc(squares, 1)
                act.wait_ge(squares, q.next("squares"))

            def take_x1(gain):
                take_model((4, 5), gain)
                take_model((6, 7), gain)
                read_out(q.now("blk"))
                square_x(1)

            def added(b, gain):
                if b == 1:
                    take_model((0, 1), gain)
                    take_model((2, 3), gain)
                used(3 if b == 0 else 1)
                block_of()
                if b == 0:
                    read_out(q.now("blk"))
                    square_x(0)

            rstd = [stat[:, S_XR + r:S_XR + r + 1] for r in range(R)]

            q.next("turn")
            act.wait_ge(turn_free, 3)
            take_model((0, 1), 0)
            take_model((2, 3), 0)
            for _ in range(AHEAD):
                split_hi()
            act.wait_ge(x_in, 16)
            square_x(0)
            act.wait_ge(small_in, 16 * SMALL_LOADS)
            act.activation(small[:, B_DF:B_DF + 32], small[:, B_DF:B_DF + 32], ACT.Exp).then_inc(act_done, 1)
            act.wait_ge(act_job, q.next("act_job"))
            act.activation(lam[:, :], lam[:, :], ACT.Exp).then_inc(act_done, 1)
            act.wait_ge(act_job, q.next("act_job"))
            act.activation(rope[:, :, :, :], rope[:, :, :, :], ACT.Sin).then_inc(act_done, 1)
            q.next("turn")

            per = dict(slab=len(KTS1), used=len(KTS1), blk=BLOCKS1, turn=TURNS1,
                       decay=RH, soft=DH, rstd=7, squares=9,
                       **{f"in{s}": 32 * len(KTS1) // RING for s in range(RING)})
            per1 = dict(per, step=STEPS_ACT1)
            loop4 = dict(slab=4, used=4, blk=2, **{f"in{s}": 32 for s in range(RING)})
            for l in q.rounds(DEPTH, per1):
                ahead = iter(KTS1[AHEAD:] + KTS1[:AHEAD])

                def splits(n):
                    for _ in range(n):
                        split_hi(next(ahead))

                projection = [q.now("blk") + n for n in range(len(COLS1) + 1)]

                def take_proj(at):
                    used(2)
                    a = block_of()
                    act.wait_ge(acc_free, q.now("blk") + 1)
                    for r in range(R):
                        ins = act.activation(proj1[:, r, at:at + NB], a[r][:, :], ACT.Copy, scale=rstd[r])
                    ins.then_inc(acc_free, 1)

                def take(dst, src):
                    b = next_turn()
                    act.wait_ge(turn_free, q.now("turn") + 1)
                    act.copy(dst, src(b)).then_inc(turn_free, 1)

                def take_outputs(at):
                    take(mixed1[:, :, at:at + P], lambda b: b[:, 0:R * P].rearrange("p (r c) -> p r c", r=R))

                def decays(heads):
                    for h in heads:
                        act.wait_ge(decay_arg, q.next("decay"))
                        act.activation(decay[h], decay[h], ACT.Exp).then_inc(decay_ready, 1)

                def exponentials(h):
                    act.wait_ge(soft_ready, q.next("soft"))
                    for m in range(2):
                        for r in range(R):
                            n = 4 * (h % 2) + 2 * m + r
                            ins = act.activation(soft1[:, h % 2, m, r * SEQ:(r + 1) * SEQ],
                                                 soft1[:, h % 2, m, r * SEQ:(r + 1) * SEQ], ACT.Exp,
                                                 scale=HD ** -0.5, bias=stat[:, S_NM + n:S_NM + n + 1],
                                                 accum_out=stat[:, S_RS + n:S_RS + n + 1])
                    ins.then_inc(probs, 1)

                def square_outputs(at, cols):
                    act.wait_ge(turn_free, q.now("turn") + 2)
                    if at < NB:
                        act.sem_inc(outputs_in, 1)
                    act.activation(sqo[:, :, at % NB:at % NB + cols], mixed1[:, :, at:at + cols],
                                   ACT.Square).then_inc(squares, 1)
                    q.next("squares")

                def side():
                    for n, at in enumerate((DQ, DK)):
                        read_out(projection[n + 1])
                        act.activation(sq1[:, :, n * 512:(n + 1) * 512], proj1[:, :, at:at + 512],
                                       ACT.Square).then_inc(squares, 1)
                        q.next("squares")
                        yield
                    for h in range(DH):
                        take(qkT1[:, h, :], lambda b: b[:, :])
                    yield
                    for h in range(DH + 3):
                        if 2 <= h < DH + 2:
                            take(combT1[:, h % 2].rearrange("p r k -> p (r k)"), lambda b: b[:, :])
                        if h >= 3:
                            take_outputs(NB + (h - 3) * DVD)
                        if h < DH:
                            exponentials(h)
                        if h == 2:
                            decays((0, 1))
                        if h == DH:
                            for j in range(RH // 2):
                                take(qkT1[:, j, :], lambda b: b[:, :])
                        if h == DH + 1:
                            decays((2, 3))
                        if h == DH + 2:
                            square_outputs(NB, NB)
                            take_outputs(0)
                            decays((4, 5))
                        yield
                    for j in range(1, RH // 2):
                        if j == 3:
                            take_hi(hT_hi[:, 4:6, :])
                        take_outputs(j * P)
                        if j == 1:
                            read_out(projection[7])
                            act.activation(proj1[:, :, RG:RG + RETW], proj1[:, :, RG:RG + RETW],
                                           ACT.Silu).then_inc(act_done, 1)
                            for kt in (0, 2):
                                take_hi(hT_hi[:, kt:kt + 2, :])
                        if j == 2:
                            square_outputs(0, HALF)
                            decays((6, 7))
                        if j == 3:
                            square_outputs(HALF, HALF)
                            take_hi(hT_hi[:, 6:8, :])
                        yield

                due = {2 * n + 1: lambda at=at: take_proj(at) for n, at in enumerate(COLS1)}
                for b in range(2):
                    due[16 + b] = lambda b=b: added(b, l * 16 + 8)
                take_x1(l * 16)
                act.wait_ge(rstd_ready, q.next("rstd"))
                attention = side()
                for s in range(18):
                    if s < 17:
                        splits(1)
                    if s in due:
                        due[s]()
                    for _ in range(PLAN1.get(s, 0)):
                        next(attention)
                splits(1)
                assert next(attention, None) is None
                take_x1(l * 16 + 8)
                def gate(first=False):
                    used(2)
                    a = block_of()
                    for r in range(R):
                        ins = act.activation(gate1[:, r, :], a[r][:, 0:HALF], ACT.Silu, scale=rstd[r])
                    ins.then_inc(act_done, 1)

                splits(2)
                act.wait_ge(rstd_ready, q.next("rstd", 6))
                for i in q.rounds(5, dict(loop4, turn=2)):
                    for j in range(2):
                        gate()
                        split_hi()
                        split_hi()
                        take_hi(hid1T_hi[:, bass.ds(i * 4 + 2 * j, 2), :])
                for _ in range(20):
                    next(ahead)
                gate()
                take_hi(hid1T_hi[:, 20:22, :])
                splits(6)
                splits(2)
                used(6)
                block_of()
                read_out(q.now("blk"))
                square_x(0)
                take_model((0, 1), l * 16 + 16)
                take_model((2, 3), l * 16 + 16, skip=1)
                splits(4)
                used(6)
                block_of()

            per2 = dict(slab=len(KTS2), used=len(KTS2), blk=BLOCKS2, turn=TURNS2, soft=12, act_job=1,
                        rstd=4, squares=5, conv=1, step=STEPS_ACT2,
                        **{f"in{s}": 32 * len(KTS2) // RING for s in range(RING)})
            for l in q.rounds(DEPTH, per2):
                ahead = iter(KTS2[AHEAD:] + KTS2[:AHEAD])

                def splits(n):
                    for _ in range(n):
                        split_hi(next(ahead))

                projection = [q.now("blk") + n for n in range(len(COLS2) + 3)]

                def ordered():
                    act.wait_ge(turn_free, q.now("turn") + 1)

                def take_block(dst, cols, scales, n):
                    used(n)
                    a = block_of()
                    act.wait_ge(acc_free, q.now("blk") + 1)
                    for r in range(R):
                        ins = act.activation(dst(r), a[r][:, 0:cols], ACT.Copy, scale=scales[r])
                    ins.then_inc(acc_free, 1)

                def load_gate_bias(u):
                    act.dma_start(bgate[:, u % 2, :], bcast(
                        t["b_gate_2"], l * (NBR * D) + ORDER[u // 2] * D + (u % 2) * NB, NB)).then_inc(bgate_in[u % 2], 16)

                def take_group(g):
                    b = next_turn()
                    ordered()
                    n = P if g < 2 else CAD if g < 6 else BQD
                    act.copy(qkT2[0:n, g % 3, :], b[0:n, :]).then_inc(turn_free, 1)

                def take_probs(h):
                    b = next_turn()
                    ordered()
                    act.copy(softT2[:, h % 2, :], b[:, 0:3 * P]).then_inc(turn_free, 1)

                def exponentials(h):
                    act.wait_ge(soft_ready, q.next("soft"))
                    for r, (a, z) in enumerate(((0, P), (P, 3 * P))):
                        n = 2 * (h % 2) + r
                        ins = act.activation(soft2[:, h % 2, a:z], soft2[:, h % 2, a:z], ACT.Exp,
                                             bias=stat[:, S_NM2 + n:S_NM2 + n + 1],
                                             accum_out=stat[:, S_RS2 + 12 * r + h:S_RS2 + 12 * r + h + 1])
                    ins.then_inc(probs, 1)

                def latents():
                    read_out(projection[4])
                    n = 0
                    for src in (p_b[:, :, QL - AV:QL - AV + 256], p_c[:, :, 0:P]):
                        for r in range(R):
                            ins = act.activation(junk[:, 0:src.shape[2]], src[:, r, :], ACT.Square,
                                                 accum_out=stat[:, S_L + n:S_L + n + 1])
                            n += 1
                            step(ins) if n < 4 else ins.then_inc(squares, 1)
                    q.next("squares")
                    b = next_turn()
                    for c in range(2):
                        ins = act.activation(lat_hi[:, c, :], b[:, c * SEQ:(c + 1) * SEQ], ACT.Copy,
                                             scale=ccols[:, bass.ds(l * 65 + 62 + c, 1)])
                    ins.then_inc(turn_hi, 1)
                    b = next_turn()
                    act.activation(lat_hi[:, 2, :], b[:, 0:SEQ], ACT.Copy,
                                   scale=ccols[:, bass.ds(l * 65 + 64, 1)]).then_inc(turn_hi, 1)

                def heads(first, end):
                    for h in range(first, end + 2):
                        if h == 10:
                            take_hi(obT_hi[0][:, :, :])
                        if h < end and 4 <= h < 10:
                            take_group(h)
                        if first < h <= end:
                            take_probs(h - 1)
                        if h < end:
                            exponentials(h)
                        if h == 3:
                            yield
                            latents()
                        if h == end + 1 == 5:
                            act.wait_ge(act_job, q.next("act_job"))
                            step(act.activation(stat[:, S_A:S_A + 8], stat[:, S_A:S_A + 8], ACT.Exp))
                            act.activation(stat[:, S_A:S_A + 8], stat[:, S_A:S_A + 8], ACT.Ln,
                                           bias=1.0).then_inc(act_done, 1)
                        yield

                def side():
                    read_out(projection[1])
                    act.activation(p_conv[:, :, 256:512], p_conv[:, :, 256:512], ACT.Sigmoid).then_inc(act_done, 1)
                    yield
                    q.next("turn")
                    yield
                    load_gate_bias(0)
                    load_gate_bias(1)
                    q.next("turn", 2)
                    take_group(0)
                    take_group(1)
                    yield
                    yield from heads(0, 4)
                    q.next("turn")
                    yield
                    take_hi(obT_hi[0][:, :, :])
                    take_group(2)
                    take_group(3)
                    yield
                    yield from heads(4, 12)
                    take_hi(obT_hi[1][:, :, :])
                    yield
                    q.next("turn")
                    yield
                    act.wait_ge(conv_in, q.next("conv"))
                    act.activation(branch[:, :, :], branch[:, :, :], ACT.Silu).then_inc(conv_out, 1)
                    yield
                    take_hi(obT_hi[0][:, :, :])
                    yield
                    for half in range(2):
                        for g in (2 * half, 2 * half + 1):
                            take_hi(hT_hi[:, 2 * g:2 * g + 2, :])
                        yield

                due, lat = {}, [[stat[:, S_LR + 2 * n + r:S_LR + 2 * n + r + 1] for r in range(R)] for n in range(2)]
                places = (lambda r: p_conv[:, r, :], lambda r: p_a[:, r, :], lambda r: p_b[:, r, :],
                          lambda r: p_c[:, r, 0:NB], lambda r: p_c[:, r, NB:DVAL - KL])
                for n, (_c0, cols) in enumerate(COLS2):
                    due[2 * n + 1] = lambda n=n, cols=cols: take_block(places[n], cols, rstd, 2)

                def latent_product(n):
                    if n == 0:
                        act.wait_ge(rstd_ready, q.next("rstd"))
                    dst = (lambda r: qB[:, r].rearrange("p h d -> p (h d)"), lambda r: kvB[:, r, :])[n]
                    take_block(dst, (384, 512)[n], lat[n], 1)

                def gate(u):
                    used(2)
                    block_of()
                    read_out(q.now("blk"))
                    act.activation(gate2[:, u % 2], term2[:, :, :], ACT.Sigmoid).then_inc(act_done, 1)
                    if u + 2 < 2 * NBR:
                        load_gate_bias(u + 2)

                def branch_product():
                    used(1)
                    block_of()

                s = 2 * len(COLS2)
                for name in PRODUCTS:
                    s += 2 if name[0] == "G" else 1
                    due[s - 1] = {"G": lambda u=int(name[1]): gate(u), "B": branch_product,
                                  "U": lambda n=int(name[1]): latent_product(n)}[name[0]]
                for b in range(2):
                    due[38 + b] = lambda b=b: added(b, l * 16 + 40)
                take_x1(l * 16 + 32)

                act.wait_ge(rstd_ready, q.next("rstd"))
                attention = side()
                for s in range(40):
                    if s < 39:
                        splits(1)
                    if s in due:
                        due[s]()
                    for _ in range(PLAN2.get(s, 0)):
                        next(attention)
                splits(1)
                assert next(attention, None) is None
                take_x1(l * 16 + 40)
                def rectify():
                    used(2)
                    a = block_of()
                    for r in range(R):
                        ins = act.activation(relu[r][:, :], a[r][:, :], ACT.Relu, scale=rstd[r])
                    ins.then_inc(act_done, 1)

                splits(2)
                act.wait_ge(rstd_ready, q.next("rstd", 2))
                for i in q.rounds(3, dict(loop4, turn=4)):
                    for j in range(2):
                        rectify()
                        split_hi()
                        split_hi()
                        for g in range(2):
                            take_hi(hid2T_hi[:, bass.ds(i * 8 + 4 * j + 2 * g, 2), :])
                for _ in range(12):
                    next(ahead)
                rectify()
                splits(2)
                for g in range(2):
                    take_hi(hid2T_hi[:, 24 + 2 * g:26 + 2 * g, :])
                rectify()
                for g in range(2):
                    take_hi(hid2T_hi[:, 28 + 2 * g:30 + 2 * g, :])
                splits(8)
                splits(2)
                used(8)
                block_of()
                read_out(q.now("blk"))
                square_x(0)
                take_model((0, 1), l * 16 + 48)
                take_model((2, 3), l * 16 + 48, skip=1)
                splits(6)
                used(8)
                block_of()
                q.next("blk")
            read_out(q.now("blk"))
            square_x(1)

        @block.vector
        def _(dve):
            q = Place(dve)
            dve.sem_inc(lo_ready, RING)
            dve.sem_inc(acc_free, 2)
            dve.sem_inc(turn_free, 2)
            dve.sem_inc(scores_out, 2)
            dve.sem_inc(out_free, 1)

            def step(ins):
                ins.then_inc(dve_step, 1)
                dve.wait_ge(dve_step, q.next("step"))

            def split_lo(kts=4):
                s = q.index("slab") % RING
                dve.wait_ge(hi_ready, q.next("slab"))
                dve.tensor_tensor(w_lo[:, s, 0:kts, :], w_raw[:, s, 0:kts, :],
                                  w_hi[:, s, 0:kts, :].bitcast(F32), ALU.subtract).then_inc(lo_ready, 1)

            def used(n):
                dve.wait_ge(slab_used, q.next("used", n) + RING)

            def block_of():
                q.next("blk")
                return acc[(q.index("blk") - 1) % 2]

            def next_turn(skip=0):
                dve.wait_ge(turned, q.next("turn") + skip)
                b = turn[(q.index("turn") - 1) % 2]
                q.next("turn", skip)
                return b

            def next_hi():
                q.next("turn")
                dve.wait_ge(turn_hi, q.next("turn_hi"))
                return turn[(q.index("turn") - 1) % 2]

            def take_lo(dst, hi):
                b = next_hi()
                n = dst.shape[1] * dst.shape[2]
                dve.tensor_tensor(dst, b[:, 0:n].rearrange("p (c n) -> p c n", n=SEQ), hi.bitcast(F32),
                                  ALU.subtract).then_inc(turn_free, 1)

            def lo_with_gain(lo, hi, src, gain):
                return dve.scalar_tensor_tensor(lo, src, gain, hi.bitcast(F32), ALU.mult, ALU.subtract)

            def take_model(tiles, gain, skip=0):
                b = next_hi()
                for j, kt in enumerate(tiles):
                    ins = lo_with_gain(hT_lo[:, kt, :], hT_hi[:, kt, :], b[:, j * SEQ:(j + 1) * SEQ],
                                       gcols[:, bass.ds(gain + kt, 1)])
                ins.then_inc(turn_free, 1 + skip)
                q.next("turn", skip)

            def add_x(b):
                a = block_of()
                for r in range(R):
                    ins = dve.tensor_tensor(x[:, r, b * NB:(b + 1) * NB], x[:, r, b * NB:(b + 1) * NB],
                                            a[r][:, :], ALU.add)
                ins.then_inc(acc_free, 1)

            def mean(dst, src, n):
                dve.tensor_scalar(dst, src, 1.0 / n, EPS, ALU.mult, ALU.add).then_inc(mean_ready, 1)

            def mean_x():
                dve.wait_ge(squares, q.next("squares", 2))
                step(dve.tensor_tensor(stat[:, S_XM:S_XM + 2], stat[:, S_X:S_X + 2], stat[:, S_X + 2:S_X + 4], ALU.add))
                mean(stat[:, S_XM:S_XM + 2], stat[:, S_XM:S_XM + 2], D)

            def take_x1(gain):
                take_model((4, 5), gain)
                take_model((6, 7), gain)
                mean_x()

            def added(b, gain):
                if b == 1:
                    take_model((0, 1), gain)
                    take_model((2, 3), gain)
                used(3 if b == 0 else 1)
                add_x(b)

            def root():
                dve.wait_ge(rstd_ready, q.next("rstd"))

            def per_head(at, r, heads, width):
                return stat[:, at + r * heads:at + (r + 1) * heads].unsqueeze(2).to_broadcast([P, heads, width])

            rstd = [stat[:, S_XR + r:S_XR + r + 1] for r in range(R)]

            b = next_turn()
            dve.tensor_copy(gcols[:, :], b[:, 0:72]).then_inc(turn_free, 1)
            dve.wait_ge(turn_free, 3)
            take_model((0, 1), 0)
            take_model((2, 3), 0)
            for _ in range(AHEAD):
                split_lo()
            b = next_turn()
            dve.tensor_copy(ccols[:, :], b[:, 0:DEPTH * 65]).then_inc(turn_free, 1)
            dve.wait_ge(consts_in, 16)
            dve.wait_ge(small_in, 16 * SMALL_LOADS)
            for n in range(2):
                step(dve.tensor_tensor(lprod[:, n, :], lrows[:, 2 * n, :], lrows[:, 2 * n + 1, :], ALU.mult))
            dve.tensor_reduce(lam[:, :], lprod[:, :, :].rearrange("p n (l d) -> p (n l) d", l=DEPTH), AX.X,
                              ALU.add).then_inc(act_job, 1)
            posf = ropet[:, 5, :, 0]
            step(dve.tensor_copy(posf, pos_i[:, :]))
            for r in range(R):
                step(dve.tensor_scalar(ropet[:, 0, r, :], cst[:, C_INV:C_INV + 16], ropet[:, 5, r, 0:1], None, ALU.mult))
            ang, turns, red = ropet[:, 0], ropet[:, 1], ropet[:, 2]
            step(dve.tensor_scalar(turns, ang, 1.0 / (2 * np.pi), 12582912.0, ALU.mult, ALU.add))
            step(dve.tensor_scalar(turns, turns, 12582912.0, None, ALU.subtract))
            parts = (6.28125, 0.0019350051879882812, 3.0199159819e-07)
            step(dve.scalar_tensor_tensor(red, turns, -parts[0], ang, ALU.mult, ALU.add))
            step(dve.scalar_tensor_tensor(red, turns, -parts[1], red, ALU.mult, ALU.add))
            step(dve.scalar_tensor_tensor(red, turns, -parts[2], red, ALU.mult, ALU.add))
            step(dve.tensor_scalar(rope[:, 1], red, 3.1415925, -3.1415925, ALU.min, ALU.max))
            step(dve.tensor_scalar(ropet[:, 3], rope[:, 1], -1.0, None, ALU.mult))
            step(dve.tensor_tensor(ropet[:, 3], ropet[:, 3], rope[:, 1], ALU.max))
            dve.tensor_scalar(rope[:, 0], ropet[:, 3], -1.0, float(np.pi / 2), ALU.mult, ALU.add).then_inc(act_job, 1)
            dve.wait_ge(act_done, q.next("act_done", 3))
            dve.tensor_scalar(small[:, B_DF:B_DF + 32], small[:, B_DF:B_DF + 32], -1.0, None,
                              ALU.mult).then_inc(pool_job, 1)
            step(dve.tensor_tensor(lam[:, 0:DEPTH], lam[:, 0:DEPTH], lam[:, DEPTH:2 * DEPTH], ALU.subtract))
            step(dve.tensor_tensor(lam[:, 0:DEPTH], lam[:, 0:DEPTH], cst[:, C_LI:C_LI + DEPTH], ALU.add))
            step(dve.tensor_scalar(lam[:, 0:DEPTH], lam[:, 0:DEPTH], -1.0, None, ALU.mult))

            loop4 = dict(slab=4, used=4, blk=2)
            for l in q.rounds(DEPTH, dict(slab=len(KTS1), used=len(KTS1), blk=BLOCKS1, turn=TURNS1,
                                          turn_hi=4 + 4 + 11 + 4, squares=9, rstd=7, act_done=12, scores=16,
                                          decay=RH, probs=DH, step=STEPS_DVE1)):
                ahead = iter(KTS1[AHEAD:] + KTS1[:AHEAD])

                def splits(n):
                    for _ in range(n):
                        split_lo(next(ahead))

                def soften(h):
                    for m in range(2):
                        dve.wait_ge(scores, q.next("scores"))
                        slope = 2.0 ** (-8.0 * (h + 1) / DH)
                        dve.scalar_tensor_tensor(soft1[:, h % 2, m, :], cst[:, C_DA:C_DA + R * SEQ],
                                                 -slope * HD ** 0.5, score[m][:, :], ALU.mult, ALU.add
                                                 ).then_inc(scores_out, 1)
                    dve.wait_ge(scores_out, q.now("scores") + 2)
                    at = S_NM + 4 * (h % 2)
                    step(dve.tensor_reduce(stat[:, at:at + 4], soft1[:, h % 2].rearrange("p m (r k) -> p (m r) k", r=R),
                                           AX.X, ALU.max))
                    dve.tensor_scalar(stat[:, at:at + 4], stat[:, at:at + 4], -HD ** -0.5, None,
                                      ALU.mult).then_inc(soft_ready, 1)

                def combine(h):
                    dve.wait_ge(probs, q.next("probs"))
                    at, rs = S_RC + 4 * (h % 2), S_RS + 4 * (h % 2)
                    step(dve.reciprocal(stat[:, at:at + 4], stat[:, rs:rs + 4]))
                    step(dve.tensor_scalar(stat[:, at + 2:at + 4], stat[:, at + 2:at + 4], lam[:, bass.ds(l, 1)], None, ALU.mult))
                    for r in range(R):
                        ins = dve.tensor_scalar(comb1[:, h % 2, r, :], soft1[:, h % 2, 1, r * SEQ:(r + 1) * SEQ],
                                                stat[:, at + 2 + r:at + 3 + r], None, ALU.mult)
                    step(ins)
                    for r in range(R):
                        ins = dve.scalar_tensor_tensor(comb1[:, h % 2, r, :], soft1[:, h % 2, 0, r * SEQ:(r + 1) * SEQ],
                                                       stat[:, at + r:at + r + 1], comb1[:, h % 2, r, :], ALU.mult, ALU.add)
                    step(ins)
                    dve.sem_inc(dve_ready, 1)
                    if h >= 2:
                        dve.sem_inc(pool_job, 1)

                def retain(heads):
                    for h in heads:
                        dve.wait_ge(scores, q.next("scores"))
                        dve.wait_ge(decay_ready, q.next("decay"))
                        dve.scalar_tensor_tensor(ret_p[:, h % 2, :], score[h % 2][:, :], HD ** -0.5, decay[h],
                                                 ALU.mult, ALU.mult).then_inc(scores_out, 1)

                def means(at, src, heads, d):
                    dve.wait_ge(squares, q.next("squares"))
                    n = R * heads
                    step(dve.tensor_reduce(stat[:, at:at + n], src.rearrange("p r (h d) -> p r h d", d=d),
                                           AX.X, ALU.add))
                    mean(stat[:, at:at + n], stat[:, at:at + n], d)

                def over_rms(dst, src, at, heads, d):
                    for r in range(R):
                        ins = dve.tensor_tensor(dst[:, r, :].rearrange("p (h d) -> p h d", d=d),
                                                src[:, r, :].rearrange("p (h d) -> p h d", d=d),
                                                per_head(at, r, heads, d), ALU.mult)
                    return ins

                def ret_half(c):
                    means(S_O + 8 * c, sqo[:, :, c * HALF:(c + 1) * HALF], 4, HD)
                    root()
                    over_rms(mixed1[:, :, c * HALF:(c + 1) * HALF], proj1[:, :, RG + c * HALF:RG + (c + 1) * HALF],
                             S_OR + 8 * c, 4, HD).then_inc(dve_ready, 1)

                def take_mixed(kts):
                    for kt in kts:
                        dve.wait_ge(turn_free, q.now("turn") + 2)
                        take_lo(hT_lo[:, kt:kt + 2, :], hT_hi[:, kt:kt + 2, :])

                def side():
                    for n, at in enumerate((DQ, DK)):
                        means(S_Q + 16 * n, sq1[:, :, n * 512:(n + 1) * 512], 8, HD)
                        root()
                        v = proj1[:, :, at:at + 512]
                        over_rms(v, v, S_QR + 16 * n, 8, HD).then_inc(dve_ready if n else pool_job, 1)
                        yield
                    q.next("turn", DH)
                    yield
                    for h in range(DH + 3):
                        if h < DH:
                            soften(h)
                        if 0 < h <= DH:
                            combine(h - 1)
                        if 2 <= h < DH + 2:
                            q.next("turn")
                        if h >= 3:
                            q.next("turn")
                        if h == DH:
                            q.next("turn", RH // 2)
                        if h == DH + 1:
                            retain((0, 1))
                        if h == DH + 2:
                            q.next("turn")
                            retain((2, 3))
                            means(S_P, sqo[:, :, :], DH, DVD)
                        yield
                    root()
                    step(dve.tensor_scalar(stat[:, S_PR:S_PR + 8], stat[:, S_PR:S_PR + 8],
                                           cst[:, bass.ds(l + C_OML, 1)], None, ALU.mult))
                    v = mixed1[:, :, NB:D]
                    over_rms(v, v, S_PR, DH, DVD).then_inc(pool_job, 1)
                    q.next("turn")
                    q.next("act_done")
                    retain((4, 5))
                    take_mixed((0, 2))
                    yield
                    q.next("turn")
                    retain((6, 7))
                    ret_half(0)
                    yield
                    take_mixed((4,))
                    q.next("turn")
                    ret_half(1)
                    take_mixed((6,))
                    yield

                def others(n):
                    used(n)
                    block_of()

                due = {2 * n + 1: lambda: others(2) for n in range(len(COLS1))}
                for b in range(2):
                    due[16 + b] = lambda b=b: added(b, l * 16 + 8)
                take_x1(l * 16)
                root()
                attention = side()
                for s in range(18):
                    if s < 17:
                        splits(1)
                    if s in due:
                        due[s]()
                    for _ in range(PLAN1.get(s, 0)):
                        next(attention)
                splits(1)
                assert next(attention, None) is None
                take_x1(l * 16 + 8)
                def up():
                    used(2)
                    a = block_of()
                    dve.wait_ge(act_done, q.next("act_done"))
                    for r in range(R):
                        ins = dve.scalar_tensor_tensor(hid1[:, r, :], a[r][:, HALF:NB], rstd[r], gate1[:, r, :],
                                                       ALU.mult, ALU.mult)
                    ins.then_inc(acc_free, 1)

                splits(2)
                root()
                hold(dve)
                for i in q.rounds(5, dict(loop4, turn=2, turn_hi=2, act_done=2)):
                    for j in range(2):
                        up()
                        split_lo()
                        split_lo()
                        take_lo(hid1T_lo[:, bass.ds(i * 4 + 2 * j, 2), :], hid1T_hi[:, bass.ds(i * 4 + 2 * j, 2), :])
                for _ in range(20):
                    next(ahead)
                up()
                take_lo(hid1T_lo[:, 20:22, :], hid1T_hi[:, 20:22, :])
                splits(8)
                used(6)
                add_x(0)
                take_model((0, 1), l * 16 + 16)
                take_model((2, 3), l * 16 + 16, skip=1)
                splits(4)
                used(6)
                add_x(1)

            for l in q.rounds(DEPTH, dict(slab=len(KTS2), used=len(KTS2), blk=BLOCKS2, turn=TURNS2,
                                          turn_hi=2 + 4 + 4 + 4 + 16 + 4, squares=5, rstd=4, act_done=18, scores=12,
                                          heads=3, layer_in=64, bgate0=64, bgate1=64, step=STEPS_DVE2)):
                ahead = iter(KTS2[AHEAD:] + KTS2[:AHEAD])

                def splits(n):
                    for _ in range(n):
                        split_lo(next(ahead))

                projection = [q.now("blk") + n for n in range(len(COLS2) + 3)]
                done = q.now("act_done")
                q.next("act_done", 2 + 2 * NBR)
                z, m, a8, lf = (stat[:, s:s + 8] for s in (S_Z, S_M, S_A, S_LF))

                def ordered():
                    dve.wait_ge(turn_free, q.now("turn") + 1)

                def lo_of(dst, hi):
                    dve.wait_ge(turn_free, q.now("turn") + 2)
                    take_lo(dst, hi)

                def soften(h):
                    dve.wait_ge(scores, q.next("scores"))
                    bias = abias[:, h, :] if h < 4 else cst[:, C_MCA:C_MCA + 384] if h < 8 else cst[:, C_MCH:C_MCH + 384]
                    dve.scalar_tensor_tensor(soft2[:, h % 2, :], score[0][:, 0:384],
                                             HD ** -0.5 if h < 8 else BQD ** -0.5, bias, ALU.mult, ALU.add
                                             ).then_inc(scores_out, 1)
                    dve.wait_ge(scores_out, q.now("scores") + 2)
                    n = S_NM2 + 2 * (h % 2)
                    dve.tensor_reduce(stat[:, n:n + 1], soft2[:, h % 2, 0:P], AX.X, ALU.max, negate=True)
                    dve.tensor_reduce(stat[:, n + 1:n + 2], soft2[:, h % 2, P:3 * P], AX.X, ALU.max,
                                      negate=True).then_inc(soft_ready, 1)

                def normalise(n):
                    dve.wait_ge(heads_out, q.next("heads"))
                    rs, rc = (stat[:, at:at + 24].rearrange("p (r h) -> p r h", r=R)[:, :, 4 * n:4 * n + 4]
                              for at in (S_RS2, S_RC2))
                    step(dve.reciprocal(rc, rs))
                    for r in range(R):
                        at = S_RC2 + 12 * r + 4 * n
                        ins = dve.tensor_tensor(branch[:, r, :].rearrange("p (h d) -> p h d", d=HD),
                                                score[1][:, r * BW:(r + 1) * BW].rearrange("p (h d) -> p h d", d=HD),
                                                stat[:, at:at + 4].unsqueeze(2).to_broadcast([P, 4, HD]), ALU.mult)
                    ins.then_inc(out_free, 1)

                def latents():
                    dve.wait_ge(squares, q.next("squares"))
                    step(dve.tensor_scalar(stat[:, S_L:S_L + 2], stat[:, S_L:S_L + 2], 1.0 / 256, EPS, ALU.mult, ALU.add))
                    mean(stat[:, S_L + 2:S_L + 4], stat[:, S_L + 2:S_L + 4], P)
                    b = next_hi()
                    ordered()
                    for c in range(2):
                        ins = lo_with_gain(lat_lo[:, c, :], lat_hi[:, c, :], b[:, c * SEQ:(c + 1) * SEQ],
                                           ccols[:, bass.ds(l * 65 + 62 + c, 1)])
                    ins.then_inc(turn_free, 1)
                    b = next_hi()
                    lo_with_gain(lat_lo[:, 2, :], lat_hi[:, 2, :], b[:, 0:SEQ],
                                 ccols[:, bass.ds(l * 65 + 64, 1)]).then_inc(turn_free, 1)

                def heads(first, end):
                    for h in range(first, end + 2):
                        if h == 10:
                            lo_of(obT_lo[0][:, :, :], obT_hi[0][:, :, :])
                        if h < end:
                            soften(h)
                            q.next("turn", 1 if 4 <= h < 10 else 0)
                        if first < h <= end:
                            q.next("turn")
                        if h == 3:
                            yield
                            latents()
                        if h == end + 1 == 5:
                            dve.wait_ge(acc_free, projection[5] + 2)
                            for r in range(R):
                                step(dve.tensor_tensor(z[:, 4 * r:4 * r + 4], p_c[:, r, CF - KL:CF - KL + 4],
                                                       small[:, bass.ds(l * 4 + B_FB, 4)], ALU.add))
                            step(dve.tensor_scalar(m, z, -1.0, None, ALU.mult))
                            dve.tensor_tensor(a8, m, z, ALU.min).then_inc(act_job, 1)
                            step(dve.tensor_scalar(z, z, 0.0, None, ALU.min))
                        if h in (9, 13):
                            normalise((h - 5) // 4)
                        yield

                def side():
                    dve.wait_ge(act_done, done + 1)
                    dve.tensor_tensor(p_conv[:, :, 0:256], p_conv[:, :, 0:256], p_conv[:, :, 256:512],
                                      ALU.mult).then_inc(dve_ready, 1)
                    yield
                    step(dve.memset(uT[:, :, 0:TAPS - 1], 0.0))
                    b = next_turn()
                    step(dve.tensor_copy(uT[:, :, TAPS - 1:], b[:, :].rearrange("p (c n) -> p c n", c=2)))
                    dve.sem_inc(turn_free, 1)
                    yield
                    dve.wait_ge(layer_in, q.next("layer_in", 64))
                    for g in range(2):
                        b = next_turn()
                        v = b[:, :].rearrange("p (h k) -> p h k", h=2)
                        dve.tensor_tensor(abias[:, 2 * g:2 * g + 2, 0:P], v[:, :, P:2 * P],
                                          cst[:, C_MCH:C_MCH + P].unsqueeze(1).to_broadcast([P, 2, P]), ALU.add)
                        dve.tensor_tensor(abias[:, 2 * g:2 * g + 2, P:3 * P], v,
                                          cst[:, C_MCH + P:C_MCH + 3 * P].unsqueeze(1).to_broadcast([P, 2, SEQ]),
                                          ALU.add).then_inc(turn_free, 1)
                    q.next("turn", 2)
                    yield
                    yield from heads(0, 4)
                    dve.wait_ge(act_done, done + 2)
                    dve.tensor_tensor(lf, z, a8, ALU.subtract).then_inc(dve_ready, 1)
                    normalise(0)
                    b = next_turn()
                    ordered()
                    sums = b[:, 0:8].rearrange("p (r h) -> p r h", r=R)
                    dve.tensor_scalar(cqa[:, :, :, HD], sums, HD ** 0.5, None, ALU.mult)
                    dve.tensor_scalar(cka[:, :, :, HD + 1], sums, -HD ** 0.5, None, ALU.mult).then_inc(turn_free, 1)
                    one = cst[:, C_ONE:C_ONE + 8].rearrange("p (r h) -> p r h", r=R)
                    dve.tensor_copy(cka[:, :, :, HD], one)
                    dve.tensor_copy(cqa[:, :, :, HD + 1], one).then_inc(dve_ready, 1)
                    yield
                    lo_of(obT_lo[0][:, :, :], obT_hi[0][:, :, :])
                    q.next("turn", 2)
                    yield
                    yield from heads(4, 12)
                    lo_of(obT_lo[1][:, :, :], obT_hi[1][:, :, :])
                    yield
                    b = next_turn()
                    rows3 = [convrow[:, n, :].unsqueeze(1).to_broadcast([P, R, 256]) for n in range(3)]
                    step(dve.tensor_tensor(branch[:, :, :], b[:, :].rearrange("p (r n) -> p r n", r=R), rows3[0], ALU.add))
                    dve.sem_inc(turn_free, 1)
                    for r in range(R):
                        ins = dve.bn_stats(stat[:, S_BN + 6 * r:S_BN + 6 * r + 6], branch[:, r, :])
                    step(ins)
                    hold(dve)
                    for r in range(R):
                        ins = dve.bn_aggr(stat[:, S_MV + 2 * r:S_MV + 2 * r + 2], stat[:, S_BN + 6 * r:S_BN + 6 * r + 6])
                    step(ins)
                    dve.tensor_scalar(stat[:, S_VR:S_VR + 2], stat[:, S_MV:S_MV + 4].rearrange("p (r n) -> p r n", n=2)[:, :, 1],
                                      EPS, None, ALU.add).then_inc(mean_ready, 1)
                    yield
                    root()
                    for r in range(R):
                        step(dve.tensor_scalar(branch[:, r, :], branch[:, r, :], stat[:, S_MV + 2 * r:S_MV + 2 * r + 1],
                                               stat[:, S_VR + r:S_VR + r + 1], ALU.subtract, ALU.mult))
                    step(dve.tensor_tensor(branch[:, :, :], branch[:, :, :], rows3[1], ALU.mult))
                    dve.tensor_tensor(branch[:, :, :], branch[:, :, :], rows3[2], ALU.add).then_inc(conv_in, 1)
                    yield
                    take_lo(obT_lo[0][:, :, :], obT_hi[0][:, :, :])
                    yield
                    for half in range(2):
                        for g in (2 * half, 2 * half + 1):
                            take_lo(hT_lo[:, 2 * g:2 * g + 2, :], hT_hi[:, 2 * g:2 * g + 2, :])
                        yield

                def taps():
                    for k in range(TAPS):
                        for c in range(2):
                            w = ccols[:, bass.ds(l * 65 + 2 * k + c, 1)]
                            src = uT[:, c, k:k + SEQ]
                            if k == 0:
                                ins = dve.tensor_scalar(yT[:, c, :], src, w, None, ALU.mult)
                            else:
                                dve.wait_ge(dve_step, q.now("step") - 1)
                                ins = dve.scalar_tensor_tensor(yT[:, c, :], src, w, yT[:, c, :], ALU.mult, ALU.add)
                            if k == TAPS - 1 and c == 1:
                                ins.then_inc(dve_ready, 1)
                            else:
                                ins.then_inc(dve_step, 1)
                                q.next("step")
                            yield

                def others(n):
                    used(n)
                    block_of()

                def latent_product(n):
                    if n == 0:
                        root()
                    others(1)

                def gate(u):
                    used(2)
                    a = block_of()
                    dve.wait_ge(acc_free, q.now("blk") + 1)
                    dve.wait_ge(bgate_in[u % 2], q.next(f"bgate{u % 2}", 16))
                    for r in range(R):
                        ins = dve.scalar_tensor_tensor(term2[:, r, :], a[r][:, :], rstd[r], bgate[:, u % 2, :],
                                                       ALU.mult, ALU.add)
                    ins.then_inc(acc_free, 1)

                def branch_product(u, gates):
                    used(1)
                    a = block_of()
                    dve.wait_ge(act_done, done + 2 + gates)
                    cols = slice((u % 2) * NB, (u % 2 + 1) * NB)
                    for r in range(R):
                        dst = mix2[:, r, cols] if u < 2 else term2[:, r, :]
                        ins = dve.tensor_tensor(dst, gate2[:, u % 2, r, :], a[r][:, :], ALU.mult)
                    ins.then_inc(acc_free, 1)
                    if u >= 2:
                        dve.wait_ge(acc_free, q.now("blk") + 2)
                        step(dve.tensor_tensor(mix2[:, :, cols], mix2[:, :, cols], term2[:, :, :], ALU.add))
                        if u >= 6:
                            dve.sem_inc(dve_ready, 1)

                due = {2 * n + 1: lambda: others(2) for n in range(len(COLS2))}
                s, gates = 2 * len(COLS2), 0
                for name in PRODUCTS:
                    s += 2 if name[0] == "G" else 1
                    gates += name[0] == "G"
                    due[s - 1] = {"G": lambda u=int(name[1]): gate(u), "U": lambda n=int(name[1]): latent_product(n),
                                  "B": lambda u=int(name[1]), g=gates: branch_product(u, g)}[name[0]]
                for b in range(2):
                    due[38 + b] = lambda b=b: added(b, l * 16 + 40)

                take_x1(l * 16 + 32)
                root()
                attention, convolution = side(), taps()
                for s in range(40):
                    if s < 39:
                        splits(1)
                    if s in due:
                        due[s]()
                    for _ in range(PLAN2.get(s, 0)):
                        next(attention)
                    if s >= TAPS_FROM:
                        for _ in range(TAPS_EACH):
                            next(convolution, None)
                splits(1)
                assert next(attention, None) is None and next(convolution, None) is None
                take_x1(l * 16 + 40)
                def up():
                    used(2)
                    a = block_of()
                    dve.wait_ge(act_done, q.next("act_done"))
                    for r in range(R):
                        ins = dve.scalar_tensor_tensor(hid2[:, r, :], a[r][:, :], rstd[r], relu[r][:, :],
                                                       ALU.mult, ALU.mult)
                    ins.then_inc(acc_free, 1)

                splits(2)
                root()
                hold(dve)
                for i in q.rounds(3, dict(loop4, turn=4, turn_hi=4, act_done=2)):
                    for j in range(2):
                        up()
                        split_lo()
                        split_lo()
                        for g in range(2):
                            at = i * 8 + 4 * j + 2 * g
                            take_lo(hid2T_lo[:, bass.ds(at, 2), :], hid2T_hi[:, bass.ds(at, 2), :])
                for _ in range(12):
                    next(ahead)
                up()
                splits(2)
                for at in (24, 26):
                    take_lo(hid2T_lo[:, at:at + 2, :], hid2T_hi[:, at:at + 2, :])
                up()
                for at in (28, 30):
                    take_lo(hid2T_lo[:, at:at + 2, :], hid2T_hi[:, at:at + 2, :])
                splits(10)
                used(8)
                add_x(0)
                take_model((0, 1), l * 16 + 48)
                take_model((2, 3), l * 16 + 48, skip=1)
                splits(6)
                used(8)
                a = block_of()
                for r in range(R):
                    ins = dve.tensor_tensor(x[:, r, NB:D], x[:, r, NB:D], a[r][:, :], ALU.add)
                ins.then_inc(acc_free, 2)
                q.next("blk")
            mean_x()
            root()
            dve.wait_ge(x_in, 32)
            for r in range(R):
                ins = dve.scalar_tensor_tensor(outrow[:, r, :], x[:, r, :], rstd[r], gfin[:, :], ALU.mult, ALU.mult)
            ins.then_inc(out_ready, 1)

        @block.gpsimd
        def _(pool):
            q = Place(pool)
            half = cst[:, C_NEG:C_NEG + 32]

            def root(dst, src, n):
                pool.wait_ge(mean_ready, q.next("mean"))
                pool.tensor_tensor(dst, src, half[:, 0:n], ALU.pow).then_inc(rstd_ready, 1)

            def root_x():
                root(stat[:, S_XR:S_XR + 2], stat[:, S_XM:S_XM + 2], 2)

            def step(ins):
                ins.then_inc(pool_step, 1)
                pool.wait_ge(pool_step, q.next("step"))

            pool.wait_ge(consts_in, 16)
            pool.wait_ge(pool_job, q.next("pool_job"))
            q.next("act_done", 3)
            step(pool.tensor_tensor(small[:, B_QG:B_QG + DEPTH * HD], small[:, B_QG:B_QG + DEPTH * HD],
                                    small[:, B_KG:B_KG + DEPTH * HD], ALU.mult))
            for l in q.rounds(DEPTH, dict(mean=7, pool_job=4, outputs=2, act_done=12, scores=16, decay=RH, blk=BLOCKS1,
                                          step=STEPS_POOL1)):
                def exponents(heads):
                    for h in heads:
                        hold(pool)
                        pool.tensor_tensor(decay[h], cst[:, C_DF:C_DF + 512],
                                           small[:, bass.ds(l * 8 + B_DF + h, 1)].to_broadcast([P, 512]), ALU.mult)
                        step(pool.tensor_tensor(junk[:, :], cst[:, C_DB:C_DB + 512],
                                                small[:, bass.ds(l * 8 + B_DB + h, 1)].to_broadcast([P, 512]), ALU.mult))
                        pool.tensor_tensor(decay[h], decay[h], junk[:, :], ALU.add).then_inc(decay_arg, 1)
                        pool.wait_ge(decay_arg, q.next("decay"))

                def gain(parts):
                    pool.wait_ge(pool_job, q.next("pool_job"))
                    hold(pool)
                    for v, g, heads, d in parts:
                        ins = pool.tensor_tensor(v.rearrange("p (h d) -> p h d", d=d), v.rearrange("p (h d) -> p h d", d=d),
                                                 small[:, bass.ds(l * d + g, d)].unsqueeze(1)
                                                 .to_broadcast([P, heads, d]), ALU.mult)
                    ins.then_inc(pool_ready, 1)

                root_x()
                root(stat[:, S_QR:S_QR + 16], stat[:, S_Q:S_Q + 16], 16)
                gain([(proj1[:, r, DQ:DQ + 512], B_QG, 8, HD) for r in range(R)])
                root(stat[:, S_QR + 16:S_QR + 32], stat[:, S_Q + 16:S_Q + 32], 16)
                pool.wait_ge(acc_free, q.now("blk") + 3)
                exponents((0, 1))
                for heads in ((2, 3), (4, 5)):
                    pool.wait_ge(pool_job, q.next("pool_job"))
                    exponents(heads)
                root(stat[:, S_PR:S_PR + 8], stat[:, S_P:S_P + 8], 8)
                gain([(mixed1[:, r, NB:D], B_DG, DH, DVD) for r in range(R)])
                q.next("scores", 2 * DH + 2)
                pool.wait_ge(scores_out, q.now("scores") + 2)
                exponents((6, 7))
                pool.wait_ge(act_done, q.next("act_done"))
                hold(pool)
                for r in range(R):
                    v = proj1[:, r, RG:RG + RETW].rearrange("p (h d) -> p h d", d=HD)
                    ins = pool.tensor_tensor(v, v, small[:, bass.ds(l * HD + B_RG, HD)].unsqueeze(1)
                                             .to_broadcast([P, RH, HD]), ALU.mult)
                step(ins)
                for c in range(2):
                    pool.wait_ge(outputs_in, q.next("outputs"))
                    v = proj1[:, :, RG + c * HALF:RG + (c + 1) * HALF]
                    hold(pool)
                    step(pool.tensor_tensor(v, v, mixed1[:, :, c * HALF:(c + 1) * HALF], ALU.mult))
                    at = 8 * c
                    root(stat[:, S_OR + at:S_OR + at + 8], stat[:, S_O + at:S_O + at + 8], 8)
                root_x()
                q.next("act_done", 11)
                q.next("scores", 16 - 2 * DH - 2)
                q.next("blk", BLOCKS1)
            for l in q.rounds(DEPTH, dict(mean=4, blk=BLOCKS2, step=STEPS_POOL2)):
                root_x()
                pool.wait_ge(acc_free, q.next("blk", 5) + 2)
                hold(pool)
                for r in range(R):
                    pool.tensor_copy(cqa[:, r, :, 0:HD], p_c[:, r, CQ - KL:CQ - KL + 256].rearrange("p (h d) -> p h d", d=HD))
                    ins = pool.tensor_copy(cka[:, r, :, 0:HD], p_c[:, r, CK - KL:CK - KL + 256].rearrange("p (h d) -> p h d", d=HD))
                ins.then_inc(pool_ready, 1)
                root(stat[:, S_LR:S_LR + 4], stat[:, S_L:S_L + 4], 4)
                def rotate(r, a, b, da, db, spread):
                    cos, sin = (rope[:, n, r, :] if not spread else
                                rope[:, n, r, :].unsqueeze(1).to_broadcast([P, 4, 16]) for n in range(2))
                    tmp = [ropetmp[:, n, 0:64].rearrange("p (h d) -> p h d", h=4) if spread else ropetmp[:, n, 0:16]
                           for n in range(4)]
                    for n, (u, v) in enumerate(((a, cos), (b, sin), (b, cos), (a, sin))):
                        step(pool.tensor_tensor(tmp[n], u, v, ALU.mult))
                    step(pool.tensor_tensor(da, tmp[0], tmp[1], ALU.subtract))
                    step(pool.tensor_tensor(db, tmp[2], tmp[3], ALU.add))

                for r in range(R):
                    a, b = p_c[:, r, P:P + 16], p_c[:, r, P + 16:P + 32]
                    rotate(r, a, b, a, b, False)
                pool.wait_ge(acc_free, q.next("blk", 3) + 2)
                for r in range(R):
                    a, b = qB[:, r, :, 64:80], qB[:, r, :, 80:96]
                    rotate(r, a, b, a, b, True)
                    hold(pool)
                    pool.tensor_copy(kB[:, r, :, 0:64], kvB[:, r, :].rearrange("p (h d) -> p h d", d=P)[:, :, 0:64])
                    ins = pool.tensor_copy(kB[:, r, :, 64:96], p_c[:, r, P:P + 32].unsqueeze(1)
                                           .to_broadcast([P, 4, 32]))
                ins.then_inc(pool_ready, 1)
                root(stat[:, S_VR:S_VR + 2], stat[:, S_VR:S_VR + 2], 2)
                root_x()
                q.next("blk", BLOCKS2 - 8)
            root_x()


_NAMES = [
    "x", "attn_norm_g", "w_in", "ret_decay_fwd", "ret_decay_bwd", "ret_norm_g", "dq_norm_g", "dk_norm_g",
    "lambda_q1", "lambda_k1", "lambda_q2", "lambda_k2", "diff_norm_g", "w_out", "ffn_norm_g", "w_gate", "w_up",
    "w_down", "positions_2", "g_mix_2", "w_in_2", "w_gate_2", "b_gate_2", "g_q_lat_2", "w_uq_2",
    "g_kv_lat_2", "w_ukv_2", "b_forget_2", "w_dw_2", "b_dw_2", "g_conv_ln_2", "b_conv_ln_2", "w_branch_2",
    "w_o_2", "g_ffn_2", "w_up_2", "w_down_2", "g_final_2"]


def kernel(**inputs):
    import concourse.bacc as bacc
    from concourse.bass_utils import run_bass_kernel_spmd

    nc = bacc.Bacc("TRN2", target_bir_lowering=False, num_devices=1)
    arrays = {name: np.ascontiguousarray(inputs[name]) for name in _NAMES}
    arrays["consts"] = shape_constants()
    falling = 2 * 128 - np.maximum(np.arange(384) - 127, 0)
    arrays["rel_ext"] = np.ascontiguousarray(inputs["rel_bias_2"][:, :, falling])
    t = {name: nc.dram_tensor(f"in_{name}", a.shape, mybir.dt.from_np(a.dtype), kind="ExternalInput").ap()
         for name, a in arrays.items()}
    out = nc.dram_tensor("out", (1, SEQ, D), F32, kind="ExternalOutput").ap()
    build(nc, t, out)
    r = run_bass_kernel_spmd(nc, [{f"in_{name}": a for name, a in arrays.items()}], core_ids=[0])
    return r.results[0]["out"]
```
